# Optimizing a Trainium2 kernel written in Bass

```python
import jax, jax.numpy as jnp
from jax import lax
import numpy as np

D_MODEL = 1024
BATCH = 1
SEQ = 256
DEPTH = 2

GRID_W = 64
CTX_LEN = 256
N_MOD = 9
NA_HEADS = 8
HEAD_DIM = 64
NA_WIDTH = NA_HEADS * HEAD_DIM
NA_KH = 8
NA_KW = 16
POOL_GROUPS = 4
POOL_CH = 128
POOL_WIDTH = POOL_GROUPS * POOL_CH
POOL_WINDOWS = (2, 4, 8, 16)
MIX_WIDTH = NA_WIDTH + POOL_WIDTH
IN_WIDTH = 3 * NA_WIDTH + POOL_WIDTH
D_FF = 2816
ROPE_THETA = 10000.0
ROPE_PAIRS = HEAD_DIM // 4
RMS_EPS = 1e-6
NEG_INF = -1e30


def rms_norm(x, g):
    xf = x.astype(jnp.float32)
    y = xf * lax.rsqrt(jnp.mean(xf * xf, axis=-1, keepdims=True) + RMS_EPS)
    return (y * g.astype(jnp.float32)).astype(x.dtype)

def modulate(h, shift, scale):
    return h * (1.0 + scale) + shift

def mod_vectors(cvec, w_mod, b_mod):
    m = jax.nn.silu(cvec) @ w_mod + b_mod
    return jnp.split(m, N_MOD, axis=-1)

def swiglu(h, w_gate_up, w_down):
    gate, up = jnp.split(h @ w_gate_up, 2, axis=-1)
    return (jax.nn.silu(gate) * up) @ w_down

def sandwich_ffn(x, w_gate_up, w_down, g_pre, g_post, shift, scale, gate):
    h = modulate(rms_norm(x, g_pre), shift, scale)
    return x + 0.5 * gate * rms_norm(swiglu(h, w_gate_up, w_down), g_post)

def axial_rope(x, rows):
    seq = rows * GRID_W
    t = jnp.arange(seq)
    inv = ROPE_THETA ** (-jnp.arange(ROPE_PAIRS, dtype=jnp.float32) / ROPE_PAIRS)

    def rot(xa, pos):
        ang = pos.astype(jnp.float32)[:, None] * inv
        cos = jnp.cos(ang)[:, None, :]
        sin = jnp.sin(ang)[:, None, :]
        x1, x2 = jnp.split(xa, 2, axis=-1)
        return jnp.concatenate([x1 * cos - x2 * sin, x2 * cos + x1 * sin], axis=-1)

    xr, xc = jnp.split(x.astype(jnp.float32), 2, axis=-1)
    return jnp.concatenate([rot(xr, t // GRID_W), rot(xc, t % GRID_W)], axis=-1).astype(x.dtype)

def neighbourhood_attention(q, k, v, kc, vc, rpb, rows):
    b, s, h, dh = q.shape
    kh = min(NA_KH, rows)
    scale = dh ** -0.5
    q = q.reshape(b, rows, GRID_W, h, dh)
    k = k.reshape(b, rows, GRID_W, h, dh)
    v = v.reshape(b, rows, GRID_W, h, dh)
    r = np.arange(rows)
    row_start = np.clip(r - kh // 2, 0, rows - kh)
    row_idx = row_start[:, None] + np.arange(kh)[None, :]
    k_blk = k[:, row_idx]
    v_blk = v[:, row_idx]
    j = np.arange(GRID_W)
    col_start = np.clip(j - NA_KW // 2, 0, GRID_W - NA_KW)
    col_valid = (j[None, :] >= col_start[:, None]) & (j[None, :] < col_start[:, None] + NA_KW)
    dr = row_idx - r[:, None]
    dc = np.clip(j[None, :] - j[:, None] + NA_KW - 1, 0, 2 * NA_KW - 2)
    bias = rpb[:, dr + NA_KH - 1]
    bias = bias[..., dc]
    bias = jnp.transpose(bias, (0, 1, 3, 2, 4)).astype(jnp.float32)
    s_loc = jnp.einsum('brqhd,brkchd->bhrqkc', q, k_blk, preferred_element_type=jnp.float32) * scale
    s_loc = jnp.where(col_valid[:, None, :], s_loc + bias, NEG_INF)
    s_ctx = jnp.einsum('brqhd,bkhd->bhrqk', q, kc, preferred_element_type=jnp.float32) * scale
    n_loc = kh * GRID_W
    scores = jnp.concatenate([s_loc.reshape(b, h, rows, GRID_W, n_loc), s_ctx], axis=-1)
    p = jax.nn.softmax(scores, axis=-1).astype(v.dtype)
    p_loc = p[..., :n_loc].reshape(b, h, rows, GRID_W, kh, GRID_W)
    p_ctx = p[..., n_loc:]
    o = jnp.einsum('bhrqkc,brkchd->brqhd', p_loc, v_blk) + jnp.einsum('bhrqk,bkhd->brqhd', p_ctx, vc)
    return o.reshape(b, s, h * dh)

def context_attention(q, k, v):
    b, l, h, dh = q.shape
    sc = jnp.einsum('bqhd,bkhd->bhqk', q, k, preferred_element_type=jnp.float32) * dh ** -0.5
    p = jax.nn.softmax(sc, axis=-1).astype(v.dtype)
    return jnp.einsum('bhqk,bkhd->bqhd', p, v).reshape(b, l, h * dh)

def pool_mix(u, w_pool, pool_scale):
    length = u.shape[-2]
    ug = u.reshape(u.shape[:-1] + (POOL_GROUPS, POOL_CH))
    uf = ug.astype(jnp.float32)
    cs = jnp.cumsum(uf, axis=-3)
    pad = [(0, 0)] * cs.ndim
    pad[-3] = (1, 0)
    cs = jnp.pad(cs, pad)
    t = np.arange(length)
    outs = []
    for g, w in enumerate(POOL_WINDOWS):
        lo = np.clip(t - w // 2, 0, length)
        hi = np.clip(t - w // 2 + w, 0, length)
        cnt = (hi - lo).astype(np.float32)[:, None]
        csg = cs[..., g, :]
        outs.append((jnp.take(csg, hi, axis=-2) - jnp.take(csg, lo, axis=-2)) / cnt)
    pooled = jnp.stack(outs, axis=-2)
    d = (pooled - uf).astype(u.dtype)
    y = jnp.einsum('...gc,gcd->...gd', d, w_pool) * pool_scale.reshape(POOL_GROUPS, POOL_CH)
    return y.reshape(u.shape)

def token_mix(hx, hc, w_in, w_out, rpb, w_pool, pool_scale, with_ctx_out):
    b, s, _ = hx.shape
    rows = s // GRID_W
    l = hc.shape[1]
    qx, kx, vx, ux = jnp.split(hx @ w_in, [NA_WIDTH, 2 * NA_WIDTH, 3 * NA_WIDTH], axis=-1)
    if with_ctx_out:
        qc, kc, vc, uc = jnp.split(hc @ w_in, [NA_WIDTH, 2 * NA_WIDTH, 3 * NA_WIDTH], axis=-1)
    else:
        kc, vc = jnp.split(hc @ w_in[:, NA_WIDTH:3 * NA_WIDTH], 2, axis=-1)
    heads = lambda t, n: t.reshape(b, n, NA_HEADS, HEAD_DIM)
    qx = axial_rope(heads(qx, s), rows)
    kx = axial_rope(heads(kx, s), rows)
    kc_h, vc_h = heads(kc, l), heads(vc, l)
    na_x = neighbourhood_attention(qx, kx, heads(vx, s), kc_h, vc_h, rpb, rows)
    pool_x = pool_mix(ux.reshape(b, rows, GRID_W, POOL_WIDTH), w_pool, pool_scale).reshape(b, s, POOL_WIDTH)
    out_x = jnp.concatenate([na_x, pool_x], axis=-1) @ w_out
    if with_ctx_out:
        na_c = context_attention(heads(qc, l), kc_h, vc_h)
        pool_c = pool_mix(uc, w_pool, pool_scale)
        out_c = jnp.concatenate([na_c, pool_c], axis=-1) @ w_out
        return out_x, out_c
    return out_x, None

def first_inputs(seed: int = 0) -> dict:
    key = jax.random.key(seed)
    ks = jax.random.split(key, 14)
    nrm = jax.random.normal
    f32 = jnp.float32
    return {
        'x': nrm(ks[0], (BATCH, SEQ, D_MODEL), f32),
        'c': nrm(ks[1], (BATCH, D_MODEL), f32),
        'ctx': nrm(ks[2], (BATCH, CTX_LEN, D_MODEL), f32),
        'c_ctx': nrm(ks[3], (D_MODEL,), f32),
        'w_mod': nrm(ks[4], (DEPTH, D_MODEL, N_MOD * D_MODEL), f32) * (0.5 * D_MODEL ** -0.5),
        'b_mod': nrm(ks[5], (DEPTH, N_MOD * D_MODEL), f32) * 0.01,
        'norm_g': 1.0 + 0.05 * nrm(ks[6], (DEPTH, 6, D_MODEL), f32),
        'w_ffn_gate_up': nrm(ks[7], (DEPTH, 2, D_MODEL, 2 * D_FF), f32) * D_MODEL ** -0.5,
        'w_ffn_down': nrm(ks[8], (DEPTH, 2, D_FF, D_MODEL), f32) * D_FF ** -0.5,
        'w_in': nrm(ks[9], (DEPTH, D_MODEL, IN_WIDTH), f32) * D_MODEL ** -0.5,
        'w_out': nrm(ks[10], (DEPTH, MIX_WIDTH, D_MODEL), f32) * MIX_WIDTH ** -0.5,
        'na_rpb': nrm(ks[11], (DEPTH, NA_HEADS, 2 * NA_KH - 1, 2 * NA_KW - 1), f32) * 0.1,
        'w_pool': nrm(ks[12], (DEPTH, POOL_GROUPS, POOL_CH, POOL_CH), f32) * POOL_CH ** -0.5,
        'pool_scale': 1.0 + 0.05 * nrm(ks[13], (DEPTH, POOL_WIDTH), f32),
    }

def first_block(x, c, ctx, c_ctx, w_mod, b_mod, norm_g, w_ffn_gate_up, w_ffn_down, w_in, w_out, na_rpb, w_pool, pool_scale):
    for l in range(DEPTH):
        last = l == DEPTH - 1
        mx = [m[:, None, :] for m in mod_vectors(c, w_mod[l], b_mod[l])]
        mc = mod_vectors(c_ctx, w_mod[l], b_mod[l])
        g = norm_g[l]
        x = sandwich_ffn(x, w_ffn_gate_up[l, 0], w_ffn_down[l, 0], g[0], g[1], mx[0], mx[1], mx[2])
        ctx = sandwich_ffn(ctx, w_ffn_gate_up[l, 0], w_ffn_down[l, 0], g[0], g[1], mc[0], mc[1], mc[2])
        hx = modulate(rms_norm(x, g[2]), mx[3], mx[4])
        hc = modulate(rms_norm(ctx, g[2]), mc[3], mc[4])
        out_x, out_c = token_mix(hx, hc, w_in[l], w_out[l], na_rpb[l], w_pool[l], pool_scale[l], not last)
        x = x + mx[5] * rms_norm(out_x, g[3])
        x = sandwich_ffn(x, w_ffn_gate_up[l, 1], w_ffn_down[l, 1], g[4], g[5], mx[6], mx[7], mx[8])
        if not last:
            ctx = ctx + mc[5] * rms_norm(out_c, g[3])
            ctx = sandwich_ffn(ctx, w_ffn_gate_up[l, 1], w_ffn_down[l, 1], g[4], g[5], mc[6], mc[7], mc[8])
    return x


DEPTH_2 = 4

CHUNK = 64
N_MIXERS = 3
N_GLA = (DEPTH_2 + 2) // 3
N_MLA = (DEPTH_2 + 1) // 3
N_CONV = DEPTH_2 // 3
ALPHA = (2 * DEPTH_2) ** 0.25
BETA = (8 * DEPTH_2) ** -0.25
LN_EPS = 1e-5
PLE_DIM = 256
D_FF_2 = 4 * D_MODEL
MAX_OFFSET = 4096

GLA_HEADS = 4
GLA_DK = D_MODEL // 2 // GLA_HEADS
GLA_DV = D_MODEL // GLA_HEADS
GLA_GATE_RANK = 16
GLA_TAU = 16.0
GLA_HK = GLA_HEADS * GLA_DK
GLA_HV = GLA_HEADS * GLA_DV
GLA_SPLITS = [GLA_HK, 2 * GLA_HK, 2 * GLA_HK + GLA_HV, 2 * GLA_HK + GLA_HV + D_MODEL]
GLA_IN = 2 * GLA_HK + GLA_HV + D_MODEL + GLA_GATE_RANK

MLA_HEADS = 8
MLA_NOPE = 128
MLA_ROPE = 64
MLA_V = 128
MLA_Q_RANK = 256
MLA_KV_RANK = 256
MLA_IN = MLA_Q_RANK + MLA_KV_RANK + MLA_ROPE
ROPE_BASE = 10000.0
Q_BLOCK = 128

CONV_WIDTH = 3


def layer_norm(x, g, b):
    xf = x.astype(jnp.float32)
    mu = jnp.mean(xf, -1, keepdims=True)
    var = jnp.mean(jnp.square(xf - mu), -1, keepdims=True)
    return ((xf - mu) * lax.rsqrt(var + LN_EPS) * g + b).astype(x.dtype)

def rms_norm_2(x, g):
    xf = x.astype(jnp.float32)
    return (xf * lax.rsqrt(jnp.mean(xf * xf, -1, keepdims=True) + RMS_EPS) * g).astype(x.dtype)

def rope(x, cos, sin):
    x1, x2 = jnp.split(x, 2, axis=-1)
    return jnp.concatenate([x1 * cos - x2 * sin, x2 * cos + x1 * sin], axis=-1)

def gla_mixer(x, w_in, w_gate_up, b_gate, norm_g, w_out):
    B_, S_, _ = x.shape
    nc = S_ // CHUNK
    q, k, v, r, g_lr = jnp.split(x @ w_in, GLA_SPLITS, axis=-1)
    log_a = jax.nn.log_sigmoid((g_lr @ w_gate_up + b_gate).astype(jnp.float32)) / GLA_TAU

    def to_chunks(t, d):
        return t.astype(jnp.float32).reshape(B_, nc, CHUNK, GLA_HEADS, d).transpose(1, 0, 3, 2, 4)

    qc = to_chunks(q, GLA_DK) * GLA_DK ** -0.5
    kc = to_chunks(k, GLA_DK)
    vc = to_chunks(v, GLA_DV)
    lc = to_chunks(log_a, GLA_DK)

    def step(state, inp):
        q_, k_, v_, la = inp
        L = jnp.cumsum(la, axis=2)
        decay = jnp.exp(-jnp.abs(L[:, :, :, None, :] - L[:, :, None, :, :]))
        scores = jnp.einsum('bhtd,bhsd,bhtsd->bhts', q_, k_, decay)
        o = scores @ v_ + (q_ * jnp.exp(L)) @ state
        L_end = L[:, :, -1:, :]
        state = (jnp.exp(L_end[:, :, 0, :, None]) * state
                 + jnp.einsum('bhsd,bhse->bhde', k_ * jnp.exp(L_end - L), v_))
        return state, o

    s0 = jnp.zeros((B_, GLA_HEADS, GLA_DK, GLA_DV), jnp.float32)
    _, o = lax.scan(step, s0, (qc, kc, vc, lc))
    o = o.transpose(1, 0, 3, 2, 4).reshape(B_, S_, GLA_HEADS, GLA_DV)
    o = rms_norm_2(o, norm_g).reshape(B_, S_, GLA_HV) * jax.nn.silu(r.astype(jnp.float32))
    return o.astype(x.dtype) @ w_out

def mla_mixer(x, cos, sin, w_in, q_norm, kv_norm, w_uq, w_ukv, w_out):
    B_, S_, _ = x.shape
    c_q, c_kv, k_rope = jnp.split(x @ w_in, [MLA_Q_RANK, MLA_Q_RANK + MLA_KV_RANK], axis=-1)
    q = (rms_norm_2(c_q, q_norm) @ w_uq).reshape(B_, S_, MLA_HEADS, MLA_NOPE + MLA_ROPE)
    kv = (rms_norm_2(c_kv, kv_norm) @ w_ukv).reshape(B_, S_, MLA_HEADS, MLA_NOPE + MLA_V)
    q_nope, q_rope = jnp.split(q, [MLA_NOPE], axis=-1)
    k_nope, v = jnp.split(kv, [MLA_NOPE], axis=-1)
    q_rope = rope(q_rope, cos[:, :, None, :], sin[:, :, None, :])
    k_rope = rope(k_rope, cos, sin)
    qf = jnp.concatenate([q_nope.astype(jnp.float32), q_rope.astype(jnp.float32)], axis=-1)
    qf = qf * (MLA_NOPE + MLA_ROPE) ** -0.5
    kf = jnp.concatenate([k_nope.astype(jnp.float32),
                          jnp.broadcast_to(k_rope.astype(jnp.float32)[:, :, None, :],
                                           (B_, S_, MLA_HEADS, MLA_ROPE))], axis=-1)
    n_qb = S_ // Q_BLOCK
    q_blocks = qf.reshape(B_, n_qb, Q_BLOCK, MLA_HEADS, MLA_NOPE + MLA_ROPE).transpose(1, 0, 2, 3, 4)
    key_chunk = jnp.arange(S_) // CHUNK

    def attend(args):
        qb, bi = args
        q_chunk = (bi * Q_BLOCK + jnp.arange(Q_BLOCK)) // CHUNK
        s = jnp.einsum('bqhd,bkhd->bhqk', qb, kf)
        s = jnp.where(key_chunk[None, :] <= q_chunk[:, None], s, -jnp.inf)
        pr = jax.nn.softmax(s, axis=-1)
        return jnp.einsum('bhqk,bkhd->bqhd', pr.astype(v.dtype), v)

    o = lax.map(attend, (q_blocks, jnp.arange(n_qb)))
    o = o.transpose(1, 0, 2, 3, 4).reshape(B_, S_, MLA_HEADS * MLA_V)
    return o.astype(x.dtype) @ w_out

def conv_mixer(x, w_in, conv_w, w_out):
    b, c, u = jnp.split(x @ w_in, 3, axis=-1)
    z = lax.conv_general_dilated(c * u, conv_w[:, None, :], window_strides=(1,),
                                 padding=[(CONV_WIDTH - 1, 0)],
                                 dimension_numbers=('NWC', 'WIO', 'NWC'),
                                 feature_group_count=D_MODEL)
    return (b * z) @ w_out

def sq_relu_mlp(x, w1, w2):
    return jnp.square(jax.nn.relu(x @ w1)) @ w2

def second_inputs(seed: int = 0) -> dict:
    key = jax.random.key(seed)
    ks = jax.random.split(key, 24)

    def nrm(i, shape, scale):
        return jax.random.normal(ks[i], shape, jnp.float32) * scale

    x = nrm(0, (BATCH, SEQ, D_MODEL), 1.0)
    p = nrm(1, (DEPTH_2, BATCH, SEQ, PLE_DIM), 1.0)
    offsets = jax.random.randint(ks[2], (BATCH, 1), 0, MAX_OFFSET, dtype=jnp.int32)
    positions = (offsets + jnp.arange(SEQ, dtype=jnp.int32)[None, :]).astype(jnp.int32)
    return {
        'x': x,
        'p': p,
        'positions': positions,
        'gla_w_in': nrm(3, (N_GLA, D_MODEL, GLA_IN), D_MODEL ** -0.5),
        'gla_w_gate_up': nrm(4, (N_GLA, GLA_GATE_RANK, GLA_HK), GLA_GATE_RANK ** -0.5),
        'gla_b_gate': nrm(5, (N_GLA, GLA_HK), 0.1),
        'gla_norm_g': 1.0 + nrm(6, (N_GLA, GLA_DV), 0.01),
        'gla_w_out': nrm(7, (N_GLA, GLA_HV, D_MODEL), GLA_HV ** -0.5 * BETA),
        'mla_w_in': nrm(8, (N_MLA, D_MODEL, MLA_IN), D_MODEL ** -0.5),
        'mla_q_norm': 1.0 + nrm(9, (N_MLA, MLA_Q_RANK), 0.01),
        'mla_kv_norm': 1.0 + nrm(10, (N_MLA, MLA_KV_RANK), 0.01),
        'mla_w_uq': nrm(11, (N_MLA, MLA_Q_RANK, MLA_HEADS * (MLA_NOPE + MLA_ROPE)), MLA_Q_RANK ** -0.5),
        'mla_w_ukv': nrm(12, (N_MLA, MLA_KV_RANK, MLA_HEADS * (MLA_NOPE + MLA_V)), MLA_KV_RANK ** -0.5),
        'mla_w_out': nrm(13, (N_MLA, MLA_HEADS * MLA_V, D_MODEL), (MLA_HEADS * MLA_V) ** -0.5 * BETA),
        'conv_w_in': nrm(14, (N_CONV, D_MODEL, 3 * D_MODEL), D_MODEL ** -0.5),
        'conv_w': nrm(15, (N_CONV, CONV_WIDTH, D_MODEL), CONV_WIDTH ** -0.5),
        'conv_w_out': nrm(16, (N_CONV, D_MODEL, D_MODEL), D_MODEL ** -0.5 * BETA),
        'ln_g': 1.0 + nrm(17, (DEPTH_2, 2, D_MODEL), 0.01),
        'ln_b': nrm(18, (DEPTH_2, 2, D_MODEL), 0.01),
        'mlp_w1': nrm(19, (DEPTH_2, D_MODEL, D_FF_2), D_MODEL ** -0.5),
        'mlp_w2': nrm(20, (DEPTH_2, D_FF_2, D_MODEL), D_FF_2 ** -0.5 * BETA),
        'ple_w_gate': nrm(21, (DEPTH_2, D_MODEL, D_MODEL), D_MODEL ** -0.5),
        'ple_w_proj': nrm(22, (DEPTH_2, PLE_DIM, D_MODEL), PLE_DIM ** -0.5),
    }

def second_block(x, p, positions, gla_w_in, gla_w_gate_up, gla_b_gate, gla_norm_g, gla_w_out,
              mla_w_in, mla_q_norm, mla_kv_norm, mla_w_uq, mla_w_ukv, mla_w_out,
              conv_w_in, conv_w, conv_w_out, ln_g, ln_b, mlp_w1, mlp_w2,
              ple_w_gate, ple_w_proj):
    inv_freq = ROPE_BASE ** (-jnp.arange(0, MLA_ROPE // 2, dtype=jnp.float32) * (2.0 / MLA_ROPE))
    ang = positions.astype(jnp.float32)[..., None] * inv_freq
    cos, sin = jnp.cos(ang), jnp.sin(ang)
    for i in range(DEPTH_2):
        j = i // N_MIXERS
        kind = i % N_MIXERS
        if kind == 0:
            h = gla_mixer(x, gla_w_in[j], gla_w_gate_up[j], gla_b_gate[j], gla_norm_g[j], gla_w_out[j])
        elif kind == 1:
            h = mla_mixer(x, cos, sin, mla_w_in[j], mla_q_norm[j], mla_kv_norm[j],
                          mla_w_uq[j], mla_w_ukv[j], mla_w_out[j])
        else:
            h = conv_mixer(x, conv_w_in[j], conv_w[j], conv_w_out[j])
        x = layer_norm(ALPHA * x + h, ln_g[i, 0], ln_b[i, 0])
        x = layer_norm(ALPHA * x + sq_relu_mlp(x, mlp_w1[i], mlp_w2[i]), ln_g[i, 1], ln_b[i, 1])
        x = x + jax.nn.sigmoid(x @ ple_w_gate[i]) * (p[i] @ ple_w_proj[i])
    return x


def setup_inputs(seed=0):
    out = dict(first_inputs(seed))
    for name, value in second_inputs(seed + 1).items():
        if name != "x":
            out[name + "_2"] = value
    return out


def reference(
    x, c, ctx, c_ctx, w_mod, b_mod, norm_g, w_ffn_gate_up, w_ffn_down, w_in, w_out, na_rpb,
    w_pool, pool_scale, p_2, positions_2, gla_w_in_2, gla_w_gate_up_2, gla_b_gate_2,
    gla_norm_g_2, gla_w_out_2, mla_w_in_2, mla_q_norm_2, mla_kv_norm_2, mla_w_uq_2, mla_w_ukv_2,
    mla_w_out_2, conv_w_in_2, conv_w_2, conv_w_out_2, ln_g_2, ln_b_2, mlp_w1_2, mlp_w2_2,
    ple_w_gate_2, ple_w_proj_2,
):
    x = first_block(
        x, c, ctx, c_ctx, w_mod, b_mod, norm_g, w_ffn_gate_up, w_ffn_down, w_in, w_out, na_rpb,
        w_pool, pool_scale,
    )
    return second_block(
        x, p_2, positions_2, gla_w_in_2, gla_w_gate_up_2, gla_b_gate_2, gla_norm_g_2,
        gla_w_out_2, mla_w_in_2, mla_q_norm_2, mla_kv_norm_2, mla_w_uq_2, mla_w_ukv_2,
        mla_w_out_2, conv_w_in_2, conv_w_2, conv_w_out_2, ln_g_2, ln_b_2, mlp_w1_2, mlp_w2_2,
        ple_w_gate_2, ple_w_proj_2,
    )


_drawn_inputs = setup_inputs


def setup_inputs(seed=0):
    import zlib

    import numpy as np

    out = dict(_drawn_inputs(seed))
    spreads = {}
    factors = {'b_mod': 3.867,
     'na_rpb': 8.0,
     'pool_scale': 3.437,
     'gla_b_gate_2': 7.887,
     'gla_norm_g_2': 8.0,
     'mla_q_norm_2': 8.0,
     'mla_kv_norm_2': 8.0}
    for name, (base, spread) in spreads.items():
        noise = np.random.default_rng([zlib.crc32(name.encode()), seed]).standard_normal(out[name].shape)
        drawn = base * np.exp(spread * noise) if base else spread * noise
        out[name] = __import__('jax').numpy.asarray(drawn.astype(out[name].dtype))
    for name, factor in factors.items():
        out[name] = (out[name] * factor).astype(out[name].dtype)
    return out
```

```python
from contextlib import ExitStack

import numpy as np
import concourse.bass as bass
from concourse import mybir

F32 = mybir.dt.float32
F32R = mybir.dt.float32r
I32 = mybir.dt.int32
ALU = mybir.AluOpType
ACT = mybir.ActivationFunctionType
AX = mybir.AxisListType

P = 128
D = 1024
DK = D // P
T = 256
TT = 2 * T
DEPTH = 2
DEPTH_2 = 4
N_MOD = 9
D_FF = 2816
FT = D_FF // P
GRID_W = 64
ROWS = T // GRID_W
NA_HEADS, HEAD_DIM, NA_KH, NA_KW = 8, 64, 8, 16
NA_WIDTH = NA_HEADS * HEAD_DIM
POOL_WINDOWS = (2, 4, 8, 16)
ROPE_PAIRS = HEAD_DIM // 4
NEG = -1e30
ALPHA = (2 * DEPTH_2) ** 0.25
CHUNK = 64
GLA_HEADS, GLA_DK, GLA_DV, GLA_RANK, GLA_TAU = 4, 128, 256, 16, 16.0
MLA_HEADS, MLA_NOPE, MLA_ROPE, MLA_V = 8, 128, 64, 128
MLA_SCALE = (MLA_NOPE + MLA_ROPE) ** -0.5
RMS_EPS, LN_EPS = 1e-6, 1e-5
EXPONENT_MAX = 80.0

RAW, CUT = 4, 2
SC = 256
MOD_SLOTS = N_MOD * D // SC


class Signal:

    def __init__(self, sem):
        self.sem, self.n = sem, 0


class Counts:

    def __init__(self, a, d, h=0, l=0, v=0, slot=0):
        self.a, self.d, self.h, self.l, self.v, self.slot = a, d, h, l, v, slot


class Place:

    def __init__(self):
        self.slot, self.side, self.mod_layer, self.mod_slot = 0, 0, 0, 0


SIGNALS = (
    "lo_ready",
    "hi_ready",
    "slot_used",
    "act_evicted",
    "dve_evicted",
    "hidden_hi",
    "hidden_lo",
    "mod_rows",
    "mod_turned",
    "mod_done",
    "act",
    "dve",
    "pe",
    "pool",
    "stored",
)


class Signals:

    def __init__(self, sems):
        self.lo_ready = Signal(sems["lo_ready"])
        self.hi_ready = Signal(sems["hi_ready"])
        self.slot_used = Signal(sems["slot_used"])
        self.act_evicted = Signal(sems["act_evicted"])
        self.dve_evicted = Signal(sems["dve_evicted"])
        self.hidden_hi = Signal(sems["hidden_hi"])
        self.hidden_lo = Signal(sems["hidden_lo"])
        self.mod_rows = Signal(sems["mod_rows"])
        self.mod_turned = Signal(sems["mod_turned"])
        self.mod_done = Signal(sems["mod_done"])
        self.act = Signal(sems["act"])
        self.dve = Signal(sems["dve"])
        self.pe = Signal(sems["pe"])
        self.pool = Signal(sems["pool"])
        self.stored = Signal(sems["stored"])


def constants():
    c = {}
    tok = np.arange(T)
    inv = (10000.0 ** (-np.arange(ROPE_PAIRS) / ROPE_PAIRS)).astype(np.float32)
    cos, sin = np.zeros((P, T), np.float32), np.zeros((P, T), np.float32)
    swap = np.zeros((P, P), np.float32)
    for p in range(P):
        d = p % HEAD_DIM
        pos = (tok // GRID_W) if d < 2 * ROPE_PAIRS else (tok % GRID_W)
        ang = pos.astype(np.float32) * inv[d % ROPE_PAIRS]
        cos[p] = np.cos(ang)
        first = (d % (2 * ROPE_PAIRS)) < ROPE_PAIRS
        sin[p] = -np.sin(ang) if first else np.sin(ang)
        swap[p + (ROPE_PAIRS if first else -ROPE_PAIRS), p] = 1.0
    c["na_cos"], c["na_sin"], c["na_swap"] = cos, sin, swap
    eye_row = np.eye(GRID_W, dtype=np.float32)[::-1]
    c["na_flip"] = np.kron(np.eye(P // GRID_W, dtype=np.float32), eye_row)
    col = np.arange(GRID_W)
    start = np.clip(col - NA_KW // 2, 0, GRID_W - NA_KW)
    valid = (col[None] >= start[:, None]) & (col[None] < start[:, None] + NA_KW)
    m = np.where(valid, 0.0, NEG).astype(np.float32)
    c["na_mask"] = np.concatenate([m, m], 0)

    def counts(length):
        t = np.arange(length)
        out = np.zeros((len(POOL_WINDOWS), length), np.float32)
        for g, w in enumerate(POOL_WINDOWS):
            out[g] = np.clip(t - w // 2 + w, 0, length) - np.clip(t - w // 2, 0, length)
        return np.broadcast_to((1.0 / out).astype(np.float32)[None], (P,) + out.shape).copy()

    c["pool_row"], c["pool_ctx"] = counts(GRID_W), counts(T)
    s, t = np.arange(CHUNK)[:, None], np.arange(CHUNK)[None]
    low = (t >= s).astype(np.float32)
    c["gla_low"], c["gla_up"] = np.concatenate([low, low]), np.concatenate([1 - low, 1 - low])
    first = np.ones((P, GLA_HEADS * T), np.float32)
    first[:, ::CHUNK] = 0.0
    c["gla_carry"] = first
    q, k = np.arange(T)[:, None] // CHUNK, np.arange(T)[None] // CHUNK
    m = np.where(k <= q, 0.0, NEG).astype(np.float32)
    c["mla_mask"] = m.reshape(2, P, T).transpose(1, 0, 2).copy()
    half = MLA_ROPE // 2
    f = (10000.0 ** (-np.arange(half) * (2.0 / MLA_ROPE))).astype(np.float32)
    sign = np.where((np.arange(P) // half) % 2 == 0, -1.0, 1.0)
    c["mla_freq"] = np.stack([np.tile(f, P // half), sign.astype(np.float32)], 1).astype(np.float32)
    c["eye"] = np.eye(P, dtype=np.float32)
    c["mod_sum"] = np.tile(np.eye(2, dtype=np.float32), (2, 1))
    return c


VECTORS = (
    ("b_mod", DEPTH * N_MOD * DK), ("norm_g", DEPTH * 6 * DK), ("pool_scale", DEPTH * 4),
    ("gla_b_gate_2", 2 * GLA_HEADS), ("gla_norm_g_2", 2 * 2), ("mla_q_norm_2", 2), ("mla_kv_norm_2", 2),
    ("ln_g_2", DEPTH_2 * 2 * DK), ("ln_b_2", DEPTH_2 * 2 * DK), ("conv_w_2", 3 * DK), ("c", DK), ("c_ctx", DK),
)
COL = {}
for _name, _rows in VECTORS:
    COL[_name] = sum(r for _, r in VECTORS[:[n for n, _ in VECTORS].index(_name)])
N_COLS = sum(r for _, r in VECTORS)


def build(nc, A, out, upto=99):
    with ExitStack() as ctx:
        def sb(name, shape, dt=F32, scope=ctx):
            return scope.enter_context(nc.sbuf_tensor(name, shape, dt))

        sems = {n: ctx.enter_context(nc.semaphore(n)) for n in SIGNALS}
        landed = [ctx.enter_context(nc.semaphore(f"landed{i}")) for i in range(RAW)]
        side_sem = ctx.enter_context(nc.semaphore("side_loaded"))
        C = {n: nc.inline_tensor(v, "table_" + n) for n, v in constants().items()}

        xt = sb("xt", [P, DK, TT])
        a_hi = sb("a_hi", [P, DK, TT], F32R)
        a_lo = sb("a_lo", [P, DK, TT], F32R)
        w_raw = sb("w_raw", [P, RAW, DK, SC])
        w_hi = sb("w_hi", [P, CUT, DK, SC], F32R)
        w_lo = sb("w_lo", [P, CUT, DK, SC], F32R)
        tmp_g = sb("tmp_g", [P, 2, TT])
        tmp_y = sb("tmp_y", [P, 2, TT])
        r_tmp = sb("r_tmp", [P, TT])
        rows_mod = r_tmp[0:4, :].rearrange("p (b c) -> p b c", c=SC)
        mod = sb("mod", [P, DEPTH * N_MOD * DK * 2])
        cols = sb("cols", [P, N_COLS])
        eye = sb("eye", [P, P])
        ones = sb("ones", [P, P])
        fac = sb("fac", [P, DK, 2])
        c_act = sb("c_act", [P, DK, 2])
        c_cut = sb("c_cut", [P, DK, 4], F32R)
        mod_sum = sb("mod_sum", [4, 2])
        stat = sb("stat", [P, 16])
        bank = [ctx.enter_context(nc.psum_tensor(f"bank{i}", [P, 512], F32)) for i in range(8)]

        Z = {}
        with ExitStack() as h:
            h_hi = sb("h_hi", [P, 16, TT], F32R, h)
            h_lo = sb("h_lo", [P, 16, TT], F32R, h)
            z = sb("z", [P, DK, TT], F32, h)
        with ExitStack() as h:
            sb("region_h_1", [P, 16 * 1024], F32, h)
            Z["pool_a"] = sb("pool_a", [P, 4 * 80 + 272], F32, h)
            Z["pool_b"] = sb("pool_b", [P, 4 * 80 + 272], F32, h)
            Z["pool_row"] = sb("pool_row_s", [P, 4, GRID_W], F32, h)
            Z["pool_ctx"] = sb("pool_ctx_s", [P, 4, T], F32, h)
            Z["w_pool"] = sb("w_pool_s", [P, 4, P], F32, h)
            Z["na_cos"] = sb("na_cos_s", [P, T], F32, h)
            Z["na_sin"] = sb("na_sin_s", [P, T], F32, h)
            Z["na_swap"] = sb("na_swap_s", [P, P], F32, h)
            Z["na_flip"] = sb("na_flip_s", [P, P], F32, h)
            Z["na_mask"] = sb("na_mask_s", [P, GRID_W], F32, h)
        with ExitStack() as h:
            qk = sb("qk", [P, 8, TT], F32, h)
            v_na = sb("v_na", [P, 4, NA_WIDTH], F32, h)
            ut = sb("ut", [P, 4, TT], F32, h)
            bias = sb("bias", [P, 2, NA_HEADS, T], F32, h)
            prob = sb("prob", [P, 3, TT], F32, h)
            probT = sb("probT", [P, 2, 4, T], F32, h)
        with ExitStack() as h:
            rows_in = sb("rows_in", [P, 4, P], F32, h)
            x_in = sb("x_in", [P, 2, 2, D], F32, h)
            zero_pad = sb("zero_pad", [P, 127], F32, h)
        with ExitStack() as h:
            qg = sb("qg", [P, GLA_HEADS, T], F32, h)
            kg = sb("kg", [P, GLA_HEADS, T], F32, h)
            v_g = sb("v_g", [P, 2, D], F32, h)
            L = sb("decay_sum", [P, GLA_HEADS, T], F32, h)
            e_l = sb("e_l", [P, GLA_HEADS, T], F32, h)
            e_end = sb("e_end", [P, GLA_HEADS, T], F32, h)
            e_pos = sb("e_pos", [P, GLA_HEADS, T], F32, h)
            e_neg = sb("e_neg", [P, GLA_HEADS, T], F32, h)
            q_low = sb("q_low", [P, GLA_HEADS, T], F32, h)
            k_low = sb("k_low", [P, GLA_HEADS, T], F32, h)
            k_tok = sb("k_tok", [P, 2, GLA_HEADS, P], F32, h)
            state = sb("state", [P, GLA_HEADS, GLA_DV], F32, h)
            sc_g = sb("sc_g", [P, 2, GLA_HEADS, CHUNK], F32, h)
            w_glr = sb("w_glr", [P, DK, GLA_RANK], F32, h)
            g_end = sb("g_end", [P, GLA_HEADS * 4], F32, h)
            g_rank = sb("g_rank", [GLA_RANK, T], F32, h)
            w_gate = sb("w_gate", [GLA_RANK, GLA_HEADS * P], F32, h)
        with ExitStack() as h:
            sb("region_h_2", [P, 16 * 1024], F32, h)
            r_gate = sb("r_gate", [P, DK, T], F32, h)
            g_low = sb("g_low", [P, CHUNK], F32, h)
            g_up = sb("g_up", [P, CHUNK], F32, h)
            g_carry = sb("g_carry", [P, GLA_HEADS * T], F32, h)
        with ExitStack() as h:
            qn = sb("qn", [P, 8, T], F32, h)
            qr = sb("qr", [P, 8, T], F32, h)
            qs = sb("qs", [P, 8, T], F32, h)
            kn = sb("kn", [P, 8, T], F32, h)
            v_m = sb("v_m", [P, 2, 8 * MLA_V], F32, h)
            kr = sb("kr", [P, 2, T], F32, h)
            c_in = sb("c_in", [P, 4, T], F32, h)
            cos_m = sb("cos_m", [P, T], F32, h)
            sin_m = sb("sin_m", [P, T], F32, h)
            mask_m = sb("mask_m", [P, 2, T], F32, h)
            prob_m = sb("prob_m", [P, 3, T], F32, h)
            probT_m = sb("probT_m", [P, 2, 2, T], F32, h)
            ang = sb("ang", [P, 3, T], F32, h)
            pos_i = sb("pos_i", [P, T], I32, h)
            freq = sb("freq", [P, 2], F32, h)
        with ExitStack() as h:
            cb = sb("cb", [P, DK, T], F32, h)
            cc = sb("cc", [P, DK, T], F32, h)
            cu = sb("cu", [P, DK, T + 2], F32, h)
        with ExitStack() as h:
            pj = sb("pj", [P, DK, T], F32, h)
            p_in = sb("p_in", [P, 2, T], F32, h)
            p_hi = sb("p_hi", [P, 2, T], F32R, h)
            p_lo = sb("p_lo", [P, 2, T], F32R, h)
            o_tok = sb("o_tok", [P, 2, D], F32, h)
        h_hi2 = h_hi[:].rearrange("p a (b t) -> p (a b) t", t=T)
        h_lo2 = h_lo[:].rearrange("p a (b t) -> p (a b) t", t=T)
        rpb_pad = nc.dram_tensor("rpb_pad", [DEPTH, NA_HEADS * (2 * NA_KH - 1), 127], F32)

        total = []

        def walk(who, e):
            S = Signals(sems)
            pe, act, dve, pool, sp = (who == x for x in ("pe", "act", "dve", "pool", "sp"))
            at = Place()
            h_hi_f = h_hi[:].rearrange("p a t -> p (a t)")
            h_lo_f = h_lo[:].rearrange("p a t -> p (a t)")
            z_f = z[:].rearrange("p a t -> p (a t)")
            xt_f = xt[:].rearrange("p a t -> p (a t)")

            def val(n, i, step):
                return n if i is None else i * step + n

            def part(flat, col, i, step, n):
                return flat[:, col:col + n] if i is None else flat[:, bass.ds(i * step + col, n)]

            def border():
                if pe or act or dve or pool:
                    for s in (S.act, S.dve, S.pe, S.pool, S.act_evicted, S.dve_evicted, S.hidden_hi, S.hidden_lo, S.mod_rows, S.mod_done):
                        if s.n and not (pe and s is S.pe):
                            e.wait_ge(s.sem, s.n)
                    if at.slot and not pe:
                        e.wait_ge(S.slot_used.sem, 2 * at.slot)

            def rep(times, body):
                if times == 1:
                    body(None)
                elif pe or act or dve or sp:
                    with e.Fori(0, times) as i:
                        body(i)

            def load(n, i, step, src, kt=DK, width=SC, view=None):
                if not sp:
                    return
                dst = w_raw[:, n % RAW, 0:kt, 0:width] if view is None else view(w_raw[:, n % RAW, :, :])
                s = src()
                if n >= RAW:
                    count = val(2 * (n - RAW + 1), i, 2 * step)
                    if i is not None:
                        count = e.snap(count)
                    e.wait_ge(S.lo_ready.sem, count)
                e.dma_start(dst, s).then_inc(landed[n % RAW], 16)

            def cut(m, i=None, step=0):
                if total and m >= total[0]:
                    return
                for half in range(2):
                    c = slice(half * P, half * P + P)
                    raw, hi, lo = w_raw[:, m % RAW, :, c], w_hi[:, m % CUT, :, c], w_lo[:, m % CUT, :, c]
                    if act:
                        if half == 0:
                            e.wait_ge(landed[m % RAW], val(16 * (m // RAW + 1), i, 16 * step // RAW))
                        if m >= CUT:
                            e.wait_ge(S.slot_used.sem, val(2 * (m - CUT) + half + 1, i, 2 * step))
                        e.activation(hi, raw, ACT.Copy).then_inc(S.hi_ready.sem, 1)
                    if dve:
                        e.wait_ge(S.hi_ready.sem, val(2 * m + half + 1, i, 2 * step))
                        e.tensor_tensor(lo, raw, hi.bitcast(F32), ALU.subtract).then_inc(S.lo_ready.sem, 1)

            def ahead(n, i, step):
                cut(n + CUT, i, step)

            def three(dst, hi, lo, rhs_hi, rhs_lo, start, stop):
                e.matmul(dst, hi, rhs_hi, start=start, stop=False)
                e.matmul(dst, hi, rhs_lo, start=False, stop=False)
                return e.matmul(dst, lo, rhs_hi, start=False, stop=stop)

            def slot_products(n, i, step, kt, k0, rhs, dsts, first=True, last=True):
                halves = 2 // len(dsts)
                for m, dst in enumerate(dsts):
                    e.wait_ge(S.lo_ready.sem, val(2 * n + m + halves, i, 2 * step))
                    for k in range(kt):
                        r_hi, r_lo = rhs(k0 + k)
                        mm = three(dst, w_hi[:, n % CUT, k, m * P:m * P + P], w_lo[:, n % CUT, k, m * P:m * P + P],
                                   r_hi, r_lo, first and k == 0, last and k == kt - 1)
                    mm.then_inc(S.slot_used.sem, halves)

            def matrix(w):
                return w.rearrange("(k p) m -> p k m", p=P)

            def mod_rows(n, i, step, j, per):
                layer, ms = at.mod_layer, at.mod_slot + j
                w = matrix(A["w_mod"][layer])
                b, count = bank[4 + j % 2][0:4, 0:SC], S.mod_rows.n + j
                load(n, i, step, lambda: w[:, :, ms * SC:ms * SC + SC] if i is None
                     else w[:, :, bass.ds(e.snap(i * (per * SC) + ms * SC), SC)])
                if pe:
                    if count > 1:
                        e.wait_ge(S.mod_rows.sem, val(count - 1, i, per))
                    e.wait_ge(S.lo_ready.sem, val(2 * n + 2, i, 2 * step))
                    for k in range(DK):
                        e.matmul(b, c_cut[:, k, :], w_hi[:, n % CUT, k, :], start=k == 0, stop=False)
                        mm = e.matmul(b, c_cut[:, k, :], w_lo[:, n % CUT, k, :], start=False, stop=k == DK - 1)
                    mm.then_inc(S.slot_used.sem, 2)
                ahead(n, i, step)
                if dve:
                    e.wait_ge(S.slot_used.sem, val(2 * n + 2, i, 2 * step))
                    if count > 1:
                        e.wait_ge(S.mod_turned.sem, val(count - 1, i, per))
                    e.tensor_copy(rows_mod[:, j % 2, :], b).then_inc(S.mod_rows.sem, 1)

            def mod_turn(i, j, per):
                t = (at.mod_layer * MOD_SLOTS + at.mod_slot + j) * 2
                b, count = bank[6 + j % 2], S.mod_rows.n + j
                if pe:
                    e.wait_ge(S.mod_rows.sem, val(count + 1, i, per))
                    if count > 1:
                        e.wait_ge(S.mod_done.sem, val(2 * count - 2, i, 2 * per))
                    for m in range(2):
                        mm = e.matmul(b[:, 2 * m:2 * m + 2], rows_mod[:, j % 2, m * P:m * P + P], mod_sum[:, :], start=True, stop=True)
                    mm.then_inc(S.mod_turned.sem, 1)
                if act:
                    e.wait_ge(S.mod_turned.sem, val(count + 1, i, per))
                    for m in range(2):
                        e.activation(part(mod[:], 2 * (t + m), i, 4 * per, 2), b[:, 2 * m:2 * m + 2], ACT.Identity,
                                     bias=part(cols[:], COL["b_mod"] + t + m, i, 2 * per, 1)).then_inc(S.mod_done.sem, 1)

            def mods_done(count):
                S.mod_rows.n += count
                S.mod_turned.n += count
                S.mod_done.n += 2 * count
                at.mod_slot += count
                if at.mod_slot == MOD_SLOTS:
                    at.mod_layer, at.mod_slot = at.mod_layer + 1, 0

            def mods(passes, per):
                def body(i):
                    for j in range(per):
                        mod_rows(at.slot + j, i, per, j, per)
                        if j:
                            mod_turn(i, j - 1, per)
                    mod_turn(i, per - 1, per)
                rep(passes, body)
                at.slot += passes * per
                mods_done(passes * per)

            def mod_vec(layer, chunk):
                o = (layer * N_MOD + chunk) * DK * 2
                return mod[:, o:o + 2 * DK].rearrange("p (k s) -> p k s", s=2)

            def gemm(w, kgs, pairs, per, rhs, evict, by, mod_per=0, first_col=0):
                each = len(kgs) + mod_per
                step = per * each
                base = by.n
                if dve and mod_per:
                    e.wait_ge(S.dve.sem, S.dve.n)
                if pe:
                    e.wait_ge(S.act_evicted.sem, S.act_evicted.n)
                    e.wait_ge(S.dve_evicted.sem, S.dve_evicted.n)
                wm = matrix(w) if sp else None

                def body(i):
                    for p in range(per):
                        n = at.slot + p * each
                        b = bank[2 * (p % 2):2 * (p % 2) + 2]
                        for g, (k0, kt) in enumerate(kgs):
                            if mod_per:
                                mod_rows(n, i, step, p * mod_per + g, per * mod_per)
                                n += 1
                            col = first_col + p * SC
                            load(n, i, step, lambda: wm[:, k0:k0 + kt, col:col + SC] if i is None
                                 else wm[:, k0:k0 + kt, bass.ds(e.snap(i * (per * SC) + col), SC)], kt)
                            if pe:
                                if g == 0 and (p >= 2 or i is not None):
                                    e.wait_ge(by.sem, val(base + 2 * (p - 1), i, 2 * per))
                                slot_products(n, i, step, kt, k0, rhs, b_ap(b), g == 0, g == len(kgs) - 1)
                            ahead(n, i, step)
                            if mod_per:
                                mod_turn(i, p * mod_per + g, per * mod_per)
                            n += 1
                        evict(i, p, per, lambda m: val(2 * n - 1 + m, i, 2 * step), b)
                width = rhs(0)[0].shape[-1]

                def b_ap(b):
                    return [x[:, 0:width] for x in b]
                rep(pairs // per, body)
                at.slot += pairs * each
                by.n += 2 * pairs
                if mod_per:
                    mods_done(mod_per * pairs)

            def hidden_at(flat, p, m, i, per, n):
                return part(flat, (2 * p + m) * n, i, 2 * per * n, n)

            def cut_hidden(i, p, per, n, base):
                for m in range(2):
                    if act:
                        e.wait_ge(S.dve_evicted.sem, val(base[0] + 2 * p + m + 1, i, 2 * per))
                        e.activation(hidden_at(h_hi_f, p, m, i, per, n), tmp_y[:, m, 0:n], ACT.Copy).then_inc(S.hidden_hi.sem, 1)
                for m in range(2):
                    if dve:
                        e.wait_ge(S.hidden_hi.sem, val(base[1] + 2 * p + m + 1, i, 2 * per))
                        e.tensor_tensor(hidden_at(h_lo_f, p, m, i, per, n), tmp_y[:, m, 0:n],
                                        hidden_at(h_hi_f, p, m, i, per, n).bitcast(F32), ALU.subtract).then_inc(S.hidden_lo.sem, 1)

            def gate_up(w, t0, pairs, n, mod_per):
                per = 1 if mod_per else 2
                each = 2 + mod_per
                step = per * each
                wm = matrix(w) if sp else None
                if dve and mod_per:
                    e.wait_ge(S.dve.sem, S.dve.n)
                if pe:
                    e.wait_ge(S.act_evicted.sem, S.act_evicted.n)
                    e.wait_ge(S.dve_evicted.sem, S.dve_evicted.n)
                base = Counts(a=S.act_evicted.n, d=S.dve_evicted.n, h=S.hidden_hi.n, l=S.hidden_lo.n, slot=at.slot)

                def body(i, p0, per):
                    for p in range(p0, p0 + per):
                        s = base.slot + p * each - 1
                        for half in range(2):
                            s += 1
                            if mod_per:
                                mod_rows(s, i, step, half, 2)
                                s += 1
                            col = half * D_FF + t0 * P + p * SC
                            load(s, i, step, lambda: wm[:, :, col:col + SC] if i is None
                                 else wm[:, :, bass.ds(e.snap(i * (per * SC) + col), SC)])
                            if pe:
                                by, b0 = (S.dve_evicted, base.d) if half else (S.act_evicted, base.a)
                                e.wait_ge(by.sem, val(b0 + 2 * p, i, 2 * per))
                                slot_products(s, i, step, DK, 0, lambda k: (a_hi[:, k, 0:n], a_lo[:, k, 0:n]),
                                              [bank[2 * half][:, 0:n], bank[2 * half + 1][:, 0:n]])
                            ahead(s, i, step)
                            if mod_per:
                                mod_turn(i, half, 2)
                            if act and half == 0:
                                for m in range(2):
                                    e.wait_ge(S.slot_used.sem, val(2 * s + m + 1, i, 2 * step))
                                    e.wait_ge(S.dve_evicted.sem, val(base.d + 2 * p - 1 + m, i, 2 * per))
                                    e.activation(tmp_g[:, m, 0:n], bank[m][:, 0:n], ACT.Silu).then_inc(S.act_evicted.sem, 1)
                        if dve:
                            for m in range(2):
                                e.wait_ge(S.slot_used.sem, val(2 * s + m + 1, i, 2 * step))
                                e.wait_ge(S.act_evicted.sem, val(base.a + 2 * p + m + 1, i, 2 * per))
                                e.wait_ge(S.hidden_hi.sem, val(base.h + 2 * p - 1 + m, i, 2 * per))
                                e.wait_ge(S.hidden_lo.sem, val(base.l + 2 * p - 1 + m, i, 2 * per))
                                e.tensor_tensor(tmp_y[:, m, 0:n], tmp_g[:, m, 0:n], bank[2 + m][:, 0:n],
                                                ALU.mult).then_inc(S.dve_evicted.sem, 1)
                        cut_hidden(i, p, per, n, (base.d, base.h))
                rep(pairs // per, lambda i: body(i, 0, per))
                if pairs % per:
                    body(None, pairs - 1, 1)
                at.slot += pairs * each
                for s in (S.act_evicted, S.dve_evicted, S.hidden_hi, S.hidden_lo):
                    s.n += 2 * pairs
                if mod_per:
                    mods_done(mod_per * pairs)

            def to_z(n, add=False):
                def evict(i, p, per, used, b):
                    for m in range(2):
                        dst = part(z_f, (2 * p + m) * TT, i, 2 * per * TT, n)
                        if act and not add:
                            e.wait_ge(S.slot_used.sem, used(m))
                            e.activation(dst, b[m][:, 0:n], ACT.Copy).then_inc(S.act_evicted.sem, 1)
                        if dve and add:
                            e.wait_ge(S.slot_used.sem, used(m))
                            e.tensor_tensor(dst, dst, b[m][:, 0:n], ALU.add).then_inc(S.dve_evicted.sem, 1)
                return evict

            def residual_to_z(i, p, per, used, b):
                if dve:
                    for m in range(2):
                        e.wait_ge(S.slot_used.sem, used(m))
                        c = (2 * p + m) * TT
                        e.scalar_tensor_tensor(out=part(z_f, c, i, 2 * per * TT, T), in0=part(xt_f, c, i, 2 * per * TT, T),
                                               scalar=ALPHA, in1=b[m][:, 0:T], op0=ALU.mult,
                                               op1=ALU.add).then_inc(S.dve_evicted.sem, 1)

            def copy_to(flat, width, n, scale=1.0, func=ACT.Copy):
                def evict(i, p, per, used, b):
                    if act:
                        for m in range(2):
                            e.wait_ge(S.slot_used.sem, used(m))
                            e.activation(part(flat, (2 * p + m) * width, i, 2 * per * width, n), b[m][:, 0:n],
                                         func, scale=scale).then_inc(S.act_evicted.sem, 1)
                return evict

            def a_op(n):
                return lambda k: (a_hi[:, k, 0:n], a_lo[:, k, 0:n])

            def token_major(w, first_col, slots, n, dst):
                tb = n // P
                wm = matrix(w) if sp else None
                if pe:
                    e.wait_ge(S.act_evicted.sem, S.act_evicted.n)
                    e.wait_ge(S.dve_evicted.sem, S.dve_evicted.n)
                for s in range(slots):
                    nn = at.slot
                    load(nn, None, 0, lambda: wm[:, :, first_col + s * SC:first_col + (s + 1) * SC])
                    if pe:
                        e.wait_ge(S.lo_ready.sem, 2 * nn + 2)
                        if s:
                            e.wait_ge(S.dve_evicted.sem, S.dve_evicted.n)
                        for t in range(tb):
                            for k in range(DK):
                                x_hi, x_lo = (x[:, k, t * P:t * P + P] for x in (a_hi, a_lo))
                                v_hi, v_lo = (x[:, nn % CUT, k, :] for x in (w_hi, w_lo))
                                mm = three(bank[t][:, 0:SC], x_hi, x_lo, v_hi, v_lo, k == 0, k == DK - 1)
                        mm.then_inc(S.slot_used.sem, 2)
                    ahead(nn, None, 0)
                    if dve:
                        e.wait_ge(S.slot_used.sem, 2 * nn + 2)
                        for t in range(tb):
                            e.tensor_copy(dst(t, s), bank[t][:, 0:SC]).then_inc(S.dve_evicted.sem, 1)
                    S.dve_evicted.n += tb
                    at.slot += 1

            def column_sums(src, tiles, n, square):
                base = S.pe.n
                for k in range(tiles):
                    if square:
                        if act:
                            if k >= 2:
                                e.wait_ge(S.pe.sem, base + k - 1)
                            e.activation(tmp_g[:, k % 2, 0:n], src(k), ACT.Square).then_inc(S.act.sem, 1)
                        S.act.n += 1
                    if pe:
                        e.wait_ge(S.act.sem, S.act.n)
                        e.matmul(bank[6][:, 0:n], ones[:, :], tmp_g[:, k % 2, 0:n] if square else src(k),
                                 start=k == 0, stop=k == tiles - 1).then_inc(S.pe.sem, 1)
                S.pe.n += tiles

            def inverse_root(n, scale, eps):
                if act:
                    e.wait_ge(S.pe.sem, S.pe.n)
                    e.activation(r_tmp[:, 0:n], bank[6][:, 0:n], ACT.Sqrt, bias=stat[:, eps:eps + 1], scale=scale).then_inc(S.act.sem, 1)
                S.act.n += 1
                if dve:
                    e.wait_ge(S.act.sem, S.act.n)
                    e.reciprocal(r_tmp[:, 0:n], r_tmp[:, 0:n]).then_inc(S.dve.sem, 1)
                S.dve.n += 1

            def vec(name, row, n=1):
                return cols[:, COL[name] + row:COL[name] + row + n]

            def streams(n):
                return [(s, slice(s * T, s * T + T)) for s in range(n // T)]

            def factor(layer, g_row, chunk, add, times):
                if dve:
                    g = vec("norm_g", (layer * 6 + g_row) * DK, DK).unsqueeze(2).to_broadcast([P, DK, 2])
                    e.scalar_tensor_tensor(out=fac[:, :, :], in0=mod_vec(layer, chunk), scalar=add if add else times,
                                           in1=g, op0=ALU.add if add else ALU.mult, op1=ALU.mult).then_inc(S.dve.sem, 1)
                S.dve.n += 1

            def pre_norm(layer, g_row, chunk, n):
                border()
                column_sums(lambda k: xt[:, k, 0:n], DK, n, True)
                inverse_root(n, 1.0, 0)
                factor(layer, g_row, chunk + 1, 1.0, None)
                if dve:
                    e.wait_ge(S.dve.sem, S.dve.n)
                shift = mod_vec(layer, chunk)
                tiles = [(k, s, c) for k in range(DK) for s, c in streams(n)]
                base_a, base_d = S.act.n, S.dve.n
                for j, (k, s, c) in enumerate(tiles):
                    if dve:
                        e.scalar_tensor_tensor(out=z[:, k, c], in0=xt[:, k, c], scalar=fac[:, k, s:s + 1],
                                               in1=r_tmp[:, c], op0=ALU.mult, op1=ALU.mult).then_inc(S.dve.sem, 1)
                    if act:
                        e.wait_ge(S.dve.sem, base_d + j + 1)
                        e.activation(a_hi[:, k, c], z[:, k, c], ACT.Identity, bias=shift[:, k, s:s + 1]).then_inc(S.act.sem, 1)
                for j, (k, s, c) in enumerate(tiles):
                    if dve:
                        e.wait_ge(S.act.sem, base_a + j + 1)
                        e.scalar_tensor_tensor(out=a_lo[:, k, c], in0=z[:, k, c], scalar=shift[:, k, s:s + 1],
                                               in1=a_hi[:, k, c].bitcast(F32), op0=ALU.add,
                                               op1=ALU.subtract).then_inc(S.dve.sem, 1)
                S.act.n += len(tiles)
                S.dve.n += 2 * len(tiles)
                if pe:
                    e.wait_ge(S.dve.sem, S.dve.n)

            def post_norm(layer, g_row, chunk, n, times):
                border()
                column_sums(lambda k: z[:, k, 0:n], DK, n, True)
                inverse_root(n, 1.0, 0)
                factor(layer, g_row, chunk, None, times)
                base = S.dve.n
                tiles = [(k, s, c) for k in range(DK) for s, c in streams(n)]
                if dve:
                    e.wait_ge(S.dve.sem, S.dve.n)
                    for k, s, c in tiles:
                        e.scalar_tensor_tensor(out=z[:, k, c], in0=z[:, k, c], scalar=fac[:, k, s:s + 1],
                                               in1=r_tmp[:, c], op0=ALU.mult, op1=ALU.mult).then_inc(S.dve.sem, 1)
                    for j, (k, s, c) in enumerate(tiles):
                        e.wait_ge(S.dve.sem, base + j + 1)
                        e.tensor_tensor(xt[:, k, c], xt[:, k, c], z[:, k, c], ALU.add).then_inc(S.dve.sem, 1)
                S.dve.n += 2 * len(tiles)

            def ffn(layer, f, n, mod_a, mod_down, mod_b):
                pre_norm(layer, 4 * f, 6 * f, n)
                parts = [(0, 16), (16, FT - 16)] if n == TT else [(0, FT)]
                w_gu, w_d = A["w_ffn_gate_up"][layer, f], A["w_ffn_down"][layer, f]
                for j, (t0, tiles) in enumerate(parts):
                    gate_up(w_gu, t0, tiles // 2, n, (mod_a, mod_b)[j])
                    if pe:
                        e.wait_ge(S.hidden_lo.sem, S.hidden_lo.n)
                    if dve:
                        e.wait_ge(S.act_evicted.sem, S.act_evicted.n)
                    kgs = [(k, min(DK, tiles - k)) for k in range(0, tiles, DK)]
                    rhs = (lambda k: (h_hi_f[:, k * n:k * n + n], h_lo_f[:, k * n:k * n + n]))
                    gemm(w_d[t0 * P:(t0 + tiles) * P, :], kgs, 4, 4, rhs, to_z(n, add=j > 0),
                         S.dve_evicted if j else S.act_evicted, mod_per=0 if j else mod_down)
                post_norm(layer, 4 * f + 1, 6 * f + 2, n, 0.5)

            def attention(units, v_of, p_buf, pt_buf, finish, vm):
                U = len(units)
                first = {"act": S.act.n, "dve": S.dve.n, "pe": S.pe.n}
                order = {"act": [], "dve": [], "pe": []}
                for t in range(U + 2):
                    if t < U:
                        order["pe"].append(("scores", t))
                        order["act"] += [("copy", t)] * (units[t]["biased"] < units[t]["keys"])
                        order["dve"] += [("bias", t)] * (units[t]["biased"] > 0) + [("max", t)]
                    if 0 <= t - 1 < U:
                        order["act"].append(("exp", t - 1))
                        order["dve"] += [("recip", t - 1), ("norm", t - 1)]
                        order["pe"].append(("turn", t - 1))
                    if 0 <= t - 2 < U:
                        order["dve"].append(("turned", t - 2))
                        if (t - 2) % 2:
                            order["pe"].append(("pv", t - 2))
                            if ((t - 2) // 2) % vm == vm - 1:
                                order["act"].append(("o_hi", t - 2))
                                order["dve"].append(("o_lo", t - 2))
                count = {step: (name, first[name] + j + 1) for name in order for j, step in enumerate(order[name])}
                signal = {"act": S.act, "dve": S.dve, "pe": S.pe}

                def after(kind, u):
                    if (kind, u) in count:
                        name, n = count[(kind, u)]
                        e.wait_ge(signal[name].sem, n)

                for kind, u in order.get(who, []):
                    x = units[u]
                    n, b = x["keys"], x["biased"]
                    pr, head = p_buf[:, u % 3, 0:n], u // 2
                    s_bank, t_bank, o_bank = bank[u % 2], bank[2 + u % 2], bank[4 + head // vm % 2]
                    top, den, inv = (stat[:, o + u % 2:o + u % 2 + 1] for o in (2, 4, 6))
                    if kind == "scores":
                        after("bias", u - 2)
                        after("copy", u - 2)
                        after("max", u - 2)
                        for j, (lhs, rhs) in enumerate(x["scores"]):
                            mm = e.matmul(s_bank[:, 0:n], lhs, rhs, start=j == 0, stop=j == len(x["scores"]) - 1)
                        mm.then_inc(S.pe.sem, 1)
                    elif kind == "copy":
                        after("scores", u)
                        after("turn", u - 3)
                        e.activation(pr[:, b:n], s_bank[:, b:n], ACT.Copy).then_inc(S.act.sem, 1)
                    elif kind == "bias":
                        after("scores", u)
                        after("copy", u)
                        after("turn", u - 3)
                        e.tensor_tensor(pr[:, 0:b], s_bank[:, 0:b], x["bias"], ALU.add).then_inc(S.dve.sem, 1)
                    elif kind == "max":
                        after("bias", u)
                        after("copy", u)
                        after("exp", u - 2)
                        e.tensor_reduce(top, pr, AX.X, ALU.max, negate=True).then_inc(S.dve.sem, 1)
                    elif kind == "exp":
                        after("max", u)
                        after("recip", u - 2)
                        e.activation(pr, pr, ACT.Exp, bias=top, accum_out=den).then_inc(S.act.sem, 1)
                    elif kind == "recip":
                        after("exp", u)
                        e.reciprocal(inv, den).then_inc(S.dve.sem, 1)
                    elif kind == "norm":
                        after("recip", u)
                        e.tensor_scalar(pr, pr, inv, None, ALU.mult).then_inc(S.dve.sem, 1)
                    elif kind == "turn":
                        after("norm", u)
                        after("turned", u - 2)
                        for kb in range(n // P):
                            mm = e.transpose(t_bank[:, kb * P:kb * P + P], pr[:, kb * P:kb * P + P], eye[:, :])
                        mm.then_inc(S.pe.sem, 1)
                    elif kind == "turned":
                        after("turn", u)
                        after("pv", (u | 1) - 4)
                        e.tensor_copy(pt_buf[:, head % 2, 0:n // P, (u % 2) * P:(u % 2) * P + P],
                                      t_bank[:, 0:n].rearrange("p (k q) -> p k q", q=P)).then_inc(S.dve.sem, 1)
                    elif kind == "pv":
                        after("turned", u)
                        if head % vm == 0:
                            after("o_lo", 2 * (head - vm - 1) + 1)
                        for kb in range(n // P):
                            lhs, row = v_of(x, kb)
                            mm = e.matmul(o_bank[row:row + P // vm, 0:T], lhs, pt_buf[:, head % 2, kb, :],
                                          start=kb == 0, stop=kb == n // P - 1)
                        mm.then_inc(S.pe.sem, 1)
                    elif kind == "o_hi":
                        after("pv", u)
                        e.activation(finish(x, a_hi), o_bank[:, 0:T], ACT.Copy).then_inc(S.act.sem, 1)
                    elif kind == "o_lo":
                        after("o_hi", u)
                        e.tensor_tensor(finish(x, a_lo), o_bank[:, 0:T], finish(x, a_hi).bitcast(F32), ALU.subtract).then_inc(S.dve.sem, 1)
                S.act.n += len(order["act"])
                S.dve.n += len(order["dve"])
                S.pe.n += len(order["pe"])

            def side_load(dst, src):
                if pool:
                    e.dma_start(dst, src).then_inc(side_sem, 16)
                at.side += 16

            def side_wait():
                e.wait_ge(side_sem, at.side)

            def begin():
                if pool:
                    e.memset(ones[:, :], 1.0 / D).then_inc(S.pool.sem, 1)
                    e.memset(stat[:, 0:1], RMS_EPS).then_inc(S.pool.sem, 1)
                    e.memset(stat[:, 1:2], LN_EPS).then_inc(S.pool.sem, 1)
                    e.memset(stat[:, 8:9], 1.0).then_inc(S.pool.sem, 1)
                    e.memset(zero_pad[:, :], 0.0).then_inc(S.pool.sem, 1)
                S.pool.n += 5
                side_load(eye[:, :], C["eye"][:])
                side_load(mod_sum[:, :], C["mod_sum"][:])
                for name, rows in VECTORS:
                    flat = A[name]
                    if len(flat.shape) == 2:
                        flat = flat.rearrange("a b -> (a b)")
                    elif len(flat.shape) == 3:
                        flat = flat.rearrange("a b c -> (a b c)")
                    flat = flat.rearrange("(r c) -> r c", c=P)
                    r = 0
                    while r < rows:
                        g, o = divmod(COL[name] + r, P)
                        n = min(rows - r, P - o)
                        side_load(rows_in[o:o + n, g, :], flat[r:r + n, :])
                        r += n
                for s, name in enumerate(("x", "ctx")):
                    side_load(x_in[:, s, :, :], A[name][0].rearrange("(b p) d -> p b d", p=P))
                cut(0)
                cut(1)
                groups = -(-N_COLS // P)
                for g in range(groups):
                    n = min(P, N_COLS - g * P)
                    if pe:
                        if g == 0:
                            side_wait()
                        e.transpose(bank[g][:, 0:n], rows_in[0:n, g, :], eye[0:n, 0:n]).then_inc(S.pe.sem, 1)
                    S.pe.n += 1
                    if dve:
                        e.wait_ge(S.pe.sem, S.pe.n)
                        e.tensor_copy(cols[:, g * P:g * P + n], bank[g][:, 0:n]).then_inc(S.dve.sem, 1)
                    S.dve.n += 1
                if act:
                    e.wait_ge(S.dve.sem, S.dve.n)
                    e.activation(c_act[:, :, 0], vec("c", 0, DK), ACT.Silu).then_inc(S.act.sem, 1)
                    e.activation(c_act[:, :, 1], vec("c_ctx", 0, DK), ACT.Silu).then_inc(S.act.sem, 1)
                    e.wait_ge(S.act.sem, S.act.n + 2)
                S.act.n += 2
                for s in range(2):
                    if act:
                        e.activation(c_cut[:, :, s], c_act[:, :, s], ACT.Copy).then_inc(S.hidden_hi.sem, 1)
                    S.hidden_hi.n += 1
                    if dve:
                        e.wait_ge(S.hidden_hi.sem, S.hidden_hi.n)
                        e.tensor_tensor(c_cut[:, :, 2 + s], c_act[:, :, s], c_cut[:, :, s].bitcast(F32), ALU.subtract).then_inc(S.hidden_lo.sem, 1)
                    S.hidden_lo.n += 1
                if pe:
                    e.wait_ge(S.hidden_lo.sem, S.hidden_lo.n)
                for j, (k, s) in enumerate((k, s) for k in range(DK) for s in range(2)):
                    by = S.act_evicted if s else S.dve_evicted
                    if pe:
                        if k >= 2:
                            e.wait_ge(by.sem, by.n - 1)
                        for b in range(2):
                            mm = e.transpose(bank[j % 4][:, b * P:b * P + P], x_in[:, s, b, k * P:k * P + P], eye[:, :])
                        mm.then_inc(S.pe.sem, 1)
                    S.pe.n += 1
                    if dve and s == 0:
                        e.wait_ge(S.pe.sem, S.pe.n)
                        e.tensor_copy(xt[:, k, 0:T], bank[j % 4][:, 0:T]).then_inc(by.sem, 1)
                    if act and s == 1:
                        e.wait_ge(S.pe.sem, S.pe.n)
                        e.activation(xt[:, k, T:TT], bank[j % 4][:, 0:T], ACT.Copy).then_inc(by.sem, 1)
                    by.n += 1
                n_rows = NA_HEADS * (2 * NA_KH - 1)
                if pool:
                    side_wait()
                    e.wait_ge(S.pool.sem, S.pool.n)
                for l in range(DEPTH):
                    side_load(rpb_pad[l, :, :], zero_pad[0:n_rows, :])
                if pool:
                    side_wait()
                for l in range(DEPTH):
                    side_load(rpb_pad[l, :, GRID_W - NA_KW:GRID_W + NA_KW - 1], A["na_rpb"][l].rearrange("h a b -> (h a) b"))
                if pool or act or dve:
                    side_wait()

            def rope_na():
                base_p, base_d = S.pe.n, S.dve.n
                for j in range(8):
                    b = bank[6 + j % 2][:, 0:T]
                    if pe:
                        if j >= 2:
                            e.wait_ge(S.dve.sem, base_d + 3 * (j - 1))
                        e.matmul(b, Z["na_swap"][:, :], qk[:, j, 0:T], start=True, stop=True).then_inc(S.pe.sem, 1)
                    if dve:
                        e.tensor_tensor(tmp_g[:, j % 2, 0:T], qk[:, j, 0:T], Z["na_cos"][:, :], ALU.mult).then_inc(S.dve.sem, 1)
                        e.wait_ge(S.pe.sem, base_p + j + 1)
                        e.tensor_tensor(tmp_y[:, j % 2, 0:T], b, Z["na_sin"][:, :], ALU.mult).then_inc(S.dve.sem, 1)
                        e.wait_ge(S.dve.sem, base_d + 3 * j + 2)
                        e.tensor_tensor(qk[:, j, 0:T], tmp_g[:, j % 2, 0:T], tmp_y[:, j % 2, 0:T], ALU.add).then_inc(S.dve.sem, 1)
                S.pe.n += 8
                S.dve.n += 24

            def pool_windows(n):
                if pool:
                    side_wait()
                    e.wait_ge(S.act_evicted.sem, S.act_evicted.n)
                def step(op):
                    if pool:
                        op().then_inc(S.pool.sem, 1)
                        e.wait_ge(S.pool.sem, S.pool.n + 1)
                    S.pool.n += 1
                views = [(lambda t: t[:, 0:320].rearrange("p (r c) -> p r c", r=ROWS), GRID_W, Z["pool_row"], slice(0, T), ROWS)]
                if n == TT:
                    views.append((lambda t: t[:, 320:592].rearrange("p (r c) -> p r c", r=1), T, Z["pool_ctx"], slice(T, TT), 1))
                for g, w in enumerate(POOL_WINDOWS):
                    for of, length, inv, tok, rows in views:
                        a, b = of(Z["pool_a"]), of(Z["pool_b"])
                        u = ut[:, g, tok].rearrange("p (r c) -> p r c", r=rows)
                        step(lambda: e.memset(a, 0.0))
                        step(lambda: e.tensor_copy(a[:, :, 8:8 + length], u))
                        have, width = 1, length + 16
                        while have < w:
                            width -= have
                            step(lambda: e.tensor_tensor(b[:, :, 0:width], a[:, :, 0:width], a[:, :, have:have + width], ALU.add))
                            a, b, have = b, a, 2 * have
                        o = 8 - w // 2
                        step(lambda: e.tensor_tensor(b[:, :, 0:length], a[:, :, o:o + length],
                                                     inv[:, g, :].unsqueeze(1).to_broadcast([P, rows, length]), ALU.mult))
                        step(lambda: e.tensor_tensor(u, b[:, :, 0:length], u, ALU.subtract))

            def pool_products(layer, n):
                base_p, base_a, base_d = S.pe.n, S.act.n, S.dve.n
                for g in range(4):
                    b = bank[6 + g % 2][:, 0:n]
                    scale = vec("pool_scale", layer * 4 + g)
                    if pe:
                        if g == 0:
                            e.wait_ge(S.pool.sem, S.pool.n)
                            e.wait_ge(S.dve.sem, S.dve.n)
                        else:
                            e.wait_ge(S.dve.sem, base_d + g - 1) if g >= 2 else None
                        e.matmul(b, Z["w_pool"][:, g, :], ut[:, g, 0:n], start=True, stop=True).then_inc(S.pe.sem, 1)
                    if act:
                        e.wait_ge(S.pe.sem, base_p + g + 1)
                        e.activation(a_hi[:, 4 + g, 0:n], b, ACT.Copy, scale=scale).then_inc(S.act.sem, 1)
                    if dve:
                        e.wait_ge(S.act.sem, base_a + g + 1)
                        e.scalar_tensor_tensor(out=a_lo[:, 4 + g, 0:n], in0=b, scalar=scale, in1=a_hi[:, 4 + g, 0:n].bitcast(F32),
                                               op0=ALU.mult, op1=ALU.subtract).then_inc(S.dve.sem, 1)
                S.pe.n += 4
                S.act.n += 4
                S.dve.n += 4

            def mix(layer, last):
                n = T if last else TT
                pre_norm(layer, 2, 3, TT)
                if pool:
                    side_wait()
                    border()
                for name in ("na_cos", "na_sin", "na_swap", "na_flip", "na_mask", "pool_row", "pool_ctx"):
                    side_load(Z[name][:], C[name][:])
                side_load(Z["w_pool"][:, :, :], A["w_pool"][layer].rearrange("g c d -> c g d"))
                rpb_rows = NA_HEADS * (2 * NA_KH - 1)
                for qt in range(2):
                    for half in range(2):
                        qrow = 2 * qt + half
                        for kr in range(ROWS):
                            src = bass.AP(tensor=rpb_pad, offset=(layer * rpb_rows + NA_KH - 1 + kr - qrow) * 127,
                                          ap=[[1, GRID_W], [(2 * NA_KH - 1) * 127, NA_HEADS], [1, GRID_W]])
                            side_load(bias[half * GRID_W:(half + 1) * GRID_W, qt, :, kr * GRID_W:(kr + 1) * GRID_W], src)
                w = A["w_in"][layer]
                qk_f = qk[:].rearrange("p a t -> p (a t)")
                gemm(w, [(0, DK)], 2, 2, a_op(n), copy_to(qk_f, TT, n, HEAD_DIM ** -0.5), S.act_evicted)
                gemm(w, [(0, DK)], 2, 2, a_op(TT), copy_to(qk_f[:, 4 * TT:], TT, TT), S.act_evicted, first_col=NA_WIDTH)
                gemm(w, [(0, DK)], 2, 2, a_op(n), copy_to(ut[:].rearrange("p a t -> p (a t)"), TT, n), S.act_evicted,
                     first_col=3 * NA_WIDTH)
                pool_windows(n)
                token_major(w, 2 * NA_WIDTH, 2, TT, lambda t, s: v_na[:, t, s * SC:(s + 1) * SC])
                flat = bias[:, :, :, :].rearrange("p q h c -> p (q h c)")
                base_p, base_d = S.pe.n, S.dve.n
                for j in range(8):
                    c, b = slice(j * 512, j * 512 + 512), bank[4 + j % 2]
                    if pe:
                        if j == 0:
                            side_wait()
                        if j >= 2:
                            e.wait_ge(S.dve.sem, base_d + j - 1)
                        e.matmul(b[:, :], Z["na_flip"][:, :], flat[:, c], start=True, stop=True).then_inc(S.pe.sem, 1)
                    if dve:
                        if j == 0:
                            side_wait()
                        e.wait_ge(S.pe.sem, base_p + j + 1)
                        e.tensor_tensor(flat[:, c].rearrange("p (r c) -> p r c", c=GRID_W), b[:, :].rearrange("p (r c) -> p r c", c=GRID_W),
                                        Z["na_mask"][:, :].unsqueeze(1).to_broadcast([P, 512 // GRID_W, GRID_W]), ALU.add).then_inc(S.dve.sem, 1)
                S.pe.n += 8
                S.dve.n += 8
                if not pool:
                    e_border()
                rope_na()
                pe_wait_all()
                units = []
                for h in range(NA_HEADS):
                    rows = slice((h % 2) * HEAD_DIM, (h % 2 + 1) * HEAD_DIM)
                    for q in range(2):
                        units.append(dict(head=h, q=q, keys=TT, biased=T, bias=bias[:, q, h, :],
                                          scores=[(qk[rows, h // 2, q * P:q * P + P], qk[rows, 4 + h // 2, :])]))
                attention(units, lambda x, kb: (v_na[:, kb, x["head"] * HEAD_DIM:(x["head"] + 1) * HEAD_DIM], (x["head"] % 2) * HEAD_DIM),
                          prob, probT, lambda x, buf: buf[:, x["head"] // 2, 0:T], 2)
                if not last:
                    units = []
                    for h in range(NA_HEADS):
                        rows = slice((h % 2) * HEAD_DIM, (h % 2 + 1) * HEAD_DIM)
                        for q in range(2):
                            units.append(dict(head=h, q=q, keys=T, biased=0, bias=None,
                                              scores=[(qk[rows, h // 2, T + q * P:T + q * P + P], qk[rows, 4 + h // 2, T:TT])]))
                    e_border()
                    attention(units, lambda x, kb: (v_na[:, 2 + kb, x["head"] * HEAD_DIM:(x["head"] + 1) * HEAD_DIM], (x["head"] % 2) * HEAD_DIM),
                              prob, probT, lambda x, buf: buf[:, x["head"] // 2, T:TT], 2)
                pool_products(layer, n)
                e_border()
                gemm(A["w_out"][layer], [(0, DK)], 4, 4, a_op(n), to_z(n), S.act_evicted)
                post_norm(layer, 3, 5, n, 1.0)

            def e_border():
                if not pool:
                    border()

            def pe_wait_all():
                if pe:
                    e.wait_ge(S.dve.sem, S.dve.n)

            def cut_x():
                border()
                base_a = S.act.n
                for j in range(4):
                    k = slice(2 * j, 2 * j + 2)
                    if act:
                        e.activation(a_hi[:, k, 0:T], xt[:, k, 0:T], ACT.Copy).then_inc(S.act.sem, 1)
                    if dve:
                        e.wait_ge(S.act.sem, base_a + j + 1)
                        e.tensor_tensor(a_lo[:, k, 0:T], xt[:, k, 0:T], a_hi[:, k, 0:T].bitcast(F32), ALU.subtract).then_inc(S.dve.sem, 1)
                S.act.n += 4
                S.dve.n += 4
                if pe:
                    e.wait_ge(S.dve.sem, S.dve.n)

            def layer_norm(i, j):
                border()
                column_sums(lambda k: z[:, k, 0:T], DK, T, False)
                base_d = S.dve.n
                for k in range(DK):
                    if dve:
                        e.wait_ge(S.pe.sem, S.pe.n)
                        e.tensor_tensor(z[:, k, 0:T], z[:, k, 0:T], bank[6][:, 0:T], ALU.subtract).then_inc(S.dve.sem, 1)
                S.dve.n += DK
                if act or pe:
                    e.wait_ge(S.dve.sem, S.dve.n)
                column_sums(lambda k: z[:, k, 0:T], DK, T, True)
                inverse_root(T, 1.0, 1)
                row = (i * 2 + j) * DK
                base_a, base_d = S.act.n, S.dve.n
                if dve:
                    e.wait_ge(S.dve.sem, S.dve.n)
                for k in range(DK):
                    if dve:
                        e.scalar_tensor_tensor(out=z[:, k, 0:T], in0=z[:, k, 0:T], scalar=vec("ln_g_2", row + k), in1=r_tmp[:, 0:T],
                                               op0=ALU.mult, op1=ALU.mult).then_inc(S.dve.sem, 1)
                    if act:
                        e.wait_ge(S.dve.sem, base_d + k + 1)
                        e.activation(a_hi[:, k, 0:T], z[:, k, 0:T], ACT.Identity, bias=vec("ln_b_2", row + k)).then_inc(S.act.sem, 1)
                if dve:
                    for k in range(DK):
                        e.wait_ge(S.dve.sem, base_d + k + 1)
                        e.tensor_scalar(xt[:, k, 0:T], z[:, k, 0:T], vec("ln_b_2", row + k), None, ALU.add).then_inc(S.dve.sem, 1)
                    for k in range(DK):
                        e.wait_ge(S.act.sem, base_a + k + 1)
                        e.scalar_tensor_tensor(out=a_lo[:, k, 0:T], in0=z[:, k, 0:T], scalar=vec("ln_b_2", row + k),
                                               in1=a_hi[:, k, 0:T].bitcast(F32), op0=ALU.add, op1=ALU.subtract).then_inc(S.dve.sem, 1)
                S.act.n += DK
                S.dve.n += 3 * DK
                if pe:
                    e.wait_ge(S.dve.sem, S.dve.n)

            def mlp(i):
                base = Counts(a=S.act_evicted.n, d=S.dve_evicted.n, h=S.hidden_hi.n, l=S.hidden_lo.n)

                def squared_relu(i, p, per, used, b):
                    if act:
                        for m in range(2):
                            e.wait_ge(S.slot_used.sem, used(m))
                            e.wait_ge(S.dve_evicted.sem, val(base.d + 2 * p - 1 + m, i, 2 * per))
                            e.activation(tmp_g[:, m, 0:T], b[m][:, 0:T], ACT.Relu).then_inc(S.act_evicted.sem, 1)
                    if dve:
                        for m in range(2):
                            e.wait_ge(S.act_evicted.sem, val(base.a + 2 * p + m + 1, i, 2 * per))
                            e.wait_ge(S.hidden_hi.sem, val(base.h + 2 * p - 1 + m, i, 2 * per))
                            e.wait_ge(S.hidden_lo.sem, val(base.l + 2 * p - 1 + m, i, 2 * per))
                            e.tensor_tensor(tmp_y[:, m, 0:T], tmp_g[:, m, 0:T], tmp_g[:, m, 0:T], ALU.mult).then_inc(S.dve_evicted.sem, 1)
                    cut_hidden(i, p, per, T, (base.d, base.h))

                gemm(A["mlp_w1_2"][i], [(0, DK)], 16, 4, a_op(T), squared_relu, S.act_evicted)
                for s in (S.dve_evicted, S.hidden_hi, S.hidden_lo):
                    s.n += 32
                if pe:
                    e.wait_ge(S.hidden_lo.sem, S.hidden_lo.n)
                gemm(A["mlp_w2_2"][i], [(8 * g, 8) for g in range(4)], 4, 2,
                     lambda k: (h_hi_f[:, k * T:k * T + T], h_lo_f[:, k * T:k * T + T]), residual_to_z, S.dve_evicted)

            def wide_slot(src, kt, width, tiles):
                n = at.slot
                view = lambda t: t.rearrange("p k c -> p (k c)")[:, 0:kt * width].rearrange("p (k c) -> p k c", c=width)
                load(n, None, 0, lambda: src, view=view)
                if pe:
                    e.wait_ge(S.lo_ready.sem, 2 * n + 2)
                    hi, lo = view(w_hi[:, n % CUT, :, :]), view(w_lo[:, n % CUT, :, :])
                    for dst, ops in tiles:
                        for k in range(kt):
                            mm = three(dst, *ops(hi, lo, k), k == 0, k == kt - 1)
                    mm.then_inc(S.slot_used.sem, 2)
                ahead(n, None, 0)
                at.slot += 1

            def ple_load(i):
                if pool:
                    side_wait()
                    border()
                side_load(p_in[:, :, :], A["p_2"][i, 0].rearrange("(b p) d -> p b d", p=P))

            def ple(i):
                base_p = S.pe.n
                for k in range(2):
                    if pe:
                        side_wait()
                        for b in range(2):
                            mm = e.transpose(bank[4 + k][:, b * P:b * P + P], p_in[:, b, k * P:k * P + P], eye[:, :])
                        mm.then_inc(S.pe.sem, 1)
                    if act:
                        e.wait_ge(S.pe.sem, base_p + k + 1)
                        e.activation(p_hi[:, k, :], bank[4 + k][:, 0:T], ACT.Copy).then_inc(S.act.sem, 1)
                    S.act.n += 1
                    if dve:
                        e.wait_ge(S.act.sem, S.act.n)
                        e.tensor_tensor(p_lo[:, k, :], bank[4 + k][:, 0:T], p_hi[:, k, :].bitcast(F32), ALU.subtract).then_inc(S.dve.sem, 1)
                    S.dve.n += 1
                S.pe.n += 2
                if pe:
                    e.wait_ge(S.dve.sem, S.dve.n)
                    e.wait_ge(S.act_evicted.sem, S.act_evicted.n)
                    e.wait_ge(S.dve_evicted.sem, S.dve_evicted.n)
                wide_slot(matrix(A["ple_w_proj_2"][i]), 2, D,
                          [(bank[m // 2][:, (m % 2) * T:(m % 2) * T + T],
                            lambda hi, lo, k, m=m: (hi[:, k, m * P:m * P + P], lo[:, k, m * P:m * P + P], p_hi[:, k, :], p_lo[:, k, :]))
                           for m in range(8)])
                pj_f = pj[:].rearrange("p a t -> p (a t)")
                for j in range(4):
                    if act:
                        e.wait_ge(S.slot_used.sem, 2 * at.slot)
                        e.activation(pj_f[:, j * TT:j * TT + TT], bank[j][:, :], ACT.Copy).then_inc(S.act_evicted.sem, 1)
                S.act_evicted.n += 4
                base = Counts(a=S.act_evicted.n, d=S.dve_evicted.n, v=S.dve.n)

                def gated(i, p, per, used, b):
                    for m in range(2):
                        if act:
                            e.wait_ge(S.slot_used.sem, used(m))
                            e.wait_ge(S.dve_evicted.sem, base.d + 2 * p - 1 + m)
                            e.activation(tmp_g[:, m, 0:T], b[m][:, 0:T], ACT.Sigmoid).then_inc(S.act_evicted.sem, 1)
                        if dve:
                            t = 2 * p + m
                            e.wait_ge(S.act_evicted.sem, base.a + t + 1)
                            e.tensor_tensor(tmp_y[:, m, 0:T], tmp_g[:, m, 0:T], pj[:, t, :], ALU.mult).then_inc(S.dve_evicted.sem, 1)
                            e.wait_ge(S.dve_evicted.sem, base.d + t + 1)
                            e.tensor_tensor(xt[:, t, 0:T], xt[:, t, 0:T], tmp_y[:, m, 0:T], ALU.add).then_inc(S.dve.sem, 1)
                gemm(A["ple_w_gate_2"][i], [(0, DK)], 4, 4, a_op(T), gated, S.act_evicted)
                S.dve_evicted.n += 8
                S.dve.n += 8

            def out_product(w):
                e_border()
                gemm(w, [(0, DK)], 4, 4, a_op(T), residual_to_z, S.dve_evicted)

            def a_from(src, base_d):
                base_a = S.act.n
                for k in range(DK):
                    if act:
                        e.wait_ge(S.dve.sem, base_d + k + 1)
                        e.activation(a_hi[:, k, 0:T], src(k), ACT.Copy).then_inc(S.act.sem, 1)
                    if dve:
                        e.wait_ge(S.act.sem, base_a + k + 1)
                        e.tensor_tensor(a_lo[:, k, 0:T], src(k), a_hi[:, k, 0:T].bitcast(F32), ALU.subtract).then_inc(S.dve.sem, 1)
                S.act.n += DK
                S.dve.n += DK

            def one(name, op):
                mine, s = {"act": (act, S.act), "dve": (dve, S.dve)}[name]
                if mine:
                    op().then_inc(s.sem, 1)
                s.n += 1
                if act or dve:
                    e.wait_ge(s.sem, s.n)

            def gla(j):
                w = A["gla_w_in_2"][j]
                if pool:
                    side_wait()
                    border()
                side_load(w_glr[:, :, :], matrix(w)[:, :, 3 * D:3 * D + GLA_RANK])
                side_load(w_gate[:, :], A["gla_w_gate_up_2"][j])
                for dst, name in ((g_low, "gla_low"), (g_up, "gla_up"), (g_carry, "gla_carry")):
                    side_load(dst[:, :], C[name][:])
                flat = lambda t: t[:].rearrange("p a t -> p (a t)")
                hk = GLA_HEADS * GLA_DK
                gemm(w, [(0, DK)], 2, 2, a_op(T), copy_to(flat(qg), T, T, GLA_DK ** -0.5), S.act_evicted)
                gemm(w, [(0, DK)], 2, 2, a_op(T), copy_to(flat(kg), T, T), S.act_evicted, first_col=hk)
                if pe:
                    side_wait()
                    for k in range(DK):
                        mm = e.matmul(bank[6][0:GLA_RANK, 0:T], w_glr[:, k, :], xt[:, k, 0:T], start=k == 0, stop=k == DK - 1)
                    mm.then_inc(S.pe.sem, 1)
                S.pe.n += 1
                if dve:
                    e.wait_ge(S.pe.sem, S.pe.n)
                    e.tensor_copy(g_rank[:, :], bank[6][0:GLA_RANK, 0:T]).then_inc(S.dve.sem, 1)
                S.dve.n += 1
                for h in range(GLA_HEADS):
                    if pe:
                        e.wait_ge(S.dve.sem, S.dve.n)
                        mm = e.matmul(bank[4 + h % 2][:, (h // 2) * T:(h // 2) * T + T], w_gate[:, h * P:h * P + P], g_rank[:, :],
                                      start=True, stop=True)
                if pe:
                    mm.then_inc(S.pe.sem, 1)
                S.pe.n += 1
                if act:
                    e.wait_ge(S.pe.sem, S.pe.n)
                    for h in range(GLA_HEADS):
                        e.activation(e_l[:, h, :], bank[4 + h % 2][:, (h // 2) * T:(h // 2) * T + T], ACT.Identity,
                                     bias=vec("gla_b_gate_2", j * GLA_HEADS + h)).then_inc(S.act.sem, 1)
                S.act.n += GLA_HEADS
                if act or dve:
                    e.wait_ge(S.act.sem, S.act.n)
                one("act", lambda: e.activation(flat(e_pos), flat(e_l), ACT.Abs))
                one("act", lambda: e.activation(flat(e_pos), flat(e_pos), ACT.Exp, scale=-1.0))
                one("act", lambda: e.activation(flat(e_pos), flat(e_pos), ACT.Ln, bias=stat[:, 8:9]))
                one("dve", lambda: e.scalar_tensor_tensor(out=flat(e_l), in0=flat(e_l), scalar=0.0, in1=flat(e_pos), op0=ALU.min, op1=ALU.subtract))
                if dve:
                    side_wait()
                one("dve", lambda: e.tensor_tensor_scan(flat(L), g_carry[:, :], flat(e_l), 0.0, ALU.mult, ALU.add))
                ch = lambda t: t[:].rearrange("p h (c t) -> p (h c) t", t=CHUNK)
                wide = [P, GLA_HEADS * 4, CHUNK]
                one("dve", lambda: e.tensor_tensor(ch(e_neg), ch(L), ch(L)[:, :, CHUNK // 2 - 1:CHUNK // 2].to_broadcast(wide), ALU.subtract))
                one("dve", lambda: e.tensor_scalar(flat(e_neg), flat(e_neg), GLA_TAU * EXPONENT_MAX, -GLA_TAU * EXPONENT_MAX, ALU.min, ALU.max))
                one("dve", lambda: e.tensor_tensor(ch(e_end), ch(L)[:, :, CHUNK - 1:CHUNK].to_broadcast(wide), ch(L), ALU.subtract))
                one("act", lambda: e.activation(flat(e_pos), flat(e_neg), ACT.Exp, scale=1 / GLA_TAU))
                one("act", lambda: e.activation(flat(e_neg), flat(e_neg), ACT.Exp, scale=-1 / GLA_TAU))
                one("act", lambda: e.activation(flat(e_l), flat(L), ACT.Exp, scale=1 / GLA_TAU))
                one("act", lambda: e.activation(flat(e_end), flat(e_end), ACT.Exp, scale=1 / GLA_TAU))
                if dve:
                    e.wait_ge(S.act_evicted.sem, S.act_evicted.n)
                one("dve", lambda: e.tensor_tensor(flat(q_low), flat(qg), flat(e_pos), ALU.mult))
                one("dve", lambda: e.tensor_tensor(flat(k_low), flat(kg), flat(e_neg), ALU.mult))
                one("dve", lambda: e.tensor_tensor(flat(e_neg), flat(qg), flat(e_neg), ALU.mult))
                one("dve", lambda: e.tensor_tensor(flat(e_pos), flat(kg), flat(e_pos), ALU.mult))
                one("dve", lambda: e.tensor_copy(g_end[:, :].unsqueeze(2), ch(e_l)[:, :, CHUNK - 1:CHUNK]))
                one("dve", lambda: e.tensor_tensor(flat(e_l), flat(qg), flat(e_l), ALU.mult))
                one("dve", lambda: e.tensor_tensor(flat(e_end), flat(kg), flat(e_end), ALU.mult))
                token_major(w, 2 * hk, 4, T, lambda t, s: v_g[:, t, s * SC:(s + 1) * SC])
                gemm(w, [(0, DK)], 4, 4, a_op(T), copy_to(flat(r_gate), T, T, 1.0, ACT.Silu), S.act_evicted, first_col=2 * hk + D)
                e_border()
                if pe:
                    for c in range(4):
                        rows, tok = slice((c % 2) * CHUNK, (c % 2 + 1) * CHUNK), slice(c * CHUNK, (c + 1) * CHUNK)
                        for h in range(GLA_HEADS):
                            col = (c // 2 * GLA_HEADS + h) * CHUNK
                            e.matmul(bank[6][rows, col:col + CHUNK], k_low[:, h, tok], q_low[:, h, tok], start=True, stop=True)
                            mm = e.matmul(bank[7][rows, col:col + CHUNK], e_pos[:, h, tok], e_neg[:, h, tok], start=True, stop=True)
                    mm.then_inc(S.pe.sem, 1)
                    for b in range(2):
                        for h in range(GLA_HEADS):
                            mm = e.transpose(bank[4 + b][:, h * P:h * P + P], e_end[:, h, b * P:b * P + P], eye[:, :])
                    mm.then_inc(S.pe.sem, 1)
                S.pe.n += 2
                if act:
                    e.wait_ge(S.pe.sem, S.pe.n)
                    for b in range(2):
                        e.activation(k_tok[:, b, :, :].rearrange("p h d -> p (h d)"), bank[4 + b][:, :], ACT.Copy).then_inc(S.act.sem, 1)
                S.act.n += 2
                sc_f = sc_g[:, :, :, :].rearrange("p a h t -> p (a h) t")
                bk = lambda b: b[:, :].rearrange("p (a t) -> p a t", t=CHUNK)
                mask = lambda m: m[:, :].unsqueeze(1).to_broadcast([P, 8, CHUNK])
                tg = tmp_g[:, 0, :].rearrange("p (a t) -> p a t", t=CHUNK)
                if dve:
                    e.wait_ge(S.pe.sem, S.pe.n - 1)
                    e.tensor_tensor(sc_f, bk(bank[6]), mask(g_low), ALU.mult).then_inc(S.dve.sem, 1)
                    e.tensor_tensor(tg, bk(bank[7]), mask(g_up), ALU.mult).then_inc(S.dve.sem, 1)
                    e.wait_ge(S.dve.sem, S.dve.n + 2)
                    e.tensor_tensor(sc_f, sc_f, tg, ALU.add).then_inc(S.dve.sem, 1)
                S.dve.n += 3
                for c in range(4):
                    rows, tok = slice((c % 2) * CHUNK, (c % 2 + 1) * CHUNK), slice(c * CHUNK, (c + 1) * CHUNK)
                    if pe:
                        e.wait_ge(S.dve.sem, S.dve.n)
                        e.wait_ge(S.act.sem, S.act.n)
                        for h in range(GLA_HEADS):
                            for et in range(2):
                                dst = bank[h][:, et * T + c * CHUNK:et * T + (c + 1) * CHUNK]
                                e.matmul(dst, v_g[rows, c // 2, h * GLA_DV + et * P:h * GLA_DV + et * P + P], sc_g[rows, c // 2, h, :],
                                         start=True, stop=c == 0)
                                if c:
                                    e.matmul(dst, state[:, h, et * P:et * P + P], e_l[:, h, tok], start=False, stop=True)
                            if c < 3:
                                mm = e.matmul(bank[4 + h // 2][:, (h % 2) * T:(h % 2) * T + T], k_tok[rows, c // 2, h, :],
                                              v_g[rows, c // 2, h * GLA_DV:(h + 1) * GLA_DV], start=True, stop=True)
                        if c == 3:
                            mm = e.matmul(bank[6][0:1, 0:1], eye[:, 0:1], eye[:, 0:1], start=True, stop=True)
                        mm.then_inc(S.pe.sem, 1)
                    S.pe.n += 1
                    if c < 3:
                        for h in range(GLA_HEADS):
                            u = bank[4 + h // 2][:, (h % 2) * T:(h % 2) * T + T]
                            if dve:
                                e.wait_ge(S.pe.sem, S.pe.n)
                                if c == 0:
                                    e.tensor_copy(state[:, h, :], u).then_inc(S.dve.sem, 1)
                                else:
                                    e.scalar_tensor_tensor(out=state[:, h, :], in0=state[:, h, :], scalar=g_end[:, h * 4 + c:h * 4 + c + 1],
                                                           in1=u, op0=ALU.mult, op1=ALU.add).then_inc(S.dve.sem, 1)
                        S.dve.n += GLA_HEADS
                e_border()
                base_p, base_a = S.pe.n, S.act.n
                for h in range(GLA_HEADS):
                    if act:
                        if h >= 2:
                            e.wait_ge(S.pe.sem, base_p + h - 1)
                        e.activation(tmp_g[:, h % 2, :], bank[h][:, :], ACT.Square).then_inc(S.act.sem, 1)
                    if pe:
                        e.wait_ge(S.act.sem, base_a + h + 1)
                        for et in range(2):
                            mm = e.matmul(bank[6 + h // 2][:, (h % 2) * T:(h % 2) * T + T], ones[:, :], tmp_g[:, h % 2, et * T:et * T + T],
                                          start=et == 0, stop=et == 1)
                        mm.then_inc(S.pe.sem, 1)
                S.pe.n += GLA_HEADS
                S.act.n += GLA_HEADS
                if act:
                    e.wait_ge(S.pe.sem, S.pe.n)
                    for b in range(2):
                        e.activation(flat(e_neg)[:, b * TT:b * TT + TT], bank[6 + b][:, :], ACT.Sqrt, bias=stat[:, 0:1],
                                     scale=D / GLA_DV).then_inc(S.act.sem, 1)
                S.act.n += 2
                if dve:
                    e.wait_ge(S.act.sem, S.act.n)
                one("dve", lambda: e.reciprocal(flat(e_neg), flat(e_neg)))
                base_d = S.dve.n
                for t in range(8):
                    h, et = divmod(t, 2)
                    if dve:
                        e.scalar_tensor_tensor(out=qg_kg(t), in0=bank[h][:, et * T:et * T + T], scalar=vec("gla_norm_g_2", j * 2 + et),
                                               in1=e_neg[:, h, :], op0=ALU.mult, op1=ALU.mult).then_inc(S.dve.sem, 1)
                for t in range(8):
                    if dve:
                        e.wait_ge(S.dve.sem, base_d + t + 1)
                        e.tensor_tensor(qg_kg(t), qg_kg(t), r_gate[:, t, :], ALU.mult).then_inc(S.dve.sem, 1)
                S.dve.n += 16
                a_from(qg_kg, base_d + 8)
                out_product(A["gla_w_out_2"][j])

            def qg_kg(t):
                return qg[:, t, :] if t < 4 else kg[:, t - 4, :]

            TWO_PI = (6.28125, 0.0019350051879882812, 3.019916050561733e-07)

            def mla_angles():
                if dve or act:
                    side_wait()
                one("dve", lambda: e.tensor_scalar(ang[:, 0, :], pos_i[:, :], freq[:, 0:1], None, ALU.mult))
                for dst, quarter in ((cos_m, 0.25), (sin_m, 0.0)):
                    r = ang[:, 1, :]
                    one("dve", lambda: e.tensor_scalar(r, ang[:, 0, :], 1.0 / (2 * np.pi), quarter, ALU.mult, ALU.add))
                    one("dve", lambda: e.tensor_copy(pos_i[:, :], r))
                    one("dve", lambda: e.scalar_tensor_tensor(out=r, in0=pos_i[:, :], scalar=-TWO_PI[0], in1=ang[:, 0, :], op0=ALU.mult, op1=ALU.add))
                    one("dve", lambda: e.scalar_tensor_tensor(out=r, in0=pos_i[:, :], scalar=-TWO_PI[1], in1=r, op0=ALU.mult, op1=ALU.add))
                    one("dve", lambda: e.scalar_tensor_tensor(out=r, in0=pos_i[:, :], scalar=-TWO_PI[2], in1=r, op0=ALU.mult, op1=ALU.add))
                    one("dve", lambda: e.tensor_scalar(r, r, quarter * 2 * np.pi, None, ALU.add))
                    one("dve", lambda: e.tensor_scalar(ang[:, 2, :], r, float(np.pi), -2 * np.pi, ALU.is_gt, ALU.mult))
                    one("dve", lambda: e.tensor_tensor(r, r, ang[:, 2, :], ALU.add))
                    one("dve", lambda: e.tensor_scalar(r, r, 3.1415925, -3.1415925, ALU.min, ALU.max))
                    one("act", lambda: e.activation(dst[:, :], r, ACT.Sin))
                one("dve", lambda: e.tensor_scalar(sin_m[:, :], sin_m[:, :], freq[:, 1:2], None, ALU.mult))

            def mla(j):
                if pool:
                    side_wait()
                    border()
                pos = A["positions_2"]
                side_load(pos_i[:, :], bass.AP(tensor=pos.tensor, offset=pos.offset, ap=[[0, P], [1, T]]))
                side_load(freq[:, :], C["mla_freq"][:])
                side_load(mask_m[:, :, :], C["mla_mask"][:])
                w = A["mla_w_in_2"][j]
                flat = lambda t: t[:].rearrange("p a t -> p (a t)")
                mla_angles()
                gemm(w, [(0, DK)], 2, 2, a_op(T), copy_to(flat(c_in), T, T), S.act_evicted)
                n = at.slot
                load(n, None, 0, lambda: matrix(w)[:, :, 512 - 64:512 + 64], DK, P)
                if pe:
                    slot_products(n, None, 0, DK, 0, a_op(T), [bank[4][:, 0:T]])
                ahead(n, None, 0)
                at.slot += 1
                if act:
                    e.wait_ge(S.slot_used.sem, 2 * at.slot)
                    e.activation(kr[64:128, 0, :], bank[4][64:128, 0:T], ACT.Copy).then_inc(S.act.sem, 1)
                    e.activation(kr[64:96, 1, :], bank[4][96:128, 0:T], ACT.Copy).then_inc(S.act.sem, 1)
                    e.activation(kr[96:128, 1, :], bank[4][64:96, 0:T], ACT.Copy).then_inc(S.act.sem, 1)
                S.act.n += 3
                e_border()
                for c, name in enumerate(("mla_q_norm_2", "mla_kv_norm_2")):
                    if pe or act:
                        e.wait_ge(S.dve.sem, S.dve.n)
                    column_sums(lambda k: c_in[:, 2 * c + k, :], 2, T, True)
                    inverse_root(T, D / 256, 0)
                    if dve:
                        e.wait_ge(S.dve.sem, S.dve.n)
                    for t in range(2):
                        k = 2 * c + t
                        if dve:
                            e.scalar_tensor_tensor(out=c_in[:, k, :], in0=c_in[:, k, :], scalar=vec(name, t), in1=r_tmp[:, 0:T],
                                                   op0=ALU.mult, op1=ALU.mult).then_inc(S.dve.sem, 1)
                        S.dve.n += 1
                        if act:
                            e.wait_ge(S.dve.sem, S.dve.n)
                            e.activation(a_hi[:, k, 0:T], c_in[:, k, :], ACT.Copy).then_inc(S.act.sem, 1)
                        S.act.n += 1
                        if dve:
                            e.wait_ge(S.act.sem, S.act.n)
                            e.tensor_tensor(a_lo[:, k, 0:T], c_in[:, k, :], a_hi[:, k, 0:T].bitcast(F32), ALU.subtract).then_inc(S.dve.sem, 1)
                        S.dve.n += 1
                head = MLA_NOPE + MLA_ROPE
                wq = matrix(A["mla_w_uq_2"][j])
                for half in range(2):
                    e_border()
                    tiles = []
                    for h in range(4):
                        for o, c in ((0, 0), (64, T)):
                            tiles.append((bank[h][:, c:c + T], lambda hi, lo, k, o=o, h=h: (
                                hi[:, k, h * head + o:h * head + o + P], lo[:, k, h * head + o:h * head + o + P],
                                a_hi[:, k, 0:T], a_lo[:, k, 0:T])))
                    wide_slot(wq[:, :, half * 4 * head:(half + 1) * 4 * head], 2, 4 * head, tiles)
                    for h in range(4):
                        hh = half * 4 + h
                        if act:
                            e.wait_ge(S.slot_used.sem, 2 * at.slot)
                            e.activation(qn[:, hh, :], bank[h][:, 0:T], ACT.Copy, scale=MLA_SCALE).then_inc(S.act.sem, 1)
                            e.activation(qr[64:128, hh, :], bank[h][64:128, T:TT], ACT.Copy, scale=MLA_SCALE).then_inc(S.act.sem, 1)
                        if dve:
                            e.wait_ge(S.act.sem, S.act.n + 2)
                            e.tensor_scalar(qs[64:96, hh, :], bank[h][96:128, T:TT], MLA_SCALE, None, ALU.mult).then_inc(S.dve.sem, 1)
                            e.tensor_scalar(qs[96:128, hh, :], bank[h][64:96, T:TT], MLA_SCALE, None, ALU.mult).then_inc(S.dve.sem, 1)
                        S.act.n += 2
                        S.dve.n += 2
                wkv = matrix(A["mla_w_ukv_2"][j])
                for half in range(2):
                    e_border()
                    tiles = [(bank[h][:, 0:T], lambda hi, lo, k, h=h: (hi[:, k, h * 256:h * 256 + P], lo[:, k, h * 256:h * 256 + P],
                                                                      a_hi[:, 2 + k, 0:T], a_lo[:, 2 + k, 0:T])) for h in range(4)]
                    tiles += [(bank[4 + t][:, h * P:h * P + P], lambda hi, lo, k, t=t, h=h: (
                        a_hi[:, 2 + k, t * P:t * P + P], a_lo[:, 2 + k, t * P:t * P + P],
                        hi[:, k, h * 256 + P:h * 256 + 2 * P], lo[:, k, h * 256 + P:h * 256 + 2 * P])) for t in range(2) for h in range(4)]
                    wide_slot(wkv[:, :, half * D:(half + 1) * D], 2, D, tiles)
                    for h in range(4):
                        if act:
                            e.wait_ge(S.slot_used.sem, 2 * at.slot)
                            e.activation(kn[:, half * 4 + h, :], bank[h][:, 0:T], ACT.Copy).then_inc(S.act.sem, 1)
                    S.act.n += 4
                    for t in range(2):
                        if dve:
                            e.wait_ge(S.slot_used.sem, 2 * at.slot)
                            e.tensor_copy(v_m[:, t, half * 512:half * 512 + 512], bank[4 + t][:, :]).then_inc(S.dve.sem, 1)
                    S.dve.n += 2
                e_border()
                low = slice(64, 128)
                bc = lambda t: t[low, :].unsqueeze(1).to_broadcast([64, 8, T])
                one("dve", lambda: e.tensor_tensor(qr[low, :, :], qr[low, :, :], bc(cos_m), ALU.mult))
                one("dve", lambda: e.tensor_tensor(qs[low, :, :], qs[low, :, :], bc(sin_m), ALU.mult))
                one("dve", lambda: e.tensor_tensor(qr[low, :, :], qr[low, :, :], qs[low, :, :], ALU.add))
                one("dve", lambda: e.tensor_tensor(kr[low, 0, :], kr[low, 0, :], cos_m[low, :], ALU.mult))
                one("dve", lambda: e.tensor_tensor(kr[low, 1, :], kr[low, 1, :], sin_m[low, :], ALU.mult))
                one("dve", lambda: e.tensor_tensor(kr[low, 0, :], kr[low, 0, :], kr[low, 1, :], ALU.add))
                pe_wait_all()
                units = []
                for h in range(MLA_HEADS):
                    for q in range(2):
                        tok = slice(q * P, q * P + P)
                        units.append(dict(head=h, q=q, keys=T, biased=T, bias=mask_m[:, q, :],
                                          scores=[(qn[:, h, tok], kn[:, h, :]), (qr[low, h, tok], kr[low, 0, :])]))
                attention(units, lambda x, kb: (v_m[:, kb, x["head"] * MLA_V:(x["head"] + 1) * MLA_V], 0),
                          prob_m, probT_m, lambda x, buf: buf[:, x["head"], 0:T], 1)
                out_product(A["mla_w_out_2"][j])

            def conv(j):
                w = A["conv_w_in_2"][j]
                flat = lambda t: t[:].rearrange("p a t -> p (a t)")
                cu_f = flat(cu)
                if dve:
                    e.memset(cu[:, :, 0:2], 0.0).then_inc(S.dve.sem, 1)
                S.dve.n += 1
                gemm(w, [(0, DK)], 4, 4, a_op(T), copy_to(flat(cb), T, T), S.act_evicted)
                gemm(w, [(0, DK)], 4, 4, a_op(T), copy_to(flat(cc), T, T), S.act_evicted, first_col=D)
                ready = S.act_evicted.n

                def times_c(i, p, per, used, b):
                    if dve:
                        e.wait_ge(S.act_evicted.sem, ready)
                        for m in range(2):
                            e.wait_ge(S.slot_used.sem, used(m))
                            t = 2 * p + m
                            e.tensor_tensor(cu[:, t, 2:T + 2], cc[:, t, :], b[m][:, 0:T], ALU.mult).then_inc(S.dve_evicted.sem, 1)
                gemm(w, [(0, DK)], 4, 4, a_op(T), times_c, S.dve_evicted, first_col=2 * D)
                border()
                base = S.dve.n
                for tap in range(3):
                    for k in range(DK):
                        x, f = cu[:, k, tap:tap + T], vec("conv_w_2", tap * DK + k)
                        if dve:
                            if tap == 0:
                                e.tensor_scalar(cc[:, k, :], x, f, None, ALU.mult).then_inc(S.dve.sem, 1)
                            else:
                                e.wait_ge(S.dve.sem, base + (tap - 1) * DK + k + 1)
                                e.scalar_tensor_tensor(out=cc[:, k, :], in0=x, scalar=f, in1=cc[:, k, :], op0=ALU.mult,
                                                       op1=ALU.add).then_inc(S.dve.sem, 1)
                for k in range(DK):
                    if dve:
                        e.wait_ge(S.dve.sem, base + 2 * DK + k + 1)
                        e.tensor_tensor(cc[:, k, :], cc[:, k, :], cb[:, k, :], ALU.mult).then_inc(S.dve.sem, 1)
                S.dve.n += 4 * DK
                a_from(lambda k: cc[:, k, :], base + 3 * DK)
                out_product(A["conv_w_out_2"][j])

            def finish():
                border()
                base_p, base_d = S.pe.n, S.dve.n
                for j, (b, k4) in enumerate((b, k4) for b in range(2) for k4 in range(2)):
                    if pe:
                        for k in range(4):
                            mm = e.transpose(bank[j][:, k * P:k * P + P], xt[:, k4 * 4 + k, b * P:b * P + P], eye[:, :])
                        mm.then_inc(S.pe.sem, 1)
                    if dve:
                        e.wait_ge(S.pe.sem, base_p + j + 1)
                        e.tensor_copy(o_tok[:, b, k4 * 512:k4 * 512 + 512], bank[j][:, :]).then_inc(S.dve.sem, 1)
                S.pe.n += 4
                S.dve.n += 4
                if sp:
                    for b in range(2):
                        e.wait_ge(S.dve.sem, base_d + 2 * b + 2)
                        e.dma_start(out[0, b * P:(b + 1) * P, :], o_tok[:, b, :]).then_inc(S.stored.sem, 16)
                    e.wait_ge(S.stored.sem, 32)

            def network():
                yield begin()
                mods(1, 4)
                mods(2, 4)
                yield
                for layer in range(DEPTH):
                    last = layer == DEPTH - 1
                    yield ffn(layer, 0, TT, 2 * (not last), 2 * (not last), 2 * last)
                    yield mix(layer, last)
                    if not last:
                        yield ffn(layer, 1, TT, 2, 2, 2)
                    else:
                        yield ffn(layer, 1, T, 0, 0, 0)
                for i in range(DEPTH_2):
                    cut_x()
                    yield (gla, mla, conv)[i % 3](i // 3)
                    layer_norm(i, 0)
                    mlp(i)
                    ple_load(i)
                    yield layer_norm(i, 1)
                    yield ple(i)

            for j, _ in enumerate(network()):
                if j >= upto:
                    break
            finish()
            if not total:
                total.append(at.slot)

        walk("plan", None)
        with nc.Block() as block:
            @block.sync
            def _(eng):
                walk("sp", eng)

            @block.tensor
            def _(eng):
                walk("pe", eng)

            @block.scalar
            def _(eng):
                walk("act", eng)

            @block.vector
            def _(eng):
                walk("dve", eng)

            @block.gpsimd
            def _(eng):
                walk("pool", eng)


INPUTS = (
    "x", "c", "ctx", "c_ctx", "w_mod", "b_mod", "norm_g", "w_ffn_gate_up", "w_ffn_down", "w_in", "w_out", "na_rpb",
    "w_pool", "pool_scale", "p_2", "positions_2", "gla_w_in_2", "gla_w_gate_up_2", "gla_b_gate_2", "gla_norm_g_2",
    "gla_w_out_2", "mla_w_in_2", "mla_q_norm_2", "mla_kv_norm_2", "mla_w_uq_2", "mla_w_ukv_2", "mla_w_out_2",
    "conv_w_in_2", "conv_w_2", "conv_w_out_2", "ln_g_2", "ln_b_2", "mlp_w1_2", "mlp_w2_2", "ple_w_gate_2", "ple_w_proj_2",
)


def kernel(**inputs):
    import concourse.bacc as bacc
    from concourse.bass_utils import run_bass_kernel_spmd

    nc = bacc.Bacc("TRN2", target_bir_lowering=False, num_devices=1)
    arrays, A = {}, {}
    for name in INPUTS:
        a = np.ascontiguousarray(inputs[name])
        arrays[f"in_{name}"] = a
        A[name] = nc.dram_tensor(f"in_{name}", a.shape, mybir.dt.from_np(a.dtype), kind="ExternalInput").ap()
    out = nc.dram_tensor("out", (1, T, D), F32, kind="ExternalOutput").ap()
    build(nc, A, out)
    r = run_bass_kernel_spmd(nc, [arrays], core_ids=[0])
    return r.results[0]["out"]
```

```python
from contextlib import ExitStack

import numpy as np
import concourse.bass as bass
from concourse import mybir

F32 = mybir.dt.float32
F32R = mybir.dt.float32r
I32 = mybir.dt.int32
ALU = mybir.AluOpType
ACT = mybir.ActivationFunctionType
AX = mybir.AxisListType

P = 128
D = 1024
DK = D // P
T = 256
TT = 2 * T
DEPTH = 2
DEPTH_2 = 4
N_MOD = 9
D_FF = 2816
FT = D_FF // P
GRID_W = 64
ROWS = T // GRID_W
NA_HEADS, HEAD_DIM, NA_KH, NA_KW = 8, 64, 8, 16
NA_WIDTH = NA_HEADS * HEAD_DIM
POOL_WINDOWS = (2, 4, 8, 16)
ROPE_PAIRS = HEAD_DIM // 4
NEG = -1e30
ALPHA = (2 * DEPTH_2) ** 0.25
CHUNK = 64
GLA_HEADS, GLA_DK, GLA_DV, GLA_RANK, GLA_TAU = 4, 128, 256, 16, 16.0
MLA_HEADS, MLA_NOPE, MLA_ROPE, MLA_V = 8, 128, 64, 128
MLA_SCALE = (MLA_NOPE + MLA_ROPE) ** -0.5
RMS_EPS, LN_EPS = 1e-6, 1e-5
EXPONENT_MAX = 80.0

RAW, CUT = 4, 2
SC = 256
MOD_SLOTS = N_MOD * D // SC


class Signal:

    def __init__(self, sem):
        self.sem, self.n = sem, 0


class Counts:

    def __init__(self, a, d, h=0, l=0, v=0, slot=0):
        self.a, self.d, self.h, self.l, self.v, self.slot = a, d, h, l, v, slot


class Place:

    def __init__(self):
        self.slot, self.side, self.tables, self.mod_layer, self.mod_slot = 0, 0, 0, 0, 0
        self.a_ready = None
        self.x_ready = None
        self.lag = (0, 0)


SIGNALS = (
    "lo_ready",
    "hi_ready",
    "slot_used",
    "act_evicted",
    "dve_evicted",
    "hidden_hi",
    "hidden_lo",
    "mod_rows",
    "mod_turned",
    "mod_done",
    "act",
    "dve",
    "pe",
    "pool",
    "stored",
)


class Signals:

    def __init__(self, sems):
        self.lo_ready = Signal(sems["lo_ready"])
        self.hi_ready = Signal(sems["hi_ready"])
        self.slot_used = Signal(sems["slot_used"])
        self.act_evicted = Signal(sems["act_evicted"])
        self.dve_evicted = Signal(sems["dve_evicted"])
        self.hidden_hi = Signal(sems["hidden_hi"])
        self.hidden_lo = Signal(sems["hidden_lo"])
        self.mod_rows = Signal(sems["mod_rows"])
        self.mod_turned = Signal(sems["mod_turned"])
        self.mod_done = Signal(sems["mod_done"])
        self.act = Signal(sems["act"])
        self.dve = Signal(sems["dve"])
        self.pe = Signal(sems["pe"])
        self.pool = Signal(sems["pool"])
        self.stored = Signal(sems["stored"])


def constants():
    c = {}
    tok = np.arange(T)
    inv = (10000.0 ** (-np.arange(ROPE_PAIRS) / ROPE_PAIRS)).astype(np.float32)
    cos, sin = np.zeros((P, T), np.float32), np.zeros((P, T), np.float32)
    swap = np.zeros((P, P), np.float32)
    for p in range(P):
        d = p % HEAD_DIM
        pos = (tok // GRID_W) if d < 2 * ROPE_PAIRS else (tok % GRID_W)
        ang = pos.astype(np.float32) * inv[d % ROPE_PAIRS]
        cos[p] = np.cos(ang)
        first = (d % (2 * ROPE_PAIRS)) < ROPE_PAIRS
        sin[p] = -np.sin(ang) if first else np.sin(ang)
        swap[p + (ROPE_PAIRS if first else -ROPE_PAIRS), p] = 1.0
    c["na_cos"], c["na_sin"], c["na_swap"] = cos, sin, swap
    eye_row = np.eye(GRID_W, dtype=np.float32)[::-1]
    c["na_flip"] = np.kron(np.eye(P // GRID_W, dtype=np.float32), eye_row)
    col = np.arange(GRID_W)
    start = np.clip(col - NA_KW // 2, 0, GRID_W - NA_KW)
    valid = (col[None] >= start[:, None]) & (col[None] < start[:, None] + NA_KW)
    m = np.where(valid, 0.0, NEG).astype(np.float32)
    c["na_mask"] = np.concatenate([m, m], 0)

    def counts(length):
        t = np.arange(length)
        out = np.zeros((len(POOL_WINDOWS), length), np.float32)
        for g, w in enumerate(POOL_WINDOWS):
            out[g] = np.clip(t - w // 2 + w, 0, length) - np.clip(t - w // 2, 0, length)
        return np.broadcast_to((1.0 / out).astype(np.float32)[None], (P,) + out.shape).copy()

    c["pool_row"], c["pool_ctx"] = counts(GRID_W), counts(T)
    s, t = np.arange(CHUNK)[:, None], np.arange(CHUNK)[None]
    low = (t >= s).astype(np.float32)
    c["gla_low"], c["gla_up"] = np.concatenate([low, low]), np.concatenate([1 - low, 1 - low])
    first = np.ones((P, GLA_HEADS * T), np.float32)
    first[:, ::CHUNK] = 0.0
    c["gla_carry"] = first
    q, k = np.arange(T)[:, None] // CHUNK, np.arange(T)[None] // CHUNK
    m = np.where(k <= q, 0.0, NEG).astype(np.float32)
    c["mla_mask"] = m.reshape(2, P, T).transpose(1, 0, 2).copy()
    half = MLA_ROPE // 2
    f = (10000.0 ** (-np.arange(half) * (2.0 / MLA_ROPE))).astype(np.float32)
    sign = np.where((np.arange(P) // half) % 2 == 0, -1.0, 1.0)
    c["mla_freq"] = np.stack([np.tile(f, P // half), sign.astype(np.float32)], 1).astype(np.float32)
    c["eye"] = np.eye(P, dtype=np.float32)
    c["mod_sum"] = np.tile(np.eye(2, dtype=np.float32), (2, 1))
    return c


VECTORS = (
    ("b_mod", DEPTH * N_MOD * DK), ("norm_g", DEPTH * 6 * DK), ("pool_scale", DEPTH * 4),
    ("gla_b_gate_2", 2 * GLA_HEADS), ("gla_norm_g_2", 2 * 2), ("mla_q_norm_2", 2), ("mla_kv_norm_2", 2),
    ("ln_g_2", DEPTH_2 * 2 * DK), ("ln_b_2", DEPTH_2 * 2 * DK), ("conv_w_2", 3 * DK), ("c", DK), ("c_ctx", DK),
)
COL = {}
for _name, _rows in VECTORS:
    COL[_name] = sum(r for _, r in VECTORS[:[n for n, _ in VECTORS].index(_name)])
N_COLS = sum(r for _, r in VECTORS)


def build(nc, A, out, upto=99):
    with ExitStack() as ctx:
        def sb(name, shape, dt=F32, scope=ctx):
            return scope.enter_context(nc.sbuf_tensor(name, shape, dt))

        sems = {n: ctx.enter_context(nc.semaphore(n)) for n in SIGNALS}
        landed = [ctx.enter_context(nc.semaphore(f"landed{i}")) for i in range(RAW)]
        side_sem = ctx.enter_context(nc.semaphore("side_loaded"))
        table_sem = ctx.enter_context(nc.semaphore("tables_loaded"))
        C = {n: nc.inline_tensor(v, "table_" + n) for n, v in constants().items()}

        xt = sb("xt", [P, DK, TT])
        a_hi = sb("a_hi", [P, DK, TT], F32R)
        a_lo = sb("a_lo", [P, DK, TT], F32R)
        w_raw = sb("w_raw", [P, RAW, DK, SC])
        w_hi = sb("w_hi", [P, CUT, DK, SC], F32R)
        w_lo = sb("w_lo", [P, CUT, DK, SC], F32R)
        tmp_g = sb("tmp_g", [P, 2, TT])
        tmp_y = sb("tmp_y", [P, 2, TT])
        r_tmp = sb("r_tmp", [P, TT])
        rows_mod = r_tmp[0:4, :].rearrange("p (b c) -> p b c", c=SC)
        mod = sb("mod", [P, DEPTH * N_MOD * DK * 2])
        cols = sb("cols", [P, N_COLS])
        eye = sb("eye", [P, P])
        ones = sb("ones", [P, P])
        fac = sb("fac", [P, DK, 2])
        c_act = sb("c_act", [P, DK, 2])
        c_cut = sb("c_cut", [P, DK, 4], F32R)
        mod_sum = sb("mod_sum", [4, 2])
        stat = sb("stat", [P, 16])
        bank = [ctx.enter_context(nc.psum_tensor(f"bank{i}", [P, 512], F32)) for i in range(8)]

        Z = {}
        with ExitStack() as h:
            h_hi = sb("h_hi", [P, 16, TT], F32R, h)
            h_lo = sb("h_lo", [P, 16, TT], F32R, h)
            z = sb("z", [P, DK, TT], F32, h)
        with ExitStack() as h:
            sb("region_h_1", [P, 16 * 1024], F32, h)
            Z["pool_a"] = sb("pool_a", [P, 4 * 80 + 272], F32, h)
            Z["pool_b"] = sb("pool_b", [P, 4 * 80 + 272], F32, h)
            Z["pool_row"] = sb("pool_row_s", [P, 4, GRID_W], F32, h)
            Z["pool_ctx"] = sb("pool_ctx_s", [P, 4, T], F32, h)
            Z["w_pool"] = sb("w_pool_s", [P, 4, P], F32, h)
            Z["na_cos"] = sb("na_cos_s", [P, T], F32, h)
            Z["na_sin"] = sb("na_sin_s", [P, T], F32, h)
            Z["na_swap"] = sb("na_swap_s", [P, P], F32, h)
            Z["na_flip"] = sb("na_flip_s", [P, P], F32, h)
            Z["na_mask"] = sb("na_mask_s", [P, GRID_W], F32, h)
        with ExitStack() as h:
            qk = sb("qk", [P, 8, TT], F32, h)
            v_na = sb("v_na", [P, 4, NA_WIDTH], F32, h)
            ut = sb("ut", [P, 4, TT], F32, h)
            bias = sb("bias", [P, 2, NA_HEADS, T], F32, h)
            prob = sb("prob", [P, 3, TT], F32, h)
            probT = sb("probT", [P, 2, 4, T], F32, h)
        with ExitStack() as h:
            rows_in = sb("rows_in", [P, 4, P], F32, h)
            x_in = sb("x_in", [P, 2, 2, D], F32, h)
            zero_pad = sb("zero_pad", [P, 127], F32, h)
        with ExitStack() as h:
            qg = sb("qg", [P, GLA_HEADS, T], F32, h)
            kg = sb("kg", [P, GLA_HEADS, T], F32, h)
            v_g = sb("v_g", [P, 2, D], F32, h)
            L = sb("decay_sum", [P, GLA_HEADS, T], F32, h)
            e_l = sb("e_l", [P, GLA_HEADS, T], F32, h)
            e_end = sb("e_end", [P, GLA_HEADS, T], F32, h)
            e_pos = sb("e_pos", [P, GLA_HEADS, T], F32, h)
            e_neg = sb("e_neg", [P, GLA_HEADS, T], F32, h)
            q_low = sb("q_low", [P, GLA_HEADS, T], F32, h)
            k_low = sb("k_low", [P, GLA_HEADS, T], F32, h)
            k_tok = sb("k_tok", [P, 2, GLA_HEADS, P], F32, h)
            state = sb("state", [P, GLA_HEADS, GLA_DV], F32, h)
            sc_g = sb("sc_g", [P, 2, GLA_HEADS, CHUNK], F32, h)
            w_glr = sb("w_glr", [P, DK, GLA_RANK], F32, h)
            g_end = sb("g_end", [P, GLA_HEADS * 4], F32, h)
            g_rank = sb("g_rank", [GLA_RANK, T], F32, h)
            w_gate = sb("w_gate", [GLA_RANK, GLA_HEADS * P], F32, h)
        with ExitStack() as h:
            sb("region_h_2", [P, 16 * 1024], F32, h)
            r_gate = sb("r_gate", [P, DK, T], F32, h)
            g_low = sb("g_low", [P, CHUNK], F32, h)
            g_up = sb("g_up", [P, CHUNK], F32, h)
            g_carry = sb("g_carry", [P, GLA_HEADS * T], F32, h)
        with ExitStack() as h:
            qn = sb("qn", [P, 8, T], F32, h)
            qr = sb("qr", [P, 8, T], F32, h)
            qs = sb("qs", [P, 8, T], F32, h)
            kn = sb("kn", [P, 8, T], F32, h)
            v_m = sb("v_m", [P, 2, 8 * MLA_V], F32, h)
            kr = sb("kr", [P, 2, T], F32, h)
            c_in = sb("c_in", [P, 4, T], F32, h)
            cos_m = sb("cos_m", [P, T], F32, h)
            sin_m = sb("sin_m", [P, T], F32, h)
            mask_m = sb("mask_m", [P, 2, T], F32, h)
            prob_m = sb("prob_m", [P, 3, T], F32, h)
            probT_m = sb("probT_m", [P, 2, 2, T], F32, h)
            ang = sb("ang", [P, 3, T], F32, h)
            pos_i = sb("pos_i", [P, T], I32, h)
            freq = sb("freq", [P, 2], F32, h)
        with ExitStack() as h:
            cb = sb("cb", [P, DK, T], F32, h)
            cc = sb("cc", [P, DK, T], F32, h)
            cu = sb("cu", [P, DK, T + 2], F32, h)
        with ExitStack() as h:
            o_tok = sb("o_tok", [P, 2, D], F32, h)
        h_hi2 = h_hi[:].rearrange("p a (b t) -> p (a b) t", t=T)
        h_lo2 = h_lo[:].rearrange("p a (b t) -> p (a b) t", t=T)
        rpb_pad = nc.dram_tensor("rpb_pad", [DEPTH, NA_HEADS * (2 * NA_KH - 1), 127], F32)

        total = []

        def walk(who, e):
            S = Signals(sems)
            pe, act, dve, pool, sp = (who == x for x in ("pe", "act", "dve", "pool", "sp"))
            at = Place()
            h_hi_f = h_hi[:].rearrange("p a t -> p (a t)")
            h_lo_f = h_lo[:].rearrange("p a t -> p (a t)")
            z_f = z[:].rearrange("p a t -> p (a t)")
            xt_f = xt[:].rearrange("p a t -> p (a t)")

            def val(n, i, step):
                return n if i is None else i * step + n

            def part(flat, col, i, step, n):
                return flat[:, col:col + n] if i is None else flat[:, bass.ds(i * step + col, n)]

            def border(but=None):
                if pe or act or dve or pool:
                    for s in (S.act, S.dve, S.pe, S.pool, S.act_evicted, S.dve_evicted, S.hidden_hi, S.hidden_lo, S.mod_rows, S.mod_done):
                        if s.n and s is not but and not (pe and s is S.pe):
                            e.wait_ge(s.sem, s.n)
                    if at.slot and not pe:
                        e.wait_ge(S.slot_used.sem, 2 * at.slot)

            def rep(times, body, peel=False):
                if times == 1 or peel:
                    body(None, 0)
                    times, start = times - 1, 1
                else:
                    start = 0
                if times == 1:
                    body(None, start)
                elif times and (pe or act or dve or sp):
                    with e.Fori(0, times) as i:
                        body(i, start)

            def load(n, i, step, src, kt=DK, width=SC, view=None):
                if not sp:
                    return
                dst = w_raw[:, n % RAW, 0:kt, 0:width] if view is None else view(w_raw[:, n % RAW, :, :])
                s = src()
                if n >= RAW:
                    count = val(2 * (n - RAW + 1), i, 2 * step)
                    if i is not None:
                        count = e.snap(count)
                    e.wait_ge(S.lo_ready.sem, count)
                e.dma_start(dst, s).then_inc(landed[n % RAW], 16)

            def cut(m, i=None, step=0):
                if total and m >= total[0]:
                    return
                for half in range(2):
                    c = slice(half * P, half * P + P)
                    raw, hi, lo = w_raw[:, m % RAW, :, c], w_hi[:, m % CUT, :, c], w_lo[:, m % CUT, :, c]
                    if act:
                        if half == 0:
                            e.wait_ge(landed[m % RAW], val(16 * (m // RAW + 1), i, 16 * step // RAW))
                        if m >= CUT:
                            e.wait_ge(S.slot_used.sem, val(2 * (m - CUT) + half + 1, i, 2 * step))
                        e.activation(hi, raw, ACT.Copy).then_inc(S.hi_ready.sem, 1)
                    if dve:
                        e.wait_ge(S.hi_ready.sem, val(2 * m + half + 1, i, 2 * step))
                        e.tensor_tensor(lo, raw, hi.bitcast(F32), ALU.subtract).then_inc(S.lo_ready.sem, 1)

            def ahead(n, i, step):
                cut(n + CUT, i, step)

            def three(dst, hi, lo, rhs_hi, rhs_lo, start, stop):
                e.matmul(dst, hi, rhs_hi, start=start, stop=False)
                e.matmul(dst, hi, rhs_lo, start=False, stop=False)
                return e.matmul(dst, lo, rhs_hi, start=False, stop=stop)

            def slot_products(n, i, step, kt, k0, rhs, dsts, first=True, last=True, ready=None):
                if ready:
                    for k in range(kt):
                        if k0 + k in ready:
                            e.wait_ge(ready[k0 + k][0].sem, ready[k0 + k][1])
                        r_hi, r_lo = rhs(k0 + k)
                        for m, dst in enumerate(dsts):
                            if k == 0:
                                e.wait_ge(S.lo_ready.sem, 2 * n + m + 1)
                            mm = three(dst, w_hi[:, n % CUT, k, m * P:m * P + P], w_lo[:, n % CUT, k, m * P:m * P + P],
                                       r_hi, r_lo, first and k == 0, last and k == kt - 1)
                            if k == kt - 1:
                                mm.then_inc(S.slot_used.sem, 1)
                    return
                halves = 2 // len(dsts)
                for m, dst in enumerate(dsts):
                    e.wait_ge(S.lo_ready.sem, val(2 * n + m + halves, i, 2 * step))
                    for k in range(kt):
                        r_hi, r_lo = rhs(k0 + k)
                        mm = three(dst, w_hi[:, n % CUT, k, m * P:m * P + P], w_lo[:, n % CUT, k, m * P:m * P + P],
                                   r_hi, r_lo, first and k == 0, last and k == kt - 1)
                    mm.then_inc(S.slot_used.sem, halves)

            def matrix(w):
                return w.rearrange("(k p) m -> p k m", p=P)

            def mod_rows(n, i, step, j, per):
                layer, ms = at.mod_layer, at.mod_slot + j
                w = matrix(A["w_mod"][layer])
                b, count = bank[4 + j % 2][0:4, 0:SC], S.mod_rows.n + j
                load(n, i, step, lambda: w[:, :, ms * SC:ms * SC + SC] if i is None
                     else w[:, :, bass.ds(e.snap(i * (per * SC) + ms * SC), SC)])
                if pe:
                    if count > 1:
                        e.wait_ge(S.mod_rows.sem, val(count - 1, i, per))
                    e.wait_ge(S.lo_ready.sem, val(2 * n + 2, i, 2 * step))
                    for k in range(DK):
                        e.matmul(b, c_cut[:, k, :], w_hi[:, n % CUT, k, :], start=k == 0, stop=False)
                        mm = e.matmul(b, c_cut[:, k, :], w_lo[:, n % CUT, k, :], start=False, stop=k == DK - 1)
                    mm.then_inc(S.slot_used.sem, 2)
                ahead(n, i, step)
                if dve:
                    e.wait_ge(S.slot_used.sem, val(2 * n + 2, i, 2 * step))
                    if count > 1:
                        e.wait_ge(S.mod_turned.sem, val(count - 1, i, per))
                    e.tensor_copy(rows_mod[:, j % 2, :], b).then_inc(S.mod_rows.sem, 1)

            def mod_turn(i, j, per):
                t = (at.mod_layer * MOD_SLOTS + at.mod_slot + j) * 2
                b, count = bank[7], S.mod_rows.n + j
                if pe:
                    e.wait_ge(S.mod_rows.sem, val(count + 1, i, per))
                    if count > 0:
                        e.wait_ge(S.mod_done.sem, val(2 * count, i, 2 * per))
                    for m in range(2):
                        mm = e.matmul(b[:, 2 * m:2 * m + 2], rows_mod[:, j % 2, m * P:m * P + P], mod_sum[:, :], start=True, stop=True)
                    mm.then_inc(S.mod_turned.sem, 1)
                if act:
                    e.wait_ge(S.mod_turned.sem, val(count + 1, i, per))
                    for m in range(2):
                        e.activation(part(mod[:], 2 * (t + m), i, 4 * per, 2), b[:, 2 * m:2 * m + 2], ACT.Identity,
                                     bias=part(cols[:], COL["b_mod"] + t + m, i, 2 * per, 1)).then_inc(S.mod_done.sem, 1)

            def mods_done(count):
                S.mod_rows.n += count
                S.mod_turned.n += count
                S.mod_done.n += 2 * count
                at.mod_slot += count
                if at.mod_slot == MOD_SLOTS:
                    at.mod_layer, at.mod_slot = at.mod_layer + 1, 0

            def mods(passes, per):
                def body(i, first):
                    for j in range(per):
                        mod_rows(at.slot + j, i, per, j, per)
                        if j:
                            mod_turn(i, j - 1, per)
                    mod_turn(i, per - 1, per)
                rep(passes, body)
                at.slot += passes * per
                mods_done(passes * per)

            def mod_vec(layer, chunk):
                o = (layer * N_MOD + chunk) * DK * 2
                return mod[:, o:o + 2 * DK].rearrange("p (k s) -> p k s", s=2)

            def gemm(w, kgs, pairs, per, rhs, evict, by, mod_per=0, first_col=0, sums=None, between=None):
                lag = at.lag if at.a_ready or pairs == per else (0, 0)
                at.lag = (2, 0) if by is S.act_evicted else (0, 2)
                ready, at.a_ready = at.a_ready, None
                each = len(kgs) + mod_per
                step = per * each
                base = by.n
                if dve and mod_per:
                    e.wait_ge(S.dve.sem, S.dve.n)
                last = (S.act_evicted.n, S.dve_evicted.n)
                if pe:
                    e.wait_ge(S.act_evicted.sem, last[0] - lag[0])
                    e.wait_ge(S.dve_evicted.sem, last[1] - lag[1])
                wm = matrix(w) if sp else None

                def body(i, start):
                    for p in range(start * per, (start + 1) * per):
                        n = at.slot + p * each
                        b = bank[2 * (p % 2):2 * (p % 2) + 2]
                        for g, (k0, kt) in enumerate(kgs):
                            if mod_per:
                                mod_rows(n, i, step, p * mod_per + g, per * mod_per)
                                n += 1
                            col = first_col + p * SC
                            load(n, i, step, lambda: wm[:, k0:k0 + kt, col:col + SC] if i is None
                                 else wm[:, k0:k0 + kt, bass.ds(e.snap(i * (per * SC) + col), SC)], kt)
                            if pe:
                                if g == 0 and p == 1 and i is None and lag != (0, 0):
                                    e.wait_ge(S.act_evicted.sem, last[0])
                                    e.wait_ge(S.dve_evicted.sem, last[1])
                                if g == 0 and (p >= 2 or i is not None):
                                    e.wait_ge(by.sem, val(base + 2 * (p - 1), i, 2 * per))
                                slot_products(n, i, step, kt, k0, rhs, b_ap(b), g == 0, g == len(kgs) - 1,
                                              ready if p == 0 and i is None else None)
                            if sums and g == 0 and p:
                                sums(p - 1)
                            ahead(n, i, step)
                            if mod_per:
                                mod_turn(i, p * mod_per + g, per * mod_per)
                            n += 1
                        evict(i, p, per, lambda m: val(2 * n - 1 + m, i, 2 * step), b)
                        if between:
                            next(between, None)
                width = rhs(0)[0].shape[-1]

                def b_ap(b):
                    return [x[:, 0:width] for x in b]
                rep(pairs // per, body, peel=ready is not None)
                if sums:
                    sums(pairs - 1)
                at.slot += pairs * each
                by.n += 2 * pairs
                if mod_per:
                    mods_done(mod_per * pairs)

            def hidden_at(flat, p, m, i, per, n):
                return part(flat, (2 * p + m) * n, i, 2 * per * n, n)

            def cut_hidden(i, p, per, n, base):
                for m in range(2):
                    if act:
                        e.wait_ge(S.dve_evicted.sem, val(base[0] + 2 * p + m + 1, i, 2 * per))
                        e.activation(hidden_at(h_hi_f, p, m, i, per, n), tmp_y[:, m, 0:n], ACT.Copy).then_inc(S.hidden_hi.sem, 1)
                for m in range(2):
                    if dve:
                        e.wait_ge(S.hidden_hi.sem, val(base[1] + 2 * p + m + 1, i, 2 * per))
                        e.tensor_tensor(hidden_at(h_lo_f, p, m, i, per, n), tmp_y[:, m, 0:n],
                                        hidden_at(h_hi_f, p, m, i, per, n).bitcast(F32), ALU.subtract).then_inc(S.hidden_lo.sem, 1)

            def gate_up(w, t0, pairs, n, mod_per):
                per = 1 if mod_per else 2
                each = 2 + mod_per
                step = per * each
                ready, at.a_ready = at.a_ready, None
                wm = matrix(w) if sp else None
                if dve and mod_per:
                    e.wait_ge(S.dve.sem, S.dve.n)
                if pe:
                    e.wait_ge(S.act_evicted.sem, S.act_evicted.n)
                    e.wait_ge(S.dve_evicted.sem, S.dve_evicted.n)
                base = Counts(a=S.act_evicted.n, d=S.dve_evicted.n, h=S.hidden_hi.n, l=S.hidden_lo.n, slot=at.slot)

                def body(i, p0, per):
                    for p in range(p0, p0 + per):
                        first = ready if p == 0 and i is None else None
                        s = base.slot + p * each - 1
                        for half in range(2):
                            s += 1
                            if mod_per:
                                mod_rows(s, i, step, 2 * p + half, 2 * per)
                                s += 1
                            col = half * D_FF + t0 * P + p * SC
                            load(s, i, step, lambda: wm[:, :, col:col + SC] if i is None
                                 else wm[:, :, bass.ds(e.snap(i * (per * SC) + col), SC)])
                            if pe:
                                by, b0 = (S.dve_evicted, base.d) if half else (S.act_evicted, base.a)
                                e.wait_ge(by.sem, val(b0 + 2 * p, i, 2 * per))
                                slot_products(s, i, step, DK, 0, lambda k: (a_hi[:, k, 0:n], a_lo[:, k, 0:n]),
                                              [bank[2 * half][:, 0:n], bank[2 * half + 1][:, 0:n]],
                                              ready=None if half else first)
                            ahead(s, i, step)
                            if mod_per:
                                mod_turn(i, 2 * p + half, 2 * per)
                            if act and half == 0:
                                for m in range(2):
                                    e.wait_ge(S.slot_used.sem, val(2 * s + m + 1, i, 2 * step))
                                    e.wait_ge(S.dve_evicted.sem, val(base.d + 2 * p - 1 + m, i, 2 * per))
                                    e.activation(tmp_g[:, m, 0:n], bank[m][:, 0:n], ACT.Silu).then_inc(S.act_evicted.sem, 1)
                        if dve:
                            for m in range(2):
                                e.wait_ge(S.slot_used.sem, val(2 * s + m + 1, i, 2 * step))
                                e.wait_ge(S.act_evicted.sem, val(base.a + 2 * p + m + 1, i, 2 * per))
                                e.wait_ge(S.hidden_hi.sem, val(base.h + 2 * p - 1 + m, i, 2 * per))
                                e.wait_ge(S.hidden_lo.sem, val(base.l + 2 * p - 1 + m, i, 2 * per))
                                e.tensor_tensor(tmp_y[:, m, 0:n], tmp_g[:, m, 0:n], bank[2 + m][:, 0:n],
                                                ALU.mult).then_inc(S.dve_evicted.sem, 1)
                        cut_hidden(i, p, per, n, (base.d, base.h))
                rep(pairs // per, lambda i, start: body(i, start * per, per), peel=ready is not None)
                if pairs % per:
                    body(None, pairs - 1, 1)
                at.slot += pairs * each
                at.lag = (0, 2)
                for s in (S.act_evicted, S.dve_evicted, S.hidden_hi, S.hidden_lo):
                    s.n += 2 * pairs
                if mod_per:
                    mods_done(mod_per * pairs)

            def to_z(n, add=False):
                def evict(i, p, per, used, b):
                    for m in range(2):
                        dst = part(z_f, (2 * p + m) * TT, i, 2 * per * TT, n)
                        if act and not add:
                            e.wait_ge(S.slot_used.sem, used(m))
                            e.activation(dst, b[m][:, 0:n], ACT.Copy).then_inc(S.act_evicted.sem, 1)
                        if dve and add:
                            e.wait_ge(S.slot_used.sem, used(m))
                            e.tensor_tensor(dst, dst, b[m][:, 0:n], ALU.add).then_inc(S.dve_evicted.sem, 1)
                return evict

            def residual_to_z(i, p, per, used, b):
                if dve:
                    for m in range(2):
                        e.wait_ge(S.slot_used.sem, used(m))
                        c = (2 * p + m) * TT
                        e.scalar_tensor_tensor(out=part(z_f, c, i, 2 * per * TT, T), in0=part(xt_f, c, i, 2 * per * TT, T),
                                               scalar=ALPHA, in1=b[m][:, 0:T], op0=ALU.mult,
                                               op1=ALU.add).then_inc(S.dve_evicted.sem, 1)

            def copy_to(flat, width, n, scale=1.0, func=ACT.Copy):
                def evict(i, p, per, used, b):
                    if act:
                        for m in range(2):
                            e.wait_ge(S.slot_used.sem, used(m))
                            e.activation(part(flat, (2 * p + m) * width, i, 2 * per * width, n), b[m][:, 0:n],
                                         func, scale=scale).then_inc(S.act_evicted.sem, 1)
                return evict

            def a_op(n):
                return lambda k: (a_hi[:, k, 0:n], a_lo[:, k, 0:n])

            def token_major(w, first_col, slots, n, dst, between=None):
                tb = n // P
                wm = matrix(w) if sp else None
                lag, last = at.lag, (S.act_evicted.n, S.dve_evicted.n)
                at.lag = (0, 0) if tb > 2 else (0, 2)
                turn = 1 if tb > 2 else 0
                if pe and tb == 2:
                    e.wait_ge(S.act_evicted.sem, last[0] - lag[0])
                    e.wait_ge(S.dve_evicted.sem, last[1] - lag[1])
                for s in range(slots):
                    nn = at.slot
                    load(nn, None, 0, lambda: wm[:, :, first_col + s * SC:first_col + (s + 1) * SC])
                    if pe:
                        e.wait_ge(S.lo_ready.sem, 2 * nn + 2)
                        if s == 1:
                            e.wait_ge(S.act_evicted.sem, last[0])
                            e.wait_ge(S.dve_evicted.sem, last[1])
                        if s >= 2:
                            e.wait_ge(S.dve_evicted.sem, S.dve_evicted.n - tb)
                        for t in range(tb):
                            for k in range(DK):
                                x_hi, x_lo = (x[:, k, t * P:t * P + P] for x in (a_hi, a_lo))
                                v_hi, v_lo = (x[:, nn % CUT, k, :] for x in (w_hi, w_lo))
                                mm = three(bank[(s + turn) % 2 * tb + t][:, 0:SC], x_hi, x_lo, v_hi, v_lo, k == 0, k == DK - 1)
                        mm.then_inc(S.slot_used.sem, 2)
                    ahead(nn, None, 0)
                    if dve:
                        e.wait_ge(S.slot_used.sem, 2 * nn + 2)
                        for t in range(tb):
                            e.tensor_copy(dst(t, s), bank[(s + turn) % 2 * tb + t][:, 0:SC]).then_inc(S.dve_evicted.sem, 1)
                    S.dve_evicted.n += tb
                    at.slot += 1
                    if between:
                        next(between, None)

            def column_sum(src, k, tiles, n, square, ready=None, after_pairs=False):
                if square:
                    if act:
                        if k >= 2:
                            e.wait_ge(S.pe.sem, S.pe.n if after_pairs and k % 2 == 0 else S.pe.n - 1)
                        if ready:
                            e.wait_ge(ready[0].sem, ready[1])
                        e.activation(tmp_g[:, k % 2, 0:n], src(k), ACT.Square).then_inc(S.act.sem, 1)
                    S.act.n += 1
                if pe:
                    if square or not ready:
                        e.wait_ge(S.act.sem, S.act.n)
                    else:
                        e.wait_ge(ready[0].sem, ready[1])
                    e.matmul(bank[6][:, 0:n], ones[:, :], tmp_g[:, k % 2, 0:n] if square else src(k),
                             start=k == 0, stop=k == tiles - 1).then_inc(S.pe.sem, 1)
                S.pe.n += 1

            def pair_sum(src, k, n, square, ready):
                pair = tmp_g[:, :, 0:n]
                if square:
                    if act:
                        if k:
                            e.wait_ge(S.pe.sem, S.pe.n)
                        e.wait_ge(ready[0].sem, ready[1])
                        e.activation(pair, src(slice(k, k + 2)), ACT.Square).then_inc(S.act.sem, 1)
                    S.act.n += 1
                if dve:
                    if square:
                        e.wait_ge(S.act.sem, S.act.n)
                    else:
                        e.wait_ge(ready[0].sem, ready[1])
                        if k:
                            e.wait_ge(S.pe.sem, S.pe.n)
                    x, y = (pair[:, 0, :], pair[:, 1, :]) if square else (src(k), src(k + 1))
                    e.tensor_tensor(pair[:, 0, :], x, y, ALU.add).then_inc(S.dve.sem, 1)
                S.dve.n += 1
                if pe:
                    e.wait_ge(S.dve.sem, S.dve.n)
                    e.matmul(bank[6][:, 0:n], ones[:, :], pair[:, 0, :], start=k == 0, stop=False).then_inc(S.pe.sem, 1)
                S.pe.n += 1

            def column_sums(src, tiles, n, square):
                for k in range(tiles):
                    column_sum(src, k, tiles, n, square)

            def z_sums(n, by, square):
                base = by.n

                def sums(p):
                    if 2 * p + 2 < DK:
                        pair_sum(lambda k: z[:, k, 0:n], 2 * p, n, square, (by, base + 2 * p + 2))
                        return
                    for m in range(2):
                        column_sum(lambda k: z[:, k, 0:n], 2 * p + m, DK, n, square, (by, base + 2 * p + m + 1), True)
                return sums

            def inverse_root(n, scale, eps):
                if act:
                    e.wait_ge(S.pe.sem, S.pe.n)
                    e.activation(r_tmp[:, 0:n], bank[6][:, 0:n], ACT.Sqrt, bias=stat[:, eps:eps + 1], scale=scale).then_inc(S.act.sem, 1)
                S.act.n += 1
                if dve:
                    e.wait_ge(S.act.sem, S.act.n)
                    e.reciprocal(r_tmp[:, 0:n], r_tmp[:, 0:n]).then_inc(S.dve.sem, 1)
                S.dve.n += 1

            def vec(name, row, n=1):
                return cols[:, COL[name] + row:COL[name] + row + n]

            def streams(n):
                return [(s, slice(s * T, s * T + T)) for s in range(n // T)]

            def factor(layer, g_row, chunk, add, times):
                if dve:
                    g = vec("norm_g", (layer * 6 + g_row) * DK, DK).unsqueeze(2).to_broadcast([P, DK, 2])
                    e.scalar_tensor_tensor(out=fac[:, :, :], in0=mod_vec(layer, chunk), scalar=add if add else times,
                                           in1=g, op0=ALU.add if add else ALU.mult, op1=ALU.mult).then_inc(S.dve.sem, 1)
                S.dve.n += 1

            def pre_norm(layer, g_row, chunk, n):
                if at.x_ready:
                    for k in range(DK):
                        column_sum(lambda k: xt[:, k, 0:n], k, DK, n, True, (S.dve, at.x_ready[k]))
                else:
                    border()
                    column_sums(lambda k: xt[:, k, 0:n], DK, n, True)
                at.x_ready = None
                inverse_root(n, 1.0, 0)
                factor(layer, g_row, chunk + 1, 1.0, None)
                if dve:
                    e.wait_ge(S.dve.sem, S.dve.n)
                shift = mod_vec(layer, chunk)
                tiles = [(k, s, c) for k in range(DK) for s, c in streams(n)]
                lag = len(tiles) // DK + 1
                scaled, done = {}, {}
                for j in range(len(tiles) + lag):
                    if j < len(tiles):
                        k, s, c = tiles[j]
                        if dve:
                            e.scalar_tensor_tensor(out=z[:, k, c], in0=xt[:, k, c], scalar=fac[:, k, s:s + 1],
                                                   in1=r_tmp[:, c], op0=ALU.mult, op1=ALU.mult).then_inc(S.dve.sem, 1)
                        S.dve.n += 1
                        if act:
                            e.wait_ge(S.dve.sem, S.dve.n)
                            e.activation(a_hi[:, k, c], z[:, k, c], ACT.Identity, bias=shift[:, k, s:s + 1]).then_inc(S.act.sem, 1)
                        S.act.n += 1
                        scaled[j] = S.act.n
                    if j >= lag:
                        k, s, c = tiles[j - lag]
                        if dve:
                            e.wait_ge(S.act.sem, scaled[j - lag])
                            e.scalar_tensor_tensor(out=a_lo[:, k, c], in0=z[:, k, c], scalar=shift[:, k, s:s + 1],
                                                   in1=a_hi[:, k, c].bitcast(F32), op0=ALU.add,
                                                   op1=ALU.subtract).then_inc(S.dve.sem, 1)
                        S.dve.n += 1
                        done[k] = (S.dve, S.dve.n)
                at.a_ready = done

            def post_norm(layer, g_row, chunk, n, times):
                border()
                inverse_root(n, 1.0, 0)
                factor(layer, g_row, chunk, None, times)
                if dve:
                    e.wait_ge(S.dve.sem, S.dve.n)
                tiles = [(k, s, c) for k in range(DK) for s, c in streams(n)]
                base = S.dve.n
                for j in range(len(tiles) + 1):
                    if dve and j < len(tiles):
                        k, s, c = tiles[j]
                        e.scalar_tensor_tensor(out=z[:, k, c], in0=z[:, k, c], scalar=fac[:, k, s:s + 1],
                                               in1=r_tmp[:, c], op0=ALU.mult, op1=ALU.mult).then_inc(S.dve.sem, 1)
                    if dve and j:
                        k, s, c = tiles[j - 1]
                        e.wait_ge(S.dve.sem, base + max(2 * j - 2, 1))
                        e.tensor_tensor(xt[:, k, c], xt[:, k, c], z[:, k, c], ALU.add).then_inc(S.dve.sem, 1)
                S.dve.n += 2 * len(tiles)
                each = n // T
                at.x_ready = [min(base + 2 * ((k + 1) * each - 1) + 3, S.dve.n) for k in range(DK)]

            def hidden_ready(tiles):
                n = S.hidden_lo.n
                if pe:
                    e.wait_ge(S.hidden_lo.sem, n - 2)
                at.a_ready = {tiles - 2: (S.hidden_lo, n - 1), tiles - 1: (S.hidden_lo, n)}

            def ffn(layer, f, n, mod_a, mod_down, mod_b, mod_down_b=0):
                pre_norm(layer, 4 * f, 6 * f, n)
                parts = [(0, 16), (16, FT - 16)] if n == TT else [(0, FT)]
                w_gu, w_d = A["w_ffn_gate_up"][layer, f], A["w_ffn_down"][layer, f]
                for j, (t0, tiles) in enumerate(parts):
                    gate_up(w_gu, t0, tiles // 2, n, (mod_a, mod_b)[j])
                    hidden_ready(tiles)
                    if dve:
                        e.wait_ge(S.act_evicted.sem, S.act_evicted.n)
                    kgs = [(k, min(DK, tiles - k)) for k in range(0, tiles, DK)]
                    rhs = (lambda k: (h_hi_f[:, k * n:k * n + n], h_lo_f[:, k * n:k * n + n]))
                    by = S.dve_evicted if j else S.act_evicted
                    gemm(w_d[t0 * P:(t0 + tiles) * P, :], kgs, 4, 4, rhs, to_z(n, add=j > 0), by, mod_per=mod_down_b if j else mod_down,
                         sums=z_sums(n, by, True) if j == len(parts) - 1 else None)
                post_norm(layer, 4 * f + 1, 6 * f + 2, n, 0.5)

            def attention(units, v_of, p_buf, pt_buf, finish, vm):
                U = len(units)
                first = {"act": S.act.n, "dve": S.dve.n, "pe": S.pe.n}
                order = {"act": [], "dve": [], "pe": []}
                order["pe"].append(("scores", 0))
                for t in range(U + 2):
                    if t + 1 < U:
                        order["pe"].append(("scores", t + 1))
                    if t < U:
                        order["act"] += [("copy", t)] * (units[t]["biased"] < units[t]["keys"])
                        order["dve"] += [("bias", t)] * (units[t]["biased"] > 0) + [("max", t)]
                    if 0 <= t - 1 < U:
                        order["act"].append(("exp", t - 1))
                        order["dve"] += [("recip", t - 1), ("norm", t - 1)]
                        order["pe"].append(("turn", t - 1))
                    if 0 <= t - 2 < U:
                        order["act"].append(("turned", t - 2))
                        if (t - 2) % 2:
                            order["pe"].append(("pv", t - 2))
                            if ((t - 2) // 2) % vm == vm - 1:
                                order["act"].append(("o_hi", t - 2))
                                order["dve"].append(("o_lo", t - 2))
                count = {step: (name, first[name] + j + 1) for name in order for j, step in enumerate(order[name])}
                signal = {"act": S.act, "dve": S.dve, "pe": S.pe}

                def after(kind, u):
                    if (kind, u) in count:
                        name, n = count[(kind, u)]
                        e.wait_ge(signal[name].sem, n)

                for kind, u in order.get(who, []):
                    x = units[u]
                    n, b = x["keys"], x["biased"]
                    pr, head = p_buf[:, u % 3, 0:n], u // 2
                    s_bank, t_bank, o_bank = bank[u % 2], bank[2 + u % 2], bank[4 + head // vm % 2]
                    top, den, inv = (stat[:, o + u % 2:o + u % 2 + 1] for o in (2, 4, 6))
                    if kind == "scores":
                        after("bias", u - 2)
                        after("copy", u - 2)
                        after("max", u - 2)
                        for j, (lhs, rhs) in enumerate(x["scores"]):
                            mm = e.matmul(s_bank[:, 0:n], lhs, rhs, start=j == 0, stop=j == len(x["scores"]) - 1)
                        mm.then_inc(S.pe.sem, 1)
                    elif kind == "copy":
                        after("scores", u)
                        after("turn", u - 3)
                        e.activation(pr[:, b:n], s_bank[:, b:n], ACT.Copy).then_inc(S.act.sem, 1)
                    elif kind == "bias":
                        after("scores", u)
                        after("copy", u)
                        after("turn", u - 3)
                        e.tensor_tensor(pr[:, 0:b], s_bank[:, 0:b], x["bias"], ALU.add).then_inc(S.dve.sem, 1)
                    elif kind == "max":
                        after("bias", u)
                        after("copy", u)
                        after("exp", u - 2)
                        e.tensor_reduce(top, pr, AX.X, ALU.max, negate=True).then_inc(S.dve.sem, 1)
                    elif kind == "exp":
                        after("max", u)
                        after("recip", u - 2)
                        e.activation(pr, pr, ACT.Exp, bias=top, accum_out=den).then_inc(S.act.sem, 1)
                    elif kind == "recip":
                        after("exp", u)
                        e.reciprocal(inv, den).then_inc(S.dve.sem, 1)
                    elif kind == "norm":
                        after("recip", u)
                        e.tensor_scalar(pr, pr, inv, None, ALU.mult).then_inc(S.dve.sem, 1)
                    elif kind == "turn":
                        after("norm", u)
                        after("turned", u - 2)
                        for kb in range(n // P):
                            mm = e.transpose(t_bank[:, kb * P:kb * P + P], pr[:, kb * P:kb * P + P], eye[:, :])
                        mm.then_inc(S.pe.sem, 1)
                    elif kind == "turned":
                        after("turn", u)
                        after("pv", (u | 1) - 4)
                        e.activation(pt_buf[:, head % 2, 0:n // P, (u % 2) * P:(u % 2) * P + P],
                                     t_bank[:, 0:n].rearrange("p (k q) -> p k q", q=P), ACT.Copy).then_inc(S.act.sem, 1)
                    elif kind == "pv":
                        after("turned", u)
                        if head % vm == 0:
                            after("o_lo", 2 * (head - vm - 1) + 1)
                        for kb in range(n // P):
                            lhs, row = v_of(x, kb)
                            mm = e.matmul(o_bank[row:row + P // vm, 0:T], lhs, pt_buf[:, head % 2, kb, :],
                                          start=kb == 0, stop=kb == n // P - 1)
                        mm.then_inc(S.pe.sem, 1)
                    elif kind == "o_hi":
                        after("pv", u)
                        e.activation(finish(x, a_hi), o_bank[:, 0:T], ACT.Copy).then_inc(S.act.sem, 1)
                    elif kind == "o_lo":
                        after("o_hi", u)
                        e.tensor_tensor(finish(x, a_lo), o_bank[:, 0:T], finish(x, a_hi).bitcast(F32), ALU.subtract).then_inc(S.dve.sem, 1)
                S.act.n += len(order["act"])
                S.dve.n += len(order["dve"])
                S.pe.n += len(order["pe"])

            def side_load(dst, src):
                if pool:
                    e.dma_start(dst, src).then_inc(side_sem, 16)
                at.side += 16

            def side_wait():
                e.wait_ge(side_sem, at.side)

            def begin():
                if pool:
                    e.memset(ones[:, :], 1.0 / D).then_inc(S.pool.sem, 1)
                    e.memset(stat[:, 0:1], RMS_EPS).then_inc(S.pool.sem, 1)
                    e.memset(stat[:, 1:2], LN_EPS).then_inc(S.pool.sem, 1)
                    e.memset(stat[:, 8:9], 1.0).then_inc(S.pool.sem, 1)
                    e.memset(zero_pad[:, :], 0.0).then_inc(S.pool.sem, 1)
                S.pool.n += 5
                def table_load(dst, src):
                    if act:
                        e.dma_start(dst, src).then_inc(table_sem, 16)
                    at.tables += 16
                table_load(eye[:, :], C["eye"][:])
                table_load(mod_sum[:, :], C["mod_sum"][:])
                for name, rows in VECTORS:
                    flat = A[name]
                    if len(flat.shape) == 2:
                        flat = flat.rearrange("a b -> (a b)")
                    elif len(flat.shape) == 3:
                        flat = flat.rearrange("a b c -> (a b c)")
                    flat = flat.rearrange("(r c) -> r c", c=P)
                    r = 0
                    while r < rows:
                        g, o = divmod(COL[name] + r, P)
                        n = min(rows - r, P - o)
                        table_load(rows_in[o:o + n, g, :], flat[r:r + n, :])
                        r += n
                for s, name in enumerate(("x", "ctx")):
                    side_load(x_in[:, s, :, :], A[name][0].rearrange("(b p) d -> p b d", p=P))
                cut(0)
                cut(1)
                groups = -(-N_COLS // P)
                for g in range(groups):
                    n = min(P, N_COLS - g * P)
                    if pe:
                        if g == 0:
                            e.wait_ge(table_sem, at.tables)
                        e.transpose(bank[g][:, 0:n], rows_in[0:n, g, :], eye[0:n, 0:n]).then_inc(S.pe.sem, 1)
                    S.pe.n += 1
                    if dve:
                        e.wait_ge(S.pe.sem, S.pe.n)
                        e.tensor_copy(cols[:, g * P:g * P + n], bank[g][:, 0:n]).then_inc(S.dve.sem, 1)
                    S.dve.n += 1
                if act:
                    e.wait_ge(S.dve.sem, S.dve.n)
                    e.activation(c_act[:, :, 0], vec("c", 0, DK), ACT.Silu).then_inc(S.act.sem, 1)
                    e.activation(c_act[:, :, 1], vec("c_ctx", 0, DK), ACT.Silu).then_inc(S.act.sem, 1)
                    e.wait_ge(S.act.sem, S.act.n + 2)
                S.act.n += 2
                for s in range(2):
                    if act:
                        e.activation(c_cut[:, :, s], c_act[:, :, s], ACT.Copy).then_inc(S.hidden_hi.sem, 1)
                    S.hidden_hi.n += 1
                    if dve:
                        e.wait_ge(S.hidden_hi.sem, S.hidden_hi.n)
                        e.tensor_tensor(c_cut[:, :, 2 + s], c_act[:, :, s], c_cut[:, :, s].bitcast(F32), ALU.subtract).then_inc(S.hidden_lo.sem, 1)
                    S.hidden_lo.n += 1
                if pe:
                    e.wait_ge(S.hidden_lo.sem, S.hidden_lo.n)

            def turn_x():
                if pe:
                    side_wait()
                for j, (k, s) in enumerate((k, s) for k in range(DK) for s in range(2)):
                    by = S.act_evicted if s else S.dve_evicted
                    if pe:
                        if k >= 2:
                            e.wait_ge(by.sem, by.n - 1)
                        for b in range(2):
                            mm = e.transpose(bank[j % 4][:, b * P:b * P + P], x_in[:, s, b, k * P:k * P + P], eye[:, :])
                        mm.then_inc(S.pe.sem, 1)
                    S.pe.n += 1
                    if dve and s == 0:
                        e.wait_ge(S.pe.sem, S.pe.n)
                        e.tensor_copy(xt[:, k, 0:T], bank[j % 4][:, 0:T]).then_inc(by.sem, 1)
                    if act and s == 1:
                        e.wait_ge(S.pe.sem, S.pe.n)
                        e.activation(xt[:, k, T:TT], bank[j % 4][:, 0:T], ACT.Copy).then_inc(by.sem, 1)
                    by.n += 1
                n_rows = NA_HEADS * (2 * NA_KH - 1)
                if pool:
                    side_wait()
                    e.wait_ge(S.pool.sem, S.pool.n)
                for l in range(DEPTH):
                    side_load(rpb_pad[l, :, :], zero_pad[0:n_rows, :])
                if pool:
                    side_wait()
                for l in range(DEPTH):
                    side_load(rpb_pad[l, :, GRID_W - NA_KW:GRID_W + NA_KW - 1], A["na_rpb"][l].rearrange("h a b -> (h a) b"))
                if pool or act or dve:
                    side_wait()

            def rope_na():
                base_p, base_d = S.pe.n, S.dve.n
                for j in range(8):
                    b = bank[6 + j % 2][:, 0:T]
                    if pe:
                        if j >= 2:
                            e.wait_ge(S.dve.sem, base_d + 3 * (j - 1))
                        e.matmul(b, Z["na_swap"][:, :], qk[:, j, 0:T], start=True, stop=True).then_inc(S.pe.sem, 1)
                    if dve:
                        e.tensor_tensor(tmp_g[:, j % 2, 0:T], qk[:, j, 0:T], Z["na_cos"][:, :], ALU.mult).then_inc(S.dve.sem, 1)
                        e.wait_ge(S.pe.sem, base_p + j + 1)
                        e.tensor_tensor(tmp_y[:, j % 2, 0:T], b, Z["na_sin"][:, :], ALU.mult).then_inc(S.dve.sem, 1)
                        e.wait_ge(S.dve.sem, base_d + 3 * j + 2)
                        e.tensor_tensor(qk[:, j, 0:T], tmp_g[:, j % 2, 0:T], tmp_y[:, j % 2, 0:T], ALU.add).then_inc(S.dve.sem, 1)
                S.pe.n += 8
                S.dve.n += 24

            def pool_windows(n):
                if pool:
                    side_wait()
                    e.wait_ge(S.act_evicted.sem, S.act_evicted.n)
                def step(op):
                    if pool:
                        op().then_inc(S.pool.sem, 1)
                        e.wait_ge(S.pool.sem, S.pool.n + 1)
                    S.pool.n += 1
                views = [(lambda t: t[:, 0:320].rearrange("p (r c) -> p r c", r=ROWS), GRID_W, Z["pool_row"], slice(0, T), ROWS)]
                if n == TT:
                    views.append((lambda t: t[:, 320:592].rearrange("p (r c) -> p r c", r=1), T, Z["pool_ctx"], slice(T, TT), 1))
                for g, w in enumerate(POOL_WINDOWS):
                    for of, length, inv, tok, rows in views:
                        a, b = of(Z["pool_a"]), of(Z["pool_b"])
                        u = ut[:, g, tok].rearrange("p (r c) -> p r c", r=rows)
                        step(lambda: e.memset(a, 0.0))
                        step(lambda: e.tensor_copy(a[:, :, 8:8 + length], u))
                        have, width = 1, length + 16
                        while have < w:
                            width -= have
                            step(lambda: e.tensor_tensor(b[:, :, 0:width], a[:, :, 0:width], a[:, :, have:have + width], ALU.add))
                            a, b, have = b, a, 2 * have
                        o = 8 - w // 2
                        step(lambda: e.tensor_tensor(b[:, :, 0:length], a[:, :, o:o + length],
                                                     inv[:, g, :].unsqueeze(1).to_broadcast([P, rows, length]), ALU.mult))
                        step(lambda: e.tensor_tensor(u, b[:, :, 0:length], u, ALU.subtract))

            def pool_products(layer, n):
                base_p, base_a, base_d = S.pe.n, S.act.n, S.dve.n
                for g in range(4):
                    b = bank[6 + g % 2][:, 0:n]
                    scale = vec("pool_scale", layer * 4 + g)
                    if pe:
                        if g == 0:
                            e.wait_ge(S.pool.sem, S.pool.n)
                            e.wait_ge(S.dve.sem, S.dve.n)
                        else:
                            e.wait_ge(S.dve.sem, base_d + g - 1) if g >= 2 else None
                        e.matmul(b, Z["w_pool"][:, g, :], ut[:, g, 0:n], start=True, stop=True).then_inc(S.pe.sem, 1)
                    if act:
                        e.wait_ge(S.pe.sem, base_p + g + 1)
                        e.activation(a_hi[:, 4 + g, 0:n], b, ACT.Copy, scale=scale).then_inc(S.act.sem, 1)
                    if dve:
                        e.wait_ge(S.act.sem, base_a + g + 1)
                        e.scalar_tensor_tensor(out=a_lo[:, 4 + g, 0:n], in0=b, scalar=scale, in1=a_hi[:, 4 + g, 0:n].bitcast(F32),
                                               op0=ALU.mult, op1=ALU.subtract).then_inc(S.dve.sem, 1)
                S.pe.n += 4
                S.act.n += 4
                S.dve.n += 4

            def mix(layer, last):
                n = T if last else TT
                pre_norm(layer, 2, 3, TT)
                if pool:
                    side_wait()
                    border()
                for name in ("na_cos", "na_sin", "na_swap", "na_flip", "na_mask", "pool_row", "pool_ctx"):
                    side_load(Z[name][:], C[name][:])
                side_load(Z["w_pool"][:, :, :], A["w_pool"][layer].rearrange("g c d -> c g d"))
                rpb_rows = NA_HEADS * (2 * NA_KH - 1)
                for qt in range(2):
                    for half in range(2):
                        qrow = 2 * qt + half
                        for kr in range(ROWS):
                            src = bass.AP(tensor=rpb_pad, offset=(layer * rpb_rows + NA_KH - 1 + kr - qrow) * 127,
                                          ap=[[1, GRID_W], [(2 * NA_KH - 1) * 127, NA_HEADS], [1, GRID_W]])
                            side_load(bias[half * GRID_W:(half + 1) * GRID_W, qt, :, kr * GRID_W:(kr + 1) * GRID_W], src)
                w = A["w_in"][layer]
                qk_f = qk[:].rearrange("p a t -> p (a t)")
                gemm(w, [(0, DK)], 2, 2, a_op(n), copy_to(qk_f, TT, n, HEAD_DIM ** -0.5), S.act_evicted)
                gemm(w, [(0, DK)], 2, 2, a_op(TT), copy_to(qk_f[:, 4 * TT:], TT, TT), S.act_evicted, first_col=NA_WIDTH)
                gemm(w, [(0, DK)], 2, 2, a_op(n), copy_to(ut[:].rearrange("p a t -> p (a t)"), TT, n), S.act_evicted,
                     first_col=3 * NA_WIDTH)
                pool_windows(n)
                token_major(w, 2 * NA_WIDTH, 2, TT, lambda t, s: v_na[:, t, s * SC:(s + 1) * SC])
                flat = bias[:, :, :, :].rearrange("p q h c -> p (q h c)")
                base_p, base_d = S.pe.n, S.dve.n
                for j in range(8):
                    c, b = slice(j * 512, j * 512 + 512), bank[4 + j % 2]
                    if pe:
                        if j == 0:
                            side_wait()
                            e.wait_ge(S.dve_evicted.sem, S.dve_evicted.n)
                        if j >= 2:
                            e.wait_ge(S.dve.sem, base_d + j - 1)
                        e.matmul(b[:, :], Z["na_flip"][:, :], flat[:, c], start=True, stop=True).then_inc(S.pe.sem, 1)
                    if dve:
                        if j == 0:
                            side_wait()
                        e.wait_ge(S.pe.sem, base_p + j + 1)
                        e.tensor_tensor(flat[:, c].rearrange("p (r c) -> p r c", c=GRID_W), b[:, :].rearrange("p (r c) -> p r c", c=GRID_W),
                                        Z["na_mask"][:, :].unsqueeze(1).to_broadcast([P, 512 // GRID_W, GRID_W]), ALU.add).then_inc(S.dve.sem, 1)
                S.pe.n += 8
                S.dve.n += 8
                if not pool:
                    border(but=S.pool)
                rope_na()
                pe_wait_all()
                units = []
                for h in range(NA_HEADS):
                    rows = slice((h % 2) * HEAD_DIM, (h % 2 + 1) * HEAD_DIM)
                    for q in range(2):
                        units.append(dict(head=h, q=q, keys=TT, biased=T, bias=bias[:, q, h, :],
                                          scores=[(qk[rows, h // 2, q * P:q * P + P], qk[rows, 4 + h // 2, :])]))
                attention(units, lambda x, kb: (v_na[:, kb, x["head"] * HEAD_DIM:(x["head"] + 1) * HEAD_DIM], (x["head"] % 2) * HEAD_DIM),
                          prob, probT, lambda x, buf: buf[:, x["head"] // 2, 0:T], 2)
                if not last:
                    units = []
                    for h in range(NA_HEADS):
                        rows = slice((h % 2) * HEAD_DIM, (h % 2 + 1) * HEAD_DIM)
                        for q in range(2):
                            units.append(dict(head=h, q=q, keys=T, biased=0, bias=None,
                                              scores=[(qk[rows, h // 2, T + q * P:T + q * P + P], qk[rows, 4 + h // 2, T:TT])]))
                    if not pool:
                        border(but=S.pool)
                    attention(units, lambda x, kb: (v_na[:, 2 + kb, x["head"] * HEAD_DIM:(x["head"] + 1) * HEAD_DIM], (x["head"] % 2) * HEAD_DIM),
                              prob, probT, lambda x, buf: buf[:, x["head"] // 2, T:TT], 2)
                pool_products(layer, n)
                e_border()
                gemm(A["w_out"][layer], [(0, DK)], 4, 4, a_op(n), to_z(n), S.act_evicted, sums=z_sums(n, S.act_evicted, True))
                post_norm(layer, 3, 5, n, 1.0)

            def e_border():
                if not pool:
                    border()

            def pe_wait_all():
                if pe:
                    e.wait_ge(S.dve.sem, S.dve.n)

            def cut_x():
                done = {}
                for k in range(DK):
                    if act:
                        if k == 0:
                            e.wait_ge(S.slot_used.sem, 2 * at.slot)
                        e.wait_ge(S.dve.sem, at.x_ready[k])
                        e.activation(a_hi[:, k, 0:T], xt[:, k, 0:T], ACT.Copy).then_inc(S.act.sem, 1)
                    S.act.n += 1
                    if dve:
                        e.wait_ge(S.act.sem, S.act.n)
                        e.tensor_tensor(a_lo[:, k, 0:T], xt[:, k, 0:T], a_hi[:, k, 0:T].bitcast(F32), ALU.subtract).then_inc(S.dve.sem, 1)
                    S.dve.n += 1
                    done[k] = (S.dve, S.dve.n)
                at.a_ready = done

            def layer_norm(i, j, project=None):
                border()
                base_d = S.dve.n
                for k in range(DK):
                    if dve:
                        e.tensor_tensor(z[:, k, 0:T], z[:, k, 0:T], bank[6][:, 0:T], ALU.subtract).then_inc(S.dve.sem, 1)
                S.dve.n += DK
                for k in range(DK):
                    if pe and k == 0:
                        e.wait_ge(S.dve.sem, S.dve.n)
                    column_sum(lambda k: z[:, k, 0:T], k, DK, T, True, (S.dve, base_d + k + 1))
                inverse_root(T, 1.0, 1)
                if pe:
                    e.wait_ge(S.act.sem, S.act.n)
                row = (i * 2 + j) * DK
                if dve:
                    e.wait_ge(S.dve.sem, S.dve.n)
                scaled, done = {}, {}
                for k in range(DK + 2):
                    if k < DK:
                        if dve:
                            e.scalar_tensor_tensor(out=z[:, k, 0:T], in0=z[:, k, 0:T], scalar=vec("ln_g_2", row + k), in1=r_tmp[:, 0:T],
                                                   op0=ALU.mult, op1=ALU.mult).then_inc(S.dve.sem, 1)
                        S.dve.n += 1
                        if act:
                            e.wait_ge(S.dve.sem, S.dve.n)
                            e.activation(a_hi[:, k, 0:T], z[:, k, 0:T], ACT.Identity, bias=vec("ln_b_2", row + k)).then_inc(S.act.sem, 1)
                            e.activation(xt[:, k, 0:T], z[:, k, 0:T], ACT.Identity, bias=vec("ln_b_2", row + k)).then_inc(S.act.sem, 1)
                        S.act.n += 2
                        scaled[k] = S.act.n - 1
                    if k >= 2:
                        m = k - 2
                        if dve:
                            e.wait_ge(S.act.sem, scaled[m])
                            e.scalar_tensor_tensor(out=a_lo[:, m, 0:T], in0=z[:, m, 0:T], scalar=vec("ln_b_2", row + m),
                                                   in1=a_hi[:, m, 0:T].bitcast(F32), op0=ALU.add, op1=ALU.subtract).then_inc(S.dve.sem, 1)
                        S.dve.n += 1
                        done[m] = (S.dve, S.dve.n)
                if project:
                    project()
                at.a_ready = done

            def mlp(i):
                base = Counts(a=S.act_evicted.n, d=S.dve_evicted.n, h=S.hidden_hi.n, l=S.hidden_lo.n)

                def squared_relu(i, p, per, used, b):
                    if act:
                        for m in range(2):
                            e.wait_ge(S.slot_used.sem, used(m))
                            e.wait_ge(S.dve_evicted.sem, val(base.d + 2 * p - 1 + m, i, 2 * per))
                            e.activation(tmp_g[:, m, 0:T], b[m][:, 0:T], ACT.Relu).then_inc(S.act_evicted.sem, 1)
                    if dve:
                        for m in range(2):
                            e.wait_ge(S.act_evicted.sem, val(base.a + 2 * p + m + 1, i, 2 * per))
                            e.wait_ge(S.hidden_hi.sem, val(base.h + 2 * p - 1 + m, i, 2 * per))
                            e.wait_ge(S.hidden_lo.sem, val(base.l + 2 * p - 1 + m, i, 2 * per))
                            e.tensor_tensor(tmp_y[:, m, 0:T], tmp_g[:, m, 0:T], tmp_g[:, m, 0:T], ALU.mult).then_inc(S.dve_evicted.sem, 1)
                    cut_hidden(i, p, per, T, (base.d, base.h))

                gemm(A["mlp_w1_2"][i], [(0, DK)], 16, 4, a_op(T), squared_relu, S.act_evicted)
                for s in (S.dve_evicted, S.hidden_hi, S.hidden_lo):
                    s.n += 32
                at.lag = (2, 2)
                hidden_ready(32)
                if dve:
                    e.wait_ge(S.act.sem, S.act.n)
                    e.wait_ge(S.dve.sem, S.dve.n)
                gemm(A["mlp_w2_2"][i], [(8 * g, 8) for g in range(4)], 4, 4,
                     lambda k: (h_hi_f[:, k * T:k * T + T], h_lo_f[:, k * T:k * T + T]), residual_to_z, S.dve_evicted,
                     sums=z_sums(T, S.dve_evicted, False))

            def wide_slot(src, kt, width, tiles):
                n = at.slot
                view = lambda t: t.rearrange("p k c -> p (k c)")[:, 0:kt * width].rearrange("p (k c) -> p k c", c=width)
                load(n, None, 0, lambda: src, view=view)
                if pe:
                    e.wait_ge(S.lo_ready.sem, 2 * n + 2)
                    hi, lo = view(w_hi[:, n % CUT, :, :]), view(w_lo[:, n % CUT, :, :])
                    for dst, ops in tiles:
                        for k in range(kt):
                            mm = three(dst, *ops(hi, lo, k), k == 0, k == kt - 1)
                    mm.then_inc(S.slot_used.sem, 2)
                ahead(n, None, 0)
                at.slot += 1

            p_in, p_hi, p_lo, pj = xt[:, 0:2, T:TT], a_hi[:, 0:2, T:TT], a_lo[:, 0:2, T:TT], z[:, :, T:TT]

            def ple_load(i):
                if pool:
                    side_wait()
                    border()
                side_load(p_in, A["p_2"][i, 0].rearrange("(b p) d -> p b d", p=P))

            def ple_turn():
                base_p = S.pe.n
                for k in range(2):
                    if pe:
                        if k == 0:
                            side_wait()
                            e.wait_ge(S.dve.sem, S.dve.n)
                            e.wait_ge(S.act.sem, S.act.n)
                        for b in range(2):
                            mm = e.transpose(bank[4 + k][:, b * P:b * P + P], p_in[:, b, k * P:k * P + P], eye[:, :])
                        mm.then_inc(S.pe.sem, 1)
                    if act:
                        e.wait_ge(S.pe.sem, base_p + k + 1)
                        e.activation(p_hi[:, k, :], bank[4 + k][:, 0:T], ACT.Copy).then_inc(S.act.sem, 1)
                    S.act.n += 1
                    if dve:
                        e.wait_ge(S.act.sem, S.act.n)
                        e.tensor_tensor(p_lo[:, k, :], bank[4 + k][:, 0:T], p_hi[:, k, :].bitcast(F32), ALU.subtract).then_inc(S.dve.sem, 1)
                    S.dve.n += 1
                S.pe.n += 2

            def ple_project(i):
                order = (4, 5, 7, 6)
                wide_slot(matrix(A["ple_w_proj_2"][i]), 2, D,
                          [(bank[order[m // 2]][:, (m % 2) * T:(m % 2) * T + T],
                            lambda hi, lo, k, m=m: (hi[:, k, m * P:m * P + P], lo[:, k, m * P:m * P + P], p_hi[:, k, :], p_lo[:, k, :]))
                           for m in range(8)])
                for j in range(4):
                    if act:
                        e.wait_ge(S.slot_used.sem, 2 * at.slot)
                        e.activation(pj[:, 2 * j:2 * j + 2, :], bank[order[j]][:, :].rearrange("p (m t) -> p m t", t=T),
                                     ACT.Copy).then_inc(S.act.sem, 1)
                S.act.n += 4

            def ple(i):
                if dve:
                    e.wait_ge(S.act.sem, S.act.n)
                base = Counts(a=S.act_evicted.n, d=S.dve_evicted.n, v=S.dve.n)

                def gated(i, p, per, used, b):
                    for m in range(2):
                        if act:
                            e.wait_ge(S.slot_used.sem, used(m))
                            e.wait_ge(S.dve_evicted.sem, base.d + 2 * p - 1 + m)
                            e.activation(tmp_g[:, m, 0:T], b[m][:, 0:T], ACT.Sigmoid).then_inc(S.act_evicted.sem, 1)
                        if dve:
                            t = 2 * p + m
                            e.wait_ge(S.act_evicted.sem, base.a + t + 1)
                            e.tensor_tensor(tmp_y[:, m, 0:T], tmp_g[:, m, 0:T], pj[:, t, :], ALU.mult).then_inc(S.dve_evicted.sem, 1)
                            e.wait_ge(S.dve_evicted.sem, base.d + t + 1)
                            e.tensor_tensor(xt[:, t, 0:T], xt[:, t, 0:T], tmp_y[:, m, 0:T], ALU.add).then_inc(S.dve.sem, 1)
                gemm(A["ple_w_gate_2"][i], [(0, DK)], 4, 4, a_op(T), gated, S.act_evicted)
                S.dve_evicted.n += 8
                S.dve.n += 8
                at.x_ready = [base.v + k + 1 for k in range(DK)]

            def out_product(w):
                if act or dve:
                    border()
                gemm(w, [(0, DK)], 4, 4, a_op(T), residual_to_z, S.dve_evicted, sums=z_sums(T, S.dve_evicted, False))

            def a_from(src, made):
                base_a, base_d = S.act.n, S.dve.n
                for k in range(DK):
                    if act:
                        if k == 0:
                            e.wait_ge(S.slot_used.sem, 2 * at.slot)
                        e.wait_ge(S.dve.sem, made(k))
                        e.activation(a_hi[:, k, 0:T], src(k), ACT.Copy).then_inc(S.act.sem, 1)
                    if dve:
                        e.wait_ge(S.act.sem, base_a + k + 1)
                        e.tensor_tensor(a_lo[:, k, 0:T], src(k), a_hi[:, k, 0:T].bitcast(F32), ALU.subtract).then_inc(S.dve.sem, 1)
                at.a_ready = {k: (S.dve, base_d + k + 1) for k in range(DK)}
                S.act.n += DK
                S.dve.n += DK

            def one(name, op):
                mine, s = {"act": (act, S.act), "dve": (dve, S.dve)}[name]
                if mine:
                    op().then_inc(s.sem, 1)
                s.n += 1
                if act or dve:
                    e.wait_ge(s.sem, s.n)

            def gla(j):
                w = A["gla_w_in_2"][j]
                if pool:
                    side_wait()
                    border()
                side_load(w_glr[:, :, :], matrix(w)[:, :, 3 * D:3 * D + GLA_RANK])
                side_load(w_gate[:, :], A["gla_w_gate_up_2"][j])
                for dst, name in ((g_low, "gla_low"), (g_up, "gla_up"), (g_carry, "gla_carry")):
                    side_load(dst[:, :], C[name][:])
                flat = lambda t: t[:].rearrange("p a t -> p (a t)")
                hk = GLA_HEADS * GLA_DK
                qk_out = S.act_evicted.n + 2 * GLA_HEADS

                def decays():
                    yield
                    if pe:
                        side_wait()
                        for k in range(DK):
                            mm = e.matmul(bank[6][0:GLA_RANK, 0:T], w_glr[:, k, :], xt[:, k, 0:T], start=k == 0, stop=k == DK - 1)
                        mm.then_inc(S.pe.sem, 1)
                    S.pe.n += 1
                    if dve:
                        e.wait_ge(S.pe.sem, S.pe.n)
                        e.tensor_copy(g_rank[:, :], bank[6][0:GLA_RANK, 0:T]).then_inc(S.dve.sem, 1)
                    S.dve.n += 1
                    yield
                    for h in range(GLA_HEADS):
                        if pe:
                            e.wait_ge(S.dve.sem, S.dve.n)
                            mm = e.matmul(bank[4 + h % 2][:, (h // 2) * T:(h // 2) * T + T], w_gate[:, h * P:h * P + P], g_rank[:, :],
                                          start=True, stop=True)
                    if pe:
                        mm.then_inc(S.pe.sem, 1)
                    S.pe.n += 1
                    if act:
                        e.wait_ge(S.pe.sem, S.pe.n)
                        for h in range(GLA_HEADS):
                            e.activation(e_l[:, h, :], bank[4 + h % 2][:, (h // 2) * T:(h // 2) * T + T], ACT.Identity,
                                         bias=vec("gla_b_gate_2", j * GLA_HEADS + h)).then_inc(S.act.sem, 1)
                    S.act.n += GLA_HEADS
                    if act or dve:
                        e.wait_ge(S.act.sem, S.act.n)
                    yield
                    one("act", lambda: e.activation(flat(e_pos), flat(e_l), ACT.Abs))
                    one("act", lambda: e.activation(flat(e_pos), flat(e_pos), ACT.Exp, scale=-1.0))
                    one("act", lambda: e.activation(flat(e_pos), flat(e_pos), ACT.Ln, bias=stat[:, 8:9]))
                    one("dve", lambda: e.scalar_tensor_tensor(out=flat(e_l), in0=flat(e_l), scalar=0.0, in1=flat(e_pos), op0=ALU.min, op1=ALU.subtract))
                    yield
                    if dve:
                        side_wait()
                    one("dve", lambda: e.tensor_tensor_scan(flat(L), g_carry[:, :], flat(e_l), 0.0, ALU.mult, ALU.add))
                    ch = lambda t: t[:].rearrange("p h (c t) -> p (h c) t", t=CHUNK)
                    wide = [P, GLA_HEADS * 4, CHUNK]
                    one("dve", lambda: e.tensor_tensor(ch(e_neg), ch(L), ch(L)[:, :, CHUNK // 2 - 1:CHUNK // 2].to_broadcast(wide), ALU.subtract))
                    one("dve", lambda: e.tensor_scalar(flat(e_neg), flat(e_neg), GLA_TAU * EXPONENT_MAX, -GLA_TAU * EXPONENT_MAX, ALU.min, ALU.max))
                    one("dve", lambda: e.tensor_tensor(ch(e_end), ch(L)[:, :, CHUNK - 1:CHUNK].to_broadcast(wide), ch(L), ALU.subtract))
                    yield
                    one("act", lambda: e.activation(flat(e_pos), flat(e_neg), ACT.Exp, scale=1 / GLA_TAU))
                    one("act", lambda: e.activation(flat(e_neg), flat(e_neg), ACT.Exp, scale=-1 / GLA_TAU))
                    yield
                    one("act", lambda: e.activation(flat(e_l), flat(L), ACT.Exp, scale=1 / GLA_TAU))
                    one("act", lambda: e.activation(flat(e_end), flat(e_end), ACT.Exp, scale=1 / GLA_TAU))
                    yield
                    if dve:
                        e.wait_ge(S.act_evicted.sem, qk_out)
                    one("dve", lambda: e.tensor_tensor(flat(q_low), flat(qg), flat(e_pos), ALU.mult))
                    one("dve", lambda: e.tensor_tensor(flat(k_low), flat(kg), flat(e_neg), ALU.mult))
                    yield
                    one("dve", lambda: e.tensor_tensor(flat(e_neg), flat(qg), flat(e_neg), ALU.mult))
                    one("dve", lambda: e.tensor_tensor(flat(e_pos), flat(kg), flat(e_pos), ALU.mult))
                    yield
                    one("dve", lambda: e.tensor_copy(g_end[:, :].unsqueeze(2), ch(e_l)[:, :, CHUNK - 1:CHUNK]))
                    one("dve", lambda: e.tensor_tensor(flat(e_l), flat(qg), flat(e_l), ALU.mult))
                    one("dve", lambda: e.tensor_tensor(flat(e_end), flat(kg), flat(e_end), ALU.mult))

                steps = decays()
                gemm(w, [(0, DK)], 2, 2, a_op(T), copy_to(flat(qg), T, T, GLA_DK ** -0.5), S.act_evicted, between=steps)
                gemm(w, [(0, DK)], 2, 2, a_op(T), copy_to(flat(kg), T, T), S.act_evicted, first_col=hk, between=steps)
                token_major(w, 2 * hk, 4, T, lambda t, s: v_g[:, t, s * SC:(s + 1) * SC], between=steps)
                gemm(w, [(0, DK)], 4, 4, a_op(T), copy_to(flat(r_gate), T, T, 1.0, ACT.Silu), S.act_evicted, first_col=2 * hk + D,
                     between=steps)
                for _ in steps:
                    pass
                e_border()
                if pe:
                    for c in range(4):
                        rows, tok = slice((c % 2) * CHUNK, (c % 2 + 1) * CHUNK), slice(c * CHUNK, (c + 1) * CHUNK)
                        for h in range(GLA_HEADS):
                            col = (c // 2 * GLA_HEADS + h) * CHUNK
                            e.matmul(bank[6][rows, col:col + CHUNK], k_low[:, h, tok], q_low[:, h, tok], start=True, stop=True)
                            mm = e.matmul(bank[7][rows, col:col + CHUNK], e_pos[:, h, tok], e_neg[:, h, tok], start=True, stop=True)
                    mm.then_inc(S.pe.sem, 1)
                    for b in range(2):
                        for h in range(GLA_HEADS):
                            mm = e.transpose(bank[4 + b][:, h * P:h * P + P], e_end[:, h, b * P:b * P + P], eye[:, :])
                    mm.then_inc(S.pe.sem, 1)
                S.pe.n += 2
                if act:
                    e.wait_ge(S.pe.sem, S.pe.n)
                    for b in range(2):
                        e.activation(k_tok[:, b, :, :].rearrange("p h d -> p (h d)"), bank[4 + b][:, :], ACT.Copy).then_inc(S.act.sem, 1)
                S.act.n += 2
                sc_f = sc_g[:, :, :, :].rearrange("p a h t -> p (a h) t")
                bk = lambda b: b[:, :].rearrange("p (a t) -> p a t", t=CHUNK)
                mask = lambda m: m[:, :].unsqueeze(1).to_broadcast([P, 8, CHUNK])
                tg = tmp_g[:, 0, :].rearrange("p (a t) -> p a t", t=CHUNK)
                if dve:
                    e.wait_ge(S.pe.sem, S.pe.n - 1)
                    e.tensor_tensor(sc_f, bk(bank[6]), mask(g_low), ALU.mult).then_inc(S.dve.sem, 1)
                    e.tensor_tensor(tg, bk(bank[7]), mask(g_up), ALU.mult).then_inc(S.dve.sem, 1)
                    e.wait_ge(S.dve.sem, S.dve.n + 2)
                    e.tensor_tensor(sc_f, sc_f, tg, ALU.add).then_inc(S.dve.sem, 1)
                S.dve.n += 3
                for c in range(4):
                    rows, tok = slice((c % 2) * CHUNK, (c % 2 + 1) * CHUNK), slice(c * CHUNK, (c + 1) * CHUNK)
                    if pe:
                        e.wait_ge(S.dve.sem, S.dve.n)
                        e.wait_ge(S.act.sem, S.act.n)
                        for h in range(GLA_HEADS):
                            for et in range(2):
                                dst = bank[h][:, et * T + c * CHUNK:et * T + (c + 1) * CHUNK]
                                e.matmul(dst, v_g[rows, c // 2, h * GLA_DV + et * P:h * GLA_DV + et * P + P], sc_g[rows, c // 2, h, :],
                                         start=True, stop=c == 0)
                                if c:
                                    e.matmul(dst, state[:, h, et * P:et * P + P], e_l[:, h, tok], start=False, stop=True)
                            if c < 3:
                                mm = e.matmul(bank[4 + h // 2][:, (h % 2) * T:(h % 2) * T + T], k_tok[rows, c // 2, h, :],
                                              v_g[rows, c // 2, h * GLA_DV:(h + 1) * GLA_DV], start=True, stop=True)
                        if c == 3:
                            mm = e.matmul(bank[6][0:1, 0:1], eye[:, 0:1], eye[:, 0:1], start=True, stop=True)
                        mm.then_inc(S.pe.sem, 1)
                    S.pe.n += 1
                    if c < 3:
                        for h in range(GLA_HEADS):
                            u = bank[4 + h // 2][:, (h % 2) * T:(h % 2) * T + T]
                            if dve:
                                e.wait_ge(S.pe.sem, S.pe.n)
                                if c == 0:
                                    e.tensor_copy(state[:, h, :], u).then_inc(S.dve.sem, 1)
                                else:
                                    e.scalar_tensor_tensor(out=state[:, h, :], in0=state[:, h, :], scalar=g_end[:, h * 4 + c:h * 4 + c + 1],
                                                           in1=u, op0=ALU.mult, op1=ALU.add).then_inc(S.dve.sem, 1)
                        S.dve.n += GLA_HEADS
                e_border()
                base_p, base_a = S.pe.n, S.act.n
                for h in range(GLA_HEADS):
                    if act:
                        if h >= 2:
                            e.wait_ge(S.pe.sem, base_p + h - 1)
                        e.activation(tmp_g[:, h % 2, :], bank[h][:, :], ACT.Square).then_inc(S.act.sem, 1)
                    if pe:
                        e.wait_ge(S.act.sem, base_a + h + 1)
                        for et in range(2):
                            mm = e.matmul(bank[6 + h // 2][:, (h % 2) * T:(h % 2) * T + T], ones[:, :], tmp_g[:, h % 2, et * T:et * T + T],
                                          start=et == 0, stop=et == 1)
                        mm.then_inc(S.pe.sem, 1)
                S.pe.n += GLA_HEADS
                S.act.n += GLA_HEADS
                if act:
                    e.wait_ge(S.pe.sem, S.pe.n)
                    for b in range(2):
                        e.activation(flat(e_neg)[:, b * TT:b * TT + TT], bank[6 + b][:, :], ACT.Sqrt, bias=stat[:, 0:1],
                                     scale=D / GLA_DV).then_inc(S.act.sem, 1)
                S.act.n += 2
                gated = {}
                for b in range(2):
                    if dve:
                        e.wait_ge(S.act.sem, S.act.n - 1 + b)
                        inv = flat(e_neg)[:, b * TT:b * TT + TT]
                        e.reciprocal(inv, inv).then_inc(S.dve.sem, 1)
                        e.wait_ge(S.dve.sem, S.dve.n + 1)
                    S.dve.n += 1
                    base_d = S.dve.n
                    for x in range(5):
                        if dve and x < 4:
                            t = 4 * b + x
                            h, et = divmod(t, 2)
                            e.scalar_tensor_tensor(out=qg_kg(t), in0=bank[h][:, et * T:et * T + T], scalar=vec("gla_norm_g_2", j * 2 + et),
                                                   in1=e_neg[:, h, :], op0=ALU.mult, op1=ALU.mult).then_inc(S.dve.sem, 1)
                        if dve and x:
                            t = 4 * b + x - 1
                            e.wait_ge(S.dve.sem, base_d + max(2 * x - 2, 1))
                            e.tensor_tensor(qg_kg(t), qg_kg(t), r_gate[:, t, :], ALU.mult).then_inc(S.dve.sem, 1)
                        if x:
                            gated[4 * b + x - 1] = base_d + min(2 * x + 1, 8)
                    S.dve.n += 8
                a_from(qg_kg, lambda k: gated[k])
                out_product(A["gla_w_out_2"][j])

            def qg_kg(t):
                return qg[:, t, :] if t < 4 else kg[:, t - 4, :]

            TWO_PI = (6.28125, 0.0019350051879882812, 3.019916050561733e-07)

            def mla_angles():
                if dve or act:
                    side_wait()
                one("dve", lambda: e.tensor_scalar(ang[:, 0, :], pos_i[:, :], freq[:, 0:1], None, ALU.mult))
                for dst, quarter in ((cos_m, 0.25), (sin_m, 0.0)):
                    r = ang[:, 1, :]
                    one("dve", lambda: e.tensor_scalar(r, ang[:, 0, :], 1.0 / (2 * np.pi), quarter, ALU.mult, ALU.add))
                    one("dve", lambda: e.tensor_copy(pos_i[:, :], r))
                    one("dve", lambda: e.scalar_tensor_tensor(out=r, in0=pos_i[:, :], scalar=-TWO_PI[0], in1=ang[:, 0, :], op0=ALU.mult, op1=ALU.add))
                    one("dve", lambda: e.scalar_tensor_tensor(out=r, in0=pos_i[:, :], scalar=-TWO_PI[1], in1=r, op0=ALU.mult, op1=ALU.add))
                    one("dve", lambda: e.scalar_tensor_tensor(out=r, in0=pos_i[:, :], scalar=-TWO_PI[2], in1=r, op0=ALU.mult, op1=ALU.add))
                    one("dve", lambda: e.tensor_scalar(r, r, quarter * 2 * np.pi, None, ALU.add))
                    one("dve", lambda: e.tensor_scalar(ang[:, 2, :], r, float(np.pi), -2 * np.pi, ALU.is_gt, ALU.mult))
                    one("dve", lambda: e.tensor_tensor(r, r, ang[:, 2, :], ALU.add))
                    one("dve", lambda: e.tensor_scalar(r, r, 3.1415925, -3.1415925, ALU.min, ALU.max))
                    one("act", lambda: e.activation(dst[:, :], r, ACT.Sin))
                one("dve", lambda: e.tensor_scalar(sin_m[:, :], sin_m[:, :], freq[:, 1:2], None, ALU.mult))

            def mla(j):
                if pool:
                    side_wait()
                    border()
                pos = A["positions_2"]
                side_load(pos_i[:, :], bass.AP(tensor=pos.tensor, offset=pos.offset, ap=[[0, P], [1, T]]))
                side_load(freq[:, :], C["mla_freq"][:])
                side_load(mask_m[:, :, :], C["mla_mask"][:])
                w = A["mla_w_in_2"][j]
                flat = lambda t: t[:].rearrange("p a t -> p (a t)")
                gemm(w, [(0, DK)], 2, 2, a_op(T), copy_to(flat(c_in), T, T), S.act_evicted)
                n = at.slot
                load(n, None, 0, lambda: matrix(w)[:, :, 512 - 64:512 + 64], DK, P)
                if pe:
                    slot_products(n, None, 0, DK, 0, a_op(T), [bank[4][:, 0:T]])
                ahead(n, None, 0)
                at.slot += 1
                if act:
                    e.wait_ge(S.slot_used.sem, 2 * at.slot)
                    e.activation(kr[64:128, 0, :], bank[4][64:128, 0:T], ACT.Copy).then_inc(S.act.sem, 1)
                    e.activation(kr[64:96, 1, :], bank[4][96:128, 0:T], ACT.Copy).then_inc(S.act.sem, 1)
                    e.activation(kr[96:128, 1, :], bank[4][64:96, 0:T], ACT.Copy).then_inc(S.act.sem, 1)
                S.act.n += 3
                e_border()
                for c, name in enumerate(("mla_q_norm_2", "mla_kv_norm_2")):
                    if pe or act:
                        e.wait_ge(S.dve.sem, S.dve.n)
                    column_sums(lambda k: c_in[:, 2 * c + k, :], 2, T, True)
                    inverse_root(T, D / 256, 0)
                    if dve:
                        e.wait_ge(S.dve.sem, S.dve.n)
                    for t in range(2):
                        k = 2 * c + t
                        if dve:
                            e.scalar_tensor_tensor(out=c_in[:, k, :], in0=c_in[:, k, :], scalar=vec(name, t), in1=r_tmp[:, 0:T],
                                                   op0=ALU.mult, op1=ALU.mult).then_inc(S.dve.sem, 1)
                        S.dve.n += 1
                        if act:
                            e.wait_ge(S.dve.sem, S.dve.n)
                            e.activation(a_hi[:, k, 0:T], c_in[:, k, :], ACT.Copy).then_inc(S.act.sem, 1)
                        S.act.n += 1
                        if dve:
                            e.wait_ge(S.act.sem, S.act.n)
                            e.tensor_tensor(a_lo[:, k, 0:T], c_in[:, k, :], a_hi[:, k, 0:T].bitcast(F32), ALU.subtract).then_inc(S.dve.sem, 1)
                        S.dve.n += 1
                head = MLA_NOPE + MLA_ROPE
                wq = matrix(A["mla_w_uq_2"][j])
                low = slice(64, 128)
                bc = lambda t: t[low, :].unsqueeze(1).to_broadcast([64, 4, T])

                def turned(dst, src, other, cos, sin):
                    for out_, x, y, op in ((dst, src, cos, ALU.mult), (other, other, sin, ALU.mult), (dst, dst, other, ALU.add)):
                        if dve:
                            e.wait_ge(S.dve.sem, S.dve.n)
                            e.tensor_tensor(out_, x, y, op).then_inc(S.dve.sem, 1)
                        S.dve.n += 1
                e_border()
                read = []
                for half in range(2):
                    tiles, b0 = [], 4 * half
                    for h in range(4):
                        for o, c in ((0, 0), (64, T)):
                            tiles.append((bank[b0 + h][:, c:c + T], lambda hi, lo, k, o=o, h=h: (
                                hi[:, k, h * head + o:h * head + o + P], lo[:, k, h * head + o:h * head + o + P],
                                a_hi[:, k, 0:T], a_lo[:, k, 0:T])))
                    wide_slot(wq[:, :, half * 4 * head:(half + 1) * 4 * head], 2, 4 * head, tiles)
                    for h in range(4):
                        hh, b = half * 4 + h, bank[b0 + h]
                        if act:
                            e.wait_ge(S.slot_used.sem, 2 * at.slot)
                            e.activation(qn[:, hh, :], b[:, 0:T], ACT.Copy, scale=MLA_SCALE).then_inc(S.act.sem, 1)
                            e.activation(qr[64:128, hh, :], b[64:128, T:TT], ACT.Copy, scale=MLA_SCALE).then_inc(S.act.sem, 1)
                        if dve:
                            e.wait_ge(S.act.sem, S.act.n + 2)
                            e.tensor_scalar(qs[64:96, hh, :], b[96:128, T:TT], MLA_SCALE, None, ALU.mult).then_inc(S.dve.sem, 1)
                            e.tensor_scalar(qs[96:128, hh, :], b[64:96, T:TT], MLA_SCALE, None, ALU.mult).then_inc(S.dve.sem, 1)
                        S.act.n += 2
                        S.dve.n += 2
                    read.append((S.act.n, S.dve.n))
                mla_angles()
                wkv = matrix(A["mla_w_ukv_2"][j])
                for half in range(2):
                    b0 = 4 * half
                    tiles = [(bank[b0 + h // 2][:, h % 2 * T:h % 2 * T + T], lambda hi, lo, k, h=h: (
                        hi[:, k, h * 256:h * 256 + P], lo[:, k, h * 256:h * 256 + P],
                        a_hi[:, 2 + k, 0:T], a_lo[:, 2 + k, 0:T])) for h in range(4)]
                    tiles += [(bank[b0 + 2 + t][:, h * P:h * P + P], lambda hi, lo, k, t=t, h=h: (
                        a_hi[:, 2 + k, t * P:t * P + P], a_lo[:, 2 + k, t * P:t * P + P],
                        hi[:, k, h * 256 + P:h * 256 + 2 * P], lo[:, k, h * 256 + P:h * 256 + 2 * P])) for t in range(2) for h in range(4)]
                    if pe:
                        e.wait_ge(S.act.sem, read[half][0])
                        e.wait_ge(S.dve.sem, read[half][1])
                    wide_slot(wkv[:, :, half * D:(half + 1) * D], 2, D, tiles)
                    for x in range(2):
                        if act:
                            e.wait_ge(S.slot_used.sem, 2 * at.slot)
                            e.activation(kn[:, half * 4 + 2 * x:half * 4 + 2 * x + 2, :],
                                         bank[b0 + x][:, :].rearrange("p (m t) -> p m t", t=T), ACT.Copy).then_inc(S.act.sem, 1)
                    S.act.n += 2
                    for t in range(2):
                        if dve:
                            e.wait_ge(S.slot_used.sem, 2 * at.slot)
                            e.tensor_copy(v_m[:, t, half * 512:half * 512 + 512], bank[b0 + 2 + t][:, :]).then_inc(S.dve.sem, 1)
                    S.dve.n += 2
                    if half == 0:
                        if dve:
                            e.wait_ge(S.act.sem, S.act.n)
                        turned(kr[low, 0, :], kr[low, 0, :], kr[low, 1, :], cos_m[low, :], sin_m[low, :])
                    hs = slice(4 * half, 4 * half + 4)
                    turned(qr[low, hs, :], qr[low, hs, :], qs[low, hs, :], bc(cos_m), bc(sin_m))
                e_border()
                pe_wait_all()
                units = []
                for h in range(MLA_HEADS):
                    for q in range(2):
                        tok = slice(q * P, q * P + P)
                        units.append(dict(head=h, q=q, keys=T, biased=T, bias=mask_m[:, q, :],
                                          scores=[(qn[:, h, tok], kn[:, h, :]), (qr[low, h, tok], kr[low, 0, :])]))
                attention(units, lambda x, kb: (v_m[:, kb, x["head"] * MLA_V:(x["head"] + 1) * MLA_V], 0),
                          prob_m, probT_m, lambda x, buf: buf[:, x["head"], 0:T], 1)
                e_border()
                out_product(A["mla_w_out_2"][j])

            def conv(j):
                w = A["conv_w_in_2"][j]
                flat = lambda t: t[:].rearrange("p a t -> p (a t)")
                cu_f = flat(cu)
                if dve:
                    e.memset(cu[:, :, 0:2], 0.0).then_inc(S.dve.sem, 1)
                S.dve.n += 1
                gemm(w, [(0, DK)], 4, 4, a_op(T), copy_to(flat(cb), T, T), S.act_evicted)
                gemm(w, [(0, DK)], 4, 4, a_op(T), copy_to(flat(cc), T, T), S.act_evicted, first_col=D)
                ready = S.act_evicted.n

                def times_c(i, p, per, used, b):
                    if dve:
                        e.wait_ge(S.act_evicted.sem, ready)
                        for m in range(2):
                            e.wait_ge(S.slot_used.sem, used(m))
                            t = 2 * p + m
                            e.tensor_tensor(cu[:, t, 2:T + 2], cc[:, t, :], b[m][:, 0:T], ALU.mult).then_inc(S.dve_evicted.sem, 1)
                base, out_of = S.dve.n, S.dve_evicted.n

                def taps():
                    for k in range(DK):
                        for tap in range(3):
                            x, f = cu[:, k, tap:tap + T], vec("conv_w_2", tap * DK + k)
                            if dve and tap == 0:
                                e.wait_ge(S.dve_evicted.sem, out_of + k + 1)
                                e.tensor_scalar(cc[:, k, :], x, f, None, ALU.mult).then_inc(S.dve.sem, 1)
                            elif dve:
                                e.wait_ge(S.dve.sem, base + 4 * k + tap)
                                e.scalar_tensor_tensor(out=cc[:, k, :], in0=x, scalar=f, in1=cc[:, k, :], op0=ALU.mult,
                                                       op1=ALU.add).then_inc(S.dve.sem, 1)
                        if dve:
                            e.wait_ge(S.dve.sem, base + 4 * k + 3)
                            e.tensor_tensor(cc[:, k, :], cc[:, k, :], cb[:, k, :], ALU.mult).then_inc(S.dve.sem, 1)
                        if k % 2:
                            yield
                gemm(w, [(0, DK)], 4, 4, a_op(T), times_c, S.dve_evicted, first_col=2 * D, between=taps())
                S.dve.n += 4 * DK
                a_from(lambda k: cc[:, k, :], lambda k: base + 4 * k + 4)
                out_product(A["conv_w_out_2"][j])

            def finish():
                border()
                base_p, base_d = S.pe.n, S.dve.n
                for j, (b, k4) in enumerate((b, k4) for b in range(2) for k4 in range(2)):
                    if pe:
                        for k in range(4):
                            mm = e.transpose(bank[j][:, k * P:k * P + P], xt[:, k4 * 4 + k, b * P:b * P + P], eye[:, :])
                        mm.then_inc(S.pe.sem, 1)
                    if dve:
                        e.wait_ge(S.pe.sem, base_p + j + 1)
                        e.tensor_copy(o_tok[:, b, k4 * 512:k4 * 512 + 512], bank[j][:, :]).then_inc(S.dve.sem, 1)
                S.pe.n += 4
                S.dve.n += 4
                if sp:
                    for b in range(2):
                        e.wait_ge(S.dve.sem, base_d + 2 * b + 2)
                        e.dma_start(out[0, b * P:(b + 1) * P, :], o_tok[:, b, :]).then_inc(S.stored.sem, 16)
                    e.wait_ge(S.stored.sem, 32)

            def network():
                yield begin()
                mods(1, 4)
                turn_x()
                mods(1, 4)
                yield
                for layer in range(DEPTH):
                    last = layer == DEPTH - 1
                    yield ffn(layer, 0, TT, 2 * (not last), 2 * (not last), 2 * last, 1 * (not last))
                    yield mix(layer, last)
                    if not last:
                        yield ffn(layer, 1, TT, 2, 2, 2)
                    else:
                        yield ffn(layer, 1, T, 0, 0, 0)
                for i in range(DEPTH_2):
                    cut_x()
                    ple_load(i)
                    yield (gla, mla, conv)[i % 3](i // 3)
                    ple_turn()
                    layer_norm(i, 0, lambda: ple_project(i))
                    mlp(i)
                    yield layer_norm(i, 1)
                    yield ple(i)

            for j, _ in enumerate(network()):
                if j >= upto:
                    break
            finish()
            if not total:
                total.append(at.slot)

        walk("plan", None)
        with nc.Block() as block:
            @block.sync
            def _(eng):
                walk("sp", eng)

            @block.tensor
            def _(eng):
                walk("pe", eng)

            @block.scalar
            def _(eng):
                walk("act", eng)

            @block.vector
            def _(eng):
                walk("dve", eng)

            @block.gpsimd
            def _(eng):
                walk("pool", eng)


INPUTS = (
    "x", "c", "ctx", "c_ctx", "w_mod", "b_mod", "norm_g", "w_ffn_gate_up", "w_ffn_down", "w_in", "w_out", "na_rpb",
    "w_pool", "pool_scale", "p_2", "positions_2", "gla_w_in_2", "gla_w_gate_up_2", "gla_b_gate_2", "gla_norm_g_2",
    "gla_w_out_2", "mla_w_in_2", "mla_q_norm_2", "mla_kv_norm_2", "mla_w_uq_2", "mla_w_ukv_2", "mla_w_out_2",
    "conv_w_in_2", "conv_w_2", "conv_w_out_2", "ln_g_2", "ln_b_2", "mlp_w1_2", "mlp_w2_2", "ple_w_gate_2", "ple_w_proj_2",
)


def kernel(**inputs):
    import concourse.bacc as bacc
    from concourse.bass_utils import run_bass_kernel_spmd

    nc = bacc.Bacc("TRN2", target_bir_lowering=False, num_devices=1)
    arrays, A = {}, {}
    for name in INPUTS:
        a = np.ascontiguousarray(inputs[name])
        arrays[f"in_{name}"] = a
        A[name] = nc.dram_tensor(f"in_{name}", a.shape, mybir.dt.from_np(a.dtype), kind="ExternalInput").ap()
    out = nc.dram_tensor("out", (1, T, D), F32, kind="ExternalOutput").ap()
    build(nc, A, out)
    r = run_bass_kernel_spmd(nc, [arrays], core_ids=[0])
    return r.results[0]["out"]
```
